# Optimizing a Trainium2 kernel written in Bass

```python
import math
import jax, jax.numpy as jnp
from jax import lax
import numpy as np

D_MODEL = 1024
BATCH = 1
SEQ = 256
DEPTH = 1

CTX_LEN = 256
GRID_W = 64
HEAD_DIM = 64
GQA_HEADS = 8
GQA_KV_HEADS = 2
GQA_GROUP = GQA_HEADS // GQA_KV_HEADS
DIFF_HEADS = 4
DIFF_V_DIM = 2 * HEAD_DIM
MIX_WIDTH = GQA_HEADS * HEAD_DIM + DIFF_HEADS * DIFF_V_DIM
A_Q_COLS = GQA_HEADS * HEAD_DIM
A_KV_COLS = GQA_KV_HEADS * HEAD_DIM
B_QK_COLS = DIFF_HEADS * 2 * HEAD_DIM
B_V_COLS = DIFF_HEADS * DIFF_V_DIM
QKV_COLS = A_Q_COLS + 2 * A_KV_COLS + 2 * B_QK_COLS + B_V_COLS
Q_BLOCK = 128
ROPE_THETA = 10000.0
N_EXPERTS = 32
TOP_K = 4
D_FF = D_MODEL
SWIGLU_ALPHA = 1.702
SWIGLU_LIMIT = 7.0
EXPERT_BLOCK = 128
N_MOD = 6
EPS = 1e-6


def rms_norm(x, g):
    xf = x.astype(jnp.float32)
    y = xf * lax.rsqrt(jnp.mean(xf * xf, axis=-1, keepdims=True) + EPS)
    return (y * g.astype(jnp.float32)).astype(x.dtype)

def modulate(h, shift, scale):
    return h * (1 + scale) + shift

def axial_rope_tables(n_tokens):
    rows = n_tokens // GRID_W
    row = jnp.broadcast_to(jnp.arange(rows, dtype=jnp.float32)[:, None], (rows, GRID_W)).reshape(-1)
    col = jnp.broadcast_to(jnp.arange(GRID_W, dtype=jnp.float32)[None, :], (rows, GRID_W)).reshape(-1)
    n_freq = HEAD_DIM // 4
    inv_freq = ROPE_THETA ** (-jnp.arange(n_freq, dtype=jnp.float32) / n_freq)
    ang = jnp.stack([row[:, None] * inv_freq, col[:, None] * inv_freq], axis=1)
    return jnp.cos(ang), jnp.sin(ang)

def apply_axial_rope(x, cos, sin):
    b, t, h, _ = x.shape
    xr = x.reshape(b, t, h, 2, 2, HEAD_DIM // 4)
    x1, x2 = xr[..., 0, :], xr[..., 1, :]
    cs = cos[None, :, None]
    sn = sin[None, :, None]
    out = jnp.stack([x1 * cs - x2 * sn, x2 * cs + x1 * sn], axis=-2)
    return out.reshape(x.shape).astype(x.dtype)

def split_projection(p):
    b, t, _ = p.shape
    offs = [A_Q_COLS, A_Q_COLS + A_KV_COLS, A_Q_COLS + 2 * A_KV_COLS,
            A_Q_COLS + 2 * A_KV_COLS + B_QK_COLS, A_Q_COLS + 2 * A_KV_COLS + 2 * B_QK_COLS]
    qa, ka, va, qb, kb, vb = jnp.split(p, offs, axis=-1)
    qa = qa.reshape(b, t, GQA_HEADS, HEAD_DIM)
    ka = ka.reshape(b, t, GQA_KV_HEADS, HEAD_DIM)
    va = va.reshape(b, t, GQA_KV_HEADS, HEAD_DIM)
    qb = qb.reshape(b, t, DIFF_HEADS, 2, HEAD_DIM)
    kb = kb.reshape(b, t, DIFF_HEADS, 2, HEAD_DIM)
    vb = vb.reshape(b, t, DIFF_HEADS, DIFF_V_DIM)
    return qa, ka, va, qb, kb, vb

def rope_diff(x, cos, sin):
    b, t, h, two, d = x.shape
    return apply_axial_rope(x.reshape(b, t, h * two, d), cos, sin).reshape(x.shape)

def gqa_attention(q, k, v, q_block):
    b, t, _, d = q.shape
    nb = t // q_block
    qb = q.reshape(b, nb, q_block, GQA_KV_HEADS, GQA_GROUP, d).transpose(1, 0, 3, 4, 2, 5)
    scale = d ** -0.5

    def block(qi):
        s = jnp.einsum('bhgqd,bkhd->bhgqk', qi, k, preferred_element_type=jnp.float32) * scale
        p = jax.nn.softmax(s, axis=-1)
        return jnp.einsum('bhgqk,bkhd->bqhgd', p.astype(v.dtype), v)

    o = lax.map(block, qb)
    return o.transpose(1, 0, 2, 3, 4, 5).reshape(b, t, GQA_HEADS * d)

def diff_attention(q, k, v, lam, sub_g, lambda_init, q_block):
    b, t, h, _, d = q.shape
    nb = t // q_block
    qb = q.reshape(b, nb, q_block, h, 2, d).transpose(1, 0, 3, 4, 2, 5)
    scale = d ** -0.5

    def block(qi):
        s = jnp.einsum('bhcqd,bkhcd->bhcqk', qi, k, preferred_element_type=jnp.float32) * scale
        p = jax.nn.softmax(s, axis=-1)
        a = p[:, :, 0] - lam * p[:, :, 1]
        return jnp.einsum('bhqk,bkhe->bqhe', a.astype(v.dtype), v)

    o = lax.map(block, qb).transpose(1, 0, 2, 3, 4).reshape(b, t, h, DIFF_V_DIM)
    o = rms_norm(o, sub_g) * (1.0 - lambda_init)
    return o.reshape(b, t, h * DIFF_V_DIM)

def moe_ffn(h, w_router, b_router, w_in, b_in, w_out, b_out):
    b, t, dm = h.shape
    n = b * t
    xt = h.reshape(n, dm)
    logits = (xt @ w_router + b_router).astype(jnp.float32)
    top_val, top_idx = lax.top_k(logits, TOP_K)
    gates = jax.nn.softmax(top_val, axis=-1)
    n_assign = n * TOP_K
    exp_flat = top_idx.reshape(-1).astype(jnp.int32)
    tok_flat = jnp.repeat(jnp.arange(n, dtype=jnp.int32), TOP_K)
    gate_flat = gates.reshape(-1)
    order = jnp.argsort(exp_flat)
    exp_sorted = exp_flat[order]
    counts = jax.ops.segment_sum(jnp.ones_like(exp_flat), exp_flat, num_segments=N_EXPERTS)
    starts = jnp.cumsum(counts) - counts
    padded = (counts + EXPERT_BLOCK - 1) // EXPERT_BLOCK * EXPERT_BLOCK
    pad_ends = jnp.cumsum(padded)
    pad_starts = pad_ends - padded
    dest = pad_starts[exp_sorted] + (jnp.arange(n_assign, dtype=jnp.int32) - starts[exp_sorted])
    n_blocks = -(-n_assign // EXPERT_BLOCK) + N_EXPERTS
    n_rows = n_blocks * EXPERT_BLOCK
    row_tok = jnp.full((n_rows,), n, jnp.int32).at[dest].set(tok_flat[order])
    row_gate = jnp.zeros((n_rows,), jnp.float32).at[dest].set(gate_flat[order])
    block_start = jnp.arange(n_blocks, dtype=jnp.int32) * EXPERT_BLOCK
    block_exp = jnp.minimum(jnp.searchsorted(pad_ends, block_start, side='right'), N_EXPERTS - 1)
    x_pad = jnp.concatenate([xt, jnp.zeros((1, dm), xt.dtype)], axis=0)
    xs = x_pad[row_tok].reshape(n_blocks, EXPERT_BLOCK, dm)

    def expert_block(args):
        xb, e = args
        hcat = xb @ w_in[e] + b_in[e]
        x_glu = jnp.minimum(hcat[:, :D_FF], SWIGLU_LIMIT)
        x_lin = jnp.clip(hcat[:, D_FF:], -SWIGLU_LIMIT, SWIGLU_LIMIT)
        act = x_glu * jax.nn.sigmoid(SWIGLU_ALPHA * x_glu) * (x_lin + 1)
        return act @ w_out[e] + b_out[e]

    ys = lax.map(expert_block, (xs, block_exp)).reshape(n_rows, dm)
    y = jax.ops.segment_sum(ys * row_gate[:, None].astype(ys.dtype), row_tok, num_segments=n + 1)[:n]
    return y.reshape(b, t, dm)

def first_inputs(seed: int = 0) -> dict:
    key = jax.random.key(seed)
    ks = jax.random.split(key, 21)
    f32 = jnp.float32
    nrm = lambda k, shape, s: jax.random.normal(k, shape, f32) * s
    return {
        'x': nrm(ks[0], (BATCH, SEQ, D_MODEL), 1.0),
        'c': nrm(ks[1], (BATCH, D_MODEL), 1.0),
        'ctx': nrm(ks[2], (BATCH, CTX_LEN, D_MODEL), 1.0),
        'c_ctx': nrm(ks[3], (D_MODEL,), 1.0),
        'w_ada': nrm(ks[4], (DEPTH, D_MODEL, N_MOD * D_MODEL), 0.5 * D_MODEL ** -0.5),
        'b_ada': nrm(ks[5], (DEPTH, N_MOD * D_MODEL), 0.02),
        'g_attn': 1.0 + nrm(ks[6], (DEPTH, D_MODEL), 0.05),
        'w_qkv': nrm(ks[7], (DEPTH, D_MODEL, QKV_COLS), D_MODEL ** -0.5),
        'gqa_q_norm': 1.0 + nrm(ks[8], (DEPTH, HEAD_DIM), 0.05),
        'gqa_k_norm': 1.0 + nrm(ks[9], (DEPTH, HEAD_DIM), 0.05),
        'diff_lambda': nrm(ks[10], (DEPTH, 4, HEAD_DIM), 0.1),
        'diff_subln': 1.0 + nrm(ks[11], (DEPTH, DIFF_V_DIM), 0.05),
        'w_o': nrm(ks[12], (DEPTH, MIX_WIDTH, D_MODEL), MIX_WIDTH ** -0.5),
        'g_ffn': 1.0 + nrm(ks[13], (DEPTH, D_MODEL), 0.05),
        'w_router': nrm(ks[14], (DEPTH, D_MODEL, N_EXPERTS), D_MODEL ** -0.5),
        'b_router': nrm(ks[15], (DEPTH, N_EXPERTS), 0.01),
        'w_in': nrm(ks[16], (DEPTH, N_EXPERTS, D_MODEL, 2 * D_FF), D_MODEL ** -0.5),
        'b_in': nrm(ks[17], (DEPTH, N_EXPERTS, 2 * D_FF), 0.02),
        'w_out': nrm(ks[18], (DEPTH, N_EXPERTS, D_FF, D_MODEL), D_FF ** -0.5),
        'b_out': nrm(ks[19], (DEPTH, N_EXPERTS, D_MODEL), 0.02),
        'g_final': 1.0 + nrm(ks[20], (D_MODEL,), 0.05),
    }

def first_block(x, c, ctx, c_ctx, w_ada, b_ada, g_attn, w_qkv, gqa_q_norm, gqa_k_norm, diff_lambda,
              diff_subln, w_o, g_ffn, w_router, b_router, w_in, b_in, w_out, b_out, g_final):
    n_tok = x.shape[1]
    cos, sin = axial_rope_tables(n_tok)
    for l in range(DEPTH):
        lambda_init = 0.8 - 0.6 * math.exp(-0.3 * l)
        mod_x = (jax.nn.silu(c) @ w_ada[l] + b_ada[l])[:, None, :]
        mod_c = (jax.nn.silu(c_ctx) @ w_ada[l] + b_ada[l])[None, None, :]
        sh1, sc1, gt1, sh2, sc2, gt2 = jnp.split(mod_x, N_MOD, axis=-1)
        csh1, csc1, cgt1, csh2, csc2, cgt2 = jnp.split(mod_c, N_MOD, axis=-1)

        h = modulate(rms_norm(x, g_attn[l]), sh1, sc1)
        hc = modulate(rms_norm(ctx, g_attn[l]), csh1, csc1)
        qa, ka, va, qb, kb, vb = split_projection(h @ w_qkv[l])
        qa_c, ka_c, va_c, qb_c, kb_c, vb_c = split_projection(hc @ w_qkv[l])
        qa = apply_axial_rope(rms_norm(qa, gqa_q_norm[l]), cos, sin)
        ka = apply_axial_rope(rms_norm(ka, gqa_k_norm[l]), cos, sin)
        ka_c = rms_norm(ka_c, gqa_k_norm[l])
        qb = rope_diff(qb, cos, sin)
        kb = rope_diff(kb, cos, sin)
        lamf = diff_lambda[l].astype(jnp.float32)
        lam = jnp.exp(jnp.sum(lamf[0] * lamf[1])) - jnp.exp(jnp.sum(lamf[2] * lamf[3])) + lambda_init
        ka_all = jnp.concatenate([ka_c, ka], axis=1)
        va_all = jnp.concatenate([va_c, va], axis=1)
        kb_all = jnp.concatenate([kb_c, kb], axis=1)
        vb_all = jnp.concatenate([vb_c, vb], axis=1)
        lat_mix = jnp.concatenate([
            gqa_attention(qa, ka_all, va_all, Q_BLOCK),
            diff_attention(qb, kb_all, vb_all, lam, diff_subln[l], lambda_init, Q_BLOCK),
        ], axis=-1)
        x = x + gt1 * (lat_mix @ w_o[l])
        x = x + gt2 * moe_ffn(modulate(rms_norm(x, g_ffn[l]), sh2, sc2),
                              w_router[l], b_router[l], w_in[l], b_in[l], w_out[l], b_out[l])

        if l < DEPTH - 1:
            qa_c = rms_norm(qa_c, gqa_q_norm[l])
            ctx_len = ctx.shape[1]
            ctx_mix = jnp.concatenate([
                gqa_attention(qa_c, ka_c, va_c, ctx_len),
                diff_attention(qb_c, kb_c, vb_c, lam, diff_subln[l], lambda_init, ctx_len),
            ], axis=-1)
            ctx = ctx + cgt1 * (ctx_mix @ w_o[l])
            ctx = ctx + cgt2 * moe_ffn(modulate(rms_norm(ctx, g_ffn[l]), csh2, csc2),
                                       w_router[l], b_router[l], w_in[l], b_in[l], w_out[l], b_out[l])
    return rms_norm(x, g_final)


DEPTH_2 = 2

N_MIXERS = 2
N_RET = (DEPTH_2 + 1) // 2
N_S5 = DEPTH_2 // 2
RET_HEADS = 4
RET_DK = D_MODEL // RET_HEADS
RET_DV = 2 * RET_DK
RET_QK = RET_HEADS * RET_DK
RET_V = RET_HEADS * RET_DV
RET_PROJ = 2 * RET_QK + 2 * RET_V
RET_CHUNK = 128
ROPE_BASE = 10000.0
S5_GROUP = 16
S5_GROUPS = D_MODEL // S5_GROUP
S5_STATE = 64
DT_MIN = 1e-3
DT_MAX = 1e-1
D_FF_2 = 2816
CONV_W = 3


def rms_norm_2(x):
    xf = x.astype(jnp.float32)
    return (xf * lax.rsqrt(jnp.mean(xf * xf, axis=-1, keepdims=True) + EPS)).astype(x.dtype)

def rotary(t, pos):
    half = t.shape[-1] // 2
    inv_freq = jnp.power(ROPE_BASE, -jnp.arange(half, dtype=jnp.float32) / half)
    ang = pos.astype(jnp.float32)[..., None] * inv_freq
    cos = jnp.cos(ang)[:, :, None, :]
    sin = jnp.sin(ang)[:, :, None, :]
    t1 = t[..., :half].astype(jnp.float32)
    t2 = t[..., half:].astype(jnp.float32)
    return jnp.concatenate([t1 * cos - t2 * sin, t1 * sin + t2 * cos], axis=-1).astype(t.dtype)

def retention_chunkwise(q, k, v):
    bsz, L = q.shape[0], q.shape[1]
    nc = L // RET_CHUNK
    log_gamma = jnp.log1p(-jnp.exp2(-5.0 - jnp.arange(RET_HEADS, dtype=jnp.float32)))
    idx = jnp.arange(RET_CHUNK, dtype=jnp.float32)
    diff = idx[:, None] - idx[None, :]
    intra = jnp.where(diff[None] >= 0,
                      jnp.exp(log_gamma[:, None, None] * jnp.maximum(diff, 0.0)[None]), 0.0)
    cross = jnp.exp(log_gamma[:, None] * (idx + 1.0))
    to_state = jnp.exp(log_gamma[:, None] * (RET_CHUNK - 1.0 - idx))
    chunk_decay = jnp.exp(log_gamma * RET_CHUNK)

    def to_chunks(t):
        return t.reshape(bsz, nc, RET_CHUNK, RET_HEADS, t.shape[-1]).transpose(1, 0, 3, 2, 4)

    def step(state, qkv):
        qc, kc, vc = qkv
        s = jnp.einsum('bhnd,bhmd->bhnm', qc, kc) * intra[None]
        o = (jnp.einsum('bhnm,bhmv->bhnv', s, vc)
             + jnp.einsum('bhnd,bhdv->bhnv', qc, state) * cross[None, :, :, None])
        state = (chunk_decay[None, :, None, None] * state
                 + jnp.einsum('bhmd,bhmv->bhdv', kc * to_state[None, :, :, None], vc))
        return state, o

    state0 = jnp.zeros((bsz, RET_HEADS, RET_DK, RET_DV), jnp.float32)
    _, o = lax.scan(step, state0, (to_chunks(q), to_chunks(k), to_chunks(v)))
    return o.transpose(1, 0, 3, 2, 4).reshape(bsz, L, RET_HEADS, RET_DV)

def retention_mixer(h, pos, w_in, w_out):
    bsz, L, _ = h.shape
    proj = h @ w_in
    q, k, v, g = jnp.split(proj, [RET_QK, 2 * RET_QK, 2 * RET_QK + RET_V], axis=-1)
    q = rotary(q.reshape(bsz, L, RET_HEADS, RET_DK), pos)
    k = rotary(k.reshape(bsz, L, RET_HEADS, RET_DK), pos) * (RET_DK ** -0.5)
    v = v.reshape(bsz, L, RET_HEADS, RET_DV)
    o = retention_chunkwise(q.astype(jnp.float32), k.astype(jnp.float32), v.astype(jnp.float32))
    mu = jnp.mean(o, axis=-1, keepdims=True)
    oc = o - mu
    o = oc * lax.rsqrt(jnp.mean(oc * oc, axis=-1, keepdims=True) + EPS)
    o = o.reshape(bsz, L, RET_V).astype(h.dtype)
    return (jax.nn.silu(g) * o) @ w_out

def s5_mixer(h, w_in, lam_re, lam_im, log_dt, b_re, b_im, c_re, c_im, d_skip, w_glu):
    bsz, L, _ = h.shape
    u = (h @ w_in).astype(jnp.float32)
    ug = u.reshape(bsz, L, S5_GROUPS, S5_GROUP)
    dt = jnp.exp(log_dt.astype(jnp.float32))[:, None]
    lr = lam_re.astype(jnp.float32)
    li = lam_im.astype(jnp.float32)
    mag = jnp.exp(lr * dt)
    ar = mag * jnp.cos(li * dt)
    ai = mag * jnp.sin(li * dt)
    nr = ar - 1.0
    den = lr * lr + li * li
    fr = (nr * lr + ai * li) / den
    fi = (ai * lr - nr * li) / den
    br = b_re.astype(jnp.float32)
    bi = b_im.astype(jnp.float32)
    bbr = fr[..., None] * br - fi[..., None] * bi
    bbi = fr[..., None] * bi + fi[..., None] * br
    bu_r = jnp.einsum('blgi,gpi->lbgp', ug, bbr)
    bu_i = jnp.einsum('blgi,gpi->lbgp', ug, bbi)
    a_r = jnp.broadcast_to(ar[None, None], (L, 1, S5_GROUPS, S5_STATE))
    a_i = jnp.broadcast_to(ai[None, None], (L, 1, S5_GROUPS, S5_STATE))

    def combine(e1, e2):
        a1r, a1i, b1r, b1i = e1
        a2r, a2i, b2r, b2i = e2
        return (a2r * a1r - a2i * a1i,
                a2r * a1i + a2i * a1r,
                a2r * b1r - a2i * b1i + b2r,
                a2r * b1i + a2i * b1r + b2i)

    _, _, s_r, s_i = lax.associative_scan(combine, (a_r, a_i, bu_r, bu_i), axis=0)
    y = (jnp.einsum('lbgp,gip->blgi', s_r, c_re.astype(jnp.float32))
         - jnp.einsum('lbgp,gip->blgi', s_i, c_im.astype(jnp.float32)))
    y = y.reshape(bsz, L, D_MODEL) + d_skip.astype(jnp.float32) * u
    y = jax.nn.gelu(y).astype(h.dtype)
    ya, yb = jnp.split(y @ w_glu, 2, axis=-1)
    return ya * jax.nn.sigmoid(yb)

def conv_ffn(h, w_up, conv_w, conv_b, w_down):
    val, gate = jnp.split(h @ w_up, 2, axis=-1)
    gate = lax.conv_general_dilated(gate, conv_w.astype(gate.dtype), window_strides=(1,),
                                    padding=[(CONV_W - 1, 0)],
                                    dimension_numbers=('NWC', 'WIO', 'NWC'),
                                    feature_group_count=D_FF_2) + conv_b
    return (jax.nn.silu(gate) * val) @ w_down

def second_inputs(seed: int = 0) -> dict:
    key = jax.random.key(seed)
    ks = jax.random.split(key, 24)
    f32 = jnp.float32
    nrm = lambda k, shape, s: jax.random.normal(k, shape, f32) * s
    x = nrm(ks[0], (BATCH, SEQ, D_MODEL), 1.0)
    c = nrm(ks[1], (BATCH, D_MODEL), 1.0)
    offset = jax.random.randint(ks[2], (BATCH, 1), 0, 1024, dtype=jnp.int32)
    pos = offset + jnp.arange(SEQ, dtype=jnp.int32)[None, :]
    ada_w = nrm(ks[3], (DEPTH_2, D_MODEL, 6 * D_MODEL), D_MODEL ** -0.5)
    ada_b = nrm(ks[4], (DEPTH_2, 6 * D_MODEL), 0.02)
    ret_w_in = nrm(ks[5], (N_RET, D_MODEL, RET_PROJ), D_MODEL ** -0.5)
    ret_w_out = nrm(ks[6], (N_RET, RET_V, D_MODEL), RET_V ** -0.5)
    s5_w_in = nrm(ks[7], (N_S5, D_MODEL, D_MODEL), D_MODEL ** -0.5)
    s5_lam_re = -0.5 * jnp.exp(nrm(ks[8], (N_S5, S5_GROUPS, S5_STATE), 0.02))
    s5_lam_im = (math.pi * jnp.arange(S5_STATE, dtype=f32))[None, None, :] + nrm(ks[9], (N_S5, S5_GROUPS, S5_STATE), 0.01)
    s5_log_dt = jax.random.uniform(ks[10], (N_S5, S5_GROUPS), f32, math.log(DT_MIN), math.log(DT_MAX))
    s5_b_re = nrm(ks[11], (N_S5, S5_GROUPS, S5_STATE, S5_GROUP), (2 * S5_GROUP) ** -0.5)
    s5_b_im = nrm(ks[12], (N_S5, S5_GROUPS, S5_STATE, S5_GROUP), (2 * S5_GROUP) ** -0.5)
    s5_c_re = nrm(ks[13], (N_S5, S5_GROUPS, S5_GROUP, S5_STATE), S5_STATE ** -0.5)
    s5_c_im = nrm(ks[14], (N_S5, S5_GROUPS, S5_GROUP, S5_STATE), S5_STATE ** -0.5)
    s5_d = nrm(ks[15], (N_S5, D_MODEL), 1.0)
    s5_w_glu = nrm(ks[16], (N_S5, D_MODEL, 2 * D_MODEL), D_MODEL ** -0.5)
    ffn_w_up = nrm(ks[17], (DEPTH_2, D_MODEL, 2 * D_FF_2), D_MODEL ** -0.5)
    ffn_conv_w = nrm(ks[18], (DEPTH_2, CONV_W, 1, D_FF_2), CONV_W ** -0.5)
    ffn_conv_b = nrm(ks[19], (DEPTH_2, D_FF_2), 0.02)
    ffn_w_down = nrm(ks[20], (DEPTH_2, D_FF_2, D_MODEL), D_FF_2 ** -0.5)
    final_norm_g = 1.0 + nrm(ks[21], (D_MODEL,), 0.02)
    return {"x": x, "c": c, "pos": pos, "ada_w": ada_w, "ada_b": ada_b,
            "ret_w_in": ret_w_in, "ret_w_out": ret_w_out,
            "s5_w_in": s5_w_in, "s5_lam_re": s5_lam_re, "s5_lam_im": s5_lam_im,
            "s5_log_dt": s5_log_dt, "s5_b_re": s5_b_re, "s5_b_im": s5_b_im,
            "s5_c_re": s5_c_re, "s5_c_im": s5_c_im, "s5_d": s5_d, "s5_w_glu": s5_w_glu,
            "ffn_w_up": ffn_w_up, "ffn_conv_w": ffn_conv_w, "ffn_conv_b": ffn_conv_b,
            "ffn_w_down": ffn_w_down, "final_norm_g": final_norm_g}

def second_block(x, c, pos, ada_w, ada_b, ret_w_in, ret_w_out, s5_w_in, s5_lam_re, s5_lam_im,
              s5_log_dt, s5_b_re, s5_b_im, s5_c_re, s5_c_im, s5_d, s5_w_glu,
              ffn_w_up, ffn_conv_w, ffn_conv_b, ffn_w_down, final_norm_g):
    cond = jax.nn.silu(c)
    for i in range(DEPTH_2):
        mod = cond @ ada_w[i] + ada_b[i]
        sh1, sc1, g1, sh2, sc2, g2 = jnp.split(mod[:, None, :], 6, axis=-1)
        h = rms_norm_2(x) * (1.0 + sc1) + sh1
        j = i // N_MIXERS
        if i % N_MIXERS == 0:
            y = retention_mixer(h, pos, ret_w_in[j], ret_w_out[j])
        else:
            y = s5_mixer(h, s5_w_in[j], s5_lam_re[j], s5_lam_im[j], s5_log_dt[j],
                         s5_b_re[j], s5_b_im[j], s5_c_re[j], s5_c_im[j], s5_d[j], s5_w_glu[j])
        x = x + g1 * y
        h = rms_norm_2(x) * (1.0 + sc2) + sh2
        x = x + g2 * conv_ffn(h, ffn_w_up[i], ffn_conv_w[i], ffn_conv_b[i], ffn_w_down[i])
    return rms_norm_2(x) * final_norm_g


def setup_inputs(seed=0):
    out = dict(first_inputs(seed))
    for name, value in second_inputs(seed + 1).items():
        if name != "x":
            out[name + "_2"] = value
    return out


def reference(
    x, c, ctx, c_ctx, w_ada, b_ada, g_attn, w_qkv, gqa_q_norm, gqa_k_norm, diff_lambda,
    diff_subln, w_o, g_ffn, w_router, b_router, w_in, b_in, w_out, b_out, g_final, c_2, pos_2,
    ada_w_2, ada_b_2, ret_w_in_2, ret_w_out_2, s5_w_in_2, s5_lam_re_2, s5_lam_im_2, s5_log_dt_2,
    s5_b_re_2, s5_b_im_2, s5_c_re_2, s5_c_im_2, s5_d_2, s5_w_glu_2, ffn_w_up_2, ffn_conv_w_2,
    ffn_conv_b_2, ffn_w_down_2, final_norm_g_2,
):
    x = first_block(
        x, c, ctx, c_ctx, w_ada, b_ada, g_attn, w_qkv, gqa_q_norm, gqa_k_norm, diff_lambda,
        diff_subln, w_o, g_ffn, w_router, b_router, w_in, b_in, w_out, b_out, g_final,
    )
    return second_block(
        x, c_2, pos_2, ada_w_2, ada_b_2, ret_w_in_2, ret_w_out_2, s5_w_in_2, s5_lam_re_2,
        s5_lam_im_2, s5_log_dt_2, s5_b_re_2, s5_b_im_2, s5_c_re_2, s5_c_im_2, s5_d_2,
        s5_w_glu_2, ffn_w_up_2, ffn_conv_w_2, ffn_conv_b_2, ffn_w_down_2, final_norm_g_2,
    )


_drawn_inputs = setup_inputs


def setup_inputs(seed=0):
    import zlib

    import numpy as np

    out = dict(_drawn_inputs(seed))
    spreads = {}
    factors = {'g_attn': 3.538,
     'gqa_q_norm': 8.0,
     'gqa_k_norm': 8.0,
     'b_router': 3.978,
     'b_in': 8.0,
     'b_out': 8.0,
     's5_lam_re_2': 64.0,
     's5_log_dt_2': 16.211,
     's5_b_re_2': 25.743,
     's5_b_im_2': 24.979,
     's5_c_re_2': 23.706,
     's5_c_im_2': 28.024,
     'ffn_conv_b_2': 5.172,
     'final_norm_g_2': 7.944,
     'diff_subln': 3.825,
     's5_lam_im_2': 5.839}
    for name, (base, spread) in spreads.items():
        noise = np.random.default_rng([zlib.crc32(name.encode()), seed]).standard_normal(out[name].shape)
        drawn = base * np.exp(spread * noise) if base else spread * noise
        out[name] = __import__('jax').numpy.asarray(drawn.astype(out[name].dtype))
    for name, factor in factors.items():
        out[name] = (out[name] * factor).astype(out[name].dtype)
    return out
```

```python
from contextlib import ExitStack

import numpy as np

import concourse.bass as bass
from concourse import mybir

F32 = mybir.dt.float32
I32 = mybir.dt.int32
U32 = mybir.dt.uint32
ALU = mybir.AluOpType
ACT = mybir.ActivationFunctionType
AX_X = mybir.AxisListType.X

P = 128
T = 256
TT = T // P
D = 1024
KD = D // P
HD = 64
EPS = 1e-6
N_KEYS = 512
KEY_TILES = N_KEYS // P
QKV = 2304
HEADS = 8
ATT_SCALE = HD ** -0.5
LAMBDA_INIT = 0.2
E = 32
TOP_K = 4
CAP = 72
PASSES = -(-T // CAP)
PAIRS = E // 2
ALPHA = 1.702
LIMIT = 7.0
RET_HEADS = 4
RET_DV_TILES = 4
FF = 2816
KF = FF // P
GROUPS = 64
STATE = 64
GROUP = 16
S5_PAIRS = GROUPS // 2
GELU_C = float(np.sqrt(2.0 / np.pi))
TWO_PI = 2.0 * np.pi
ROUND = 1.5 * 2.0 ** 23
PI2_A = 6.28125
PI2_B = float(np.float32(np.float32((TWO_PI - PI2_A) * 2 ** 20).round() / 2 ** 20))
PI2_C = float(TWO_PI - PI2_A - PI2_B)
PI_IN = 3.1415925
RING = 6
SLAB = 4096
BANK = 512
ARENA = 17500

SMALL = {}
_at = 0
for _name, _width in (
    ("cond", 16), ("b_ada", 48), ("g_attn", 8), ("g_q", 1), ("g_k", 1), ("g_sub", 1), ("g_ffn", 8),
    ("g_final", 8), ("b_in", E * 16), ("cond2", 8), ("b_ada2", 96), ("lam_re", S5_PAIRS),
    ("lam_im", S5_PAIRS), ("log_dt", S5_PAIRS), ("s5_d", 8), ("conv_w", 2 * 3 * KF),
    ("conv_b", 2 * KF), ("g_final2", 8), ("dlam", 4 * HD), ("b_router", E),
):
    SMALL[_name] = (_at, _width)
    _at += _width
N_SMALL = _at

CONST = {}
_at = 0
for _name, _width in (
    ("ident", P), ("ones", P), ("head_ones", P), ("rope_perm", P), ("rope_cos", T), ("rope_sin", T),
    ("before", P), ("slots", PASSES * CAP), ("experts", E), ("inv_freq", 1), ("in_mask", 2),
    ("state_mask", 2), ("eps", 1), ("decay", RET_HEADS * 2 * T),
):
    CONST[_name] = (_at, _width)
    _at += _width
N_CONST = _at


def constants():
    c = np.zeros((P, N_CONST), np.float32)

    def put(name, a):
        at, width = CONST[name]
        c[:, at:at + width] = np.asarray(a, np.float32).reshape(P, width)

    p = np.arange(P)
    put("ident", np.eye(P))
    put("ones", np.ones((P, P)))
    put("head_ones", (p[:, None] // HD) == (p[None, :] // HD))
    perm = np.zeros((P, P))
    for d in range(P):
        first = d % 32 < 16
        perm[d + 16 if first else d - 16, d] = -1.0 if first else 1.0
    put("rope_perm", perm)
    n_freq = HD // 4
    inv = (np.float32(10000.0) ** (-np.arange(n_freq, dtype=np.float32) / n_freq)).astype(np.float32)
    t = np.arange(T)
    place = np.where((p[:, None] % HD) < 32, t[None] // 64, t[None] % 64).astype(np.float32)
    ang = (place * inv[p % 16][:, None]).astype(np.float32).astype(np.float64)
    put("rope_cos", np.cos(ang))
    put("rope_sin", np.sin(ang))
    put("before", p[:, None] < p[None, :])
    put("slots", np.broadcast_to(np.arange(PASSES * CAP), (P, PASSES * CAP)))
    put("experts", np.broadcast_to(np.arange(E), (P, E)))
    half = P
    put("inv_freq", np.float32(10000.0) ** (-np.arange(half, dtype=np.float32) / half))
    put("in_mask", np.stack([(p // GROUP) % 2 == g for g in range(2)], 1))
    put("state_mask", np.stack([p // STATE == g for g in range(2)], 1))
    put("eps", np.full((P, 1), EPS))
    lag = t[None, None, :] - (p[:, None, None] + P * np.arange(2)[None, :, None])
    decay = np.zeros((P, RET_HEADS, 2, T))
    for h in range(RET_HEADS):
        log_gamma = np.log1p(-2.0 ** (-5.0 - h))
        decay[:, h] = np.where(lag >= 0, np.exp(log_gamma * np.maximum(lag, 0)), 0.0) / 16.0
    put("decay", decay)
    return c



def plan():
    chunks, slabs = {}, {}

    def chunk(*keys):
        for k in keys:
            assert k not in chunks
            chunks[k] = len(chunks)

    def slab(key, n):
        for i in range(n):
            chunk((key, i))
        slabs[key] = len(chunks)

    for s in range(4):
        slab(("ada", s), 1)
    chunk(("norm", 0), ("norm", 1))
    slab("qa", 2)
    slab("kva", 2)
    slab("qb", 2)
    slab("kb", 4)
    slab("vb", 4)
    for i in range(5):
        chunk(("qknorm", i))
    for i in range(9):
        chunk(("rope", i))
    ada = [("ada", s) for s in range(4, 12)] + [("ada2", 0, s) for s in range(12)]
    for j in range(12):
        for _ in range(2 if j < 8 else 1):
            slab(ada.pop(0), 1)
        if j < 8:
            if j % 2:
                chunk(("oa", j // 2))
        else:
            chunk(("ob", j - 8))
    assert not ada
    chunk(*(("onorm", i) for i in range(2)))
    slab("wo0", 2)
    slab("wo1", 2)
    chunk(("norm", 2), ("router", 0), ("htok", 0), ("htok", 1), ("htok", 2), ("htok", 3), ("pos", 0),
          ("gates", 0), *(("bout", i) for i in range(4)))
    before_loop = (len(chunks), len(slabs))
    chunk(("norm", 3), ("norm", 4))
    for s in range(2):
        slab(("rq", s), 2)
    for s in range(2):
        slab(("rk", s), 2)
    for s in range(4):
        slab(("rv", s), 2)
    for s in range(4):
        slab(("rg", s), 2)
    for h in range(RET_HEADS):
        chunk(("rs", h), ("ro", h, 0), ("ro", h, 1), ("rmean", h), ("rvar", h))
    for s in range(4):
        slab(("rout", s), 1)

    def ffn(layer):
        chunk(("norm", 5 + 2 * layer))
        for s in range(11):
            slab(("up", layer, s), 2)
        for s in range(8):
            slab(("down", layer, s), 1)

    ffn(0)
    for s in range(12):
        slab(("ada2", 1, s), 1)
    chunk(("norm", 6))
    for s in range(2):
        slab(("s5in", s), 2)
    for j in range(8):
        for q in range(4):
            chunk(("bu", 4 * j + q))
        chunk(("s5y", j))
    for s in range(4):
        slab(("glu", s), 2)
    ffn(1)
    chunk(("norm", 8))
    return chunks, slabs, before_loop


CHUNK, SLABS, (CHUNKS_1, SLABS_1) = plan()
SLAB_KEYS = list(SLABS)
MOE_SLABS = 12 * PAIRS


def slab_number(key):
    n = SLAB_KEYS.index(key)
    return n if n < SLABS_1 else n + MOE_SLABS


class Steps:

    def __init__(self, eng, sem, base=0):
        self.eng, self.sem, self.base, self.n = eng, sem, base, 0

    def mark(self, ins):
        ins.then_inc(self.sem, 1)
        self.n += 1

    def link(self, ins):
        self.mark(ins)
        self.eng.wait_ge(self.sem, self.base + self.n)


def transformer_blocks_kernel(nc, small, const, xT, cT, pos, w_ada, w_qkv, w_o, w_router, w_in,
                              w_out, b_out, w_ada2, w_ret, w_rout, w_s5in, s5_b, s5_c, w_glu, w_up,
                              w_down, outT):
    ctx = ExitStack()
    with ctx:
        def sb(name, shape, dt=F32):
            return ctx.enter_context(nc.sbuf_tensor(name, shape, dt))

        def sem(name):
            return ctx.enter_context(nc.semaphore(name))

        ring = sb("ring", [P, RING, SLAB])
        consts = sb("consts", [P, N_CONST])
        smalls = sb("smalls", [P, N_SMALL])
        x = sb("x", [P, KD, T])
        sq = sb("sq", [P, KD, T])
        rstd = sb("rstd", [P, 4, T])
        mod = sb("mod", [P, 48, 2])
        mod2 = sb("mod2", [P, 2, 48])
        aff = sb("aff", [P, 8, KD])
        tiny = sb("tiny", [P, 640])
        arena = sb("arena", [P, ARENA])
        psum = ctx.enter_context(nc.psum_tensor("psum", [P, 8, BANK], F32))

        def con(name, *dims):
            at, width = CONST[name]
            return consts[:, at:at + width]

        def sml(name):
            at, width = SMALL[name]
            return smalls[:, at:at + width]

        def flat(ap):
            return ap.rearrange("p a b -> p (a b)")

        class Carve:

            def __init__(self, at=0):
                self.at = at

            def __call__(self, *shape):
                n = int(np.prod(shape))
                a = arena[:, self.at:self.at + n]
                self.at += n
                assert self.at <= ARENA, self.at
                if len(shape) == 2:
                    return a.rearrange("p (a b) -> p a b", b=shape[1])
                if len(shape) == 3:
                    return a.rearrange("p (a b c) -> p a b c", b=shape[1], c=shape[2])
                return a

        cut = Carve()
        h_all = cut(KD, N_KEYS)
        q_all = cut(8, T)
        k_all = cut(5, N_KEYS)
        v_all = cut(KEY_TILES, 640)
        rope_t = cut(2, BANK)
        ctx_x = cut(KD, T)
        probs = ctx_x.rearrange("p k t -> p (k t)").rearrange("p (a b) -> p a b", b=N_KEYS)
        p_t = cut(2, KEY_TILES * T)
        diag = cut(4, P)
        mix = h_all[:, :, 0:T]
        soft = tiny[:, 0:128].rearrange("p (a b) -> p a b", b=4)
        lam = tiny[:, 256:264]
        lam_prod = tiny[:, 264:392].rearrange("p (a b) -> p a b", b=HD)

        cut = Carve()
        h_moe = cut(KD, T)
        h_tok = cut(TT, D)
        y_moe = cut(KD, T)
        x_e = cut(2, KD, CAP)
        glu = cut(2, KD, CAP)
        lin = cut(2, KD, CAP)
        tanh_e = cut(2, KD, CAP)
        y_e = cut(2, KD, CAP)
        y_slot = cut(2, D)
        g_slot = cut(2, T)
        sel = cut(2, TT, CAP)
        gsel = cut(2, TT, CAP)
        w_rt = cut(KD, E)
        b_out_sb = cut(D)
        logits = cut(TT, E)
        top = cut(TT, 8)
        top_i = cut(TT, 8)
        top_f = cut(TT, 8)
        top_e = cut(TT, 8)
        onehot = cut(2, E)
        mask = cut(TT, E)
        gate = cut(TT, E)
        slot_of = cut(TT, E)
        gates_t = cut(T)
        count = tiny[:, 400:432]
        max_count = tiny[:, 432:433]
        over = tiny[:, 433:434].bitcast(I32)
        gate_sum = tiny[:, 434:438]

        cut = Carve()
        h2 = cut(KD, T)
        after_h2 = cut.at
        rq = cut(8, T)
        rk = cut(8, T)
        rv = cut(TT, 2048)
        rg = cut(16, T)
        cos2 = cut(T)
        sin2 = cut(T)
        rot = cut(2, 2 * T)
        rs = cut(2 * T)
        ro = cut(4, T)
        cut = Carve(after_h2)
        val = cut(KF, T)
        conv = cut(2, 2 * T)
        conv_t = cut(2, 2 * T)
        cut = Carve(after_h2)
        u5 = cut(KD, T)
        y5 = cut(KD, T)
        gl = cut(KD, T)
        tab = [[cut(4, T) for _ in range(2)] for _ in range(2)]
        tab_t = cut(4, P)
        tab_u = cut(4, P)
        z1 = cut(2, T)
        z2 = cut(2, T)
        z3 = cut(2, T)
        z4 = cut(2, T)
        b_bd = cut(2, 8, P)
        c_bd = flat(sq[:]).rearrange("p (a b c) -> p a b c", a=2, b=S5_PAIRS)
        b_in5 = flat(y5)[:, 0:1024].rearrange("p (a b c) -> p a b c", a=2, b=8)
        c_in5 = flat(y5)[:, 1024:2048].rearrange("p (a b c) -> p a b c", a=2, b=S5_PAIRS)
        c_f = flat(gl)[:, 0:1024].rearrange("p (a b c) -> p a b c", a=2, b=S5_PAIRS)
        s5 = tiny[:, 0:16 * S5_PAIRS].rearrange("p (a b) -> p a b", b=S5_PAIRS)

        small_in = sem("small_in")
        const_in = sem("const_in")
        x_in = sem("x_in")
        ctx_in = sem("ctx_in")
        router_in = sem("router_in")
        bout_in = sem("bout_in")
        pos_in = sem("pos_in")
        s5_in = sem("s5_in")
        ring_full = [sem(f"ring_full{i}") for i in range(RING)]
        stored = sem("stored")
        acc_ready = sem("acc_ready")
        acc_free = [sem(f"acc_free{b}") for b in range(4)]
        cond_tanh = sem("cond_tanh")
        cond_ready = sem("cond_ready")
        affine_ready = sem("affine_ready")
        squares_ready = sem("squares_ready")
        guess_ready = sem("guess_ready")
        normed_ready = sem("normed_ready")
        h_ready = sem("h_ready")
        x_ready = sem("x_ready")
        act_g = sem("scaled_by_g")
        q_ready = sem("q_ready")
        qk_square = sem("qk_square")
        qk_guess = sem("qk_guess")
        q_normed = sem("q_normed")
        scores_ready = sem("scores_ready")
        max_ready = sem("max_ready")
        probs_ready = sem("probs_ready")
        diag_ready = sem("diag_ready")
        pt_written = sem("pt_written")
        pt_ready = sem("pt_ready")
        mix_ready = sem("mix_ready")
        lam_exp = sem("lam_exp")
        lam_sum = sem("lam_sum")
        top_ready = sem("top_ready")
        top_exp = sem("top_exp")
        mask_ready = sem("mask_ready")
        slots_ready = sem("slots_ready")
        y_init = sem("y_init")
        over_ready = sem("over_ready")
        pos_ready = sem("pos_ready")
        angle_ready = sem("angle_ready")
        sin_ready = sem("sin_ready")
        ret_tanh = sem("ret_tanh")
        ret_gate = sem("ret_gate")
        ret_qk = sem("ret_qk")
        ret_s = sem("ret_s")
        ret_o = sem("ret_o")
        ret_sq = sem("ret_sq")
        ret_guess = sem("ret_guess")
        ret_done = sem("ret_done")
        val_ready = sem("val_ready")
        conv_start = sem("conv_start")
        conv_ready = sem("conv_ready")
        conv_tanh = sem("conv_tanh")
        act_ready = sem("act_ready")
        s5_u = sem("s5_u")
        s5_dt = sem("s5_dt")
        s5_exp = sem("s5_exp")
        s5_angle = sem("s5_angle")
        s5_ab = sem("s5_ab")
        s5_table = sem("s5_table")
        s5_state = sem("s5_state")
        s5_bc = sem("s5_bc")
        s5_gelu_in = sem("s5_gelu_in")
        s5_gelu_t = sem("s5_gelu_t")
        s5_y = sem("s5_y")
        glu_tanh = sem("glu_tanh")
        dve_step = sem("dve_step")
        act_step = sem("act_step")
        pool_step = sem("pool_step")

        class MoeSems:
            def __init__(self, tag):
                self.g_ready = sem(f"expert_out_ready{tag}")
                self.g_free = [sem(f"expert_out_free{tag}_{b}") for b in range(4)]
                self.t_ready = sem(f"turned_ready{tag}")
                self.t_free = [sem(f"turned_free{tag}_{b}") for b in range(2)]
                self.s_ready = sem(f"scatter_ready{tag}")
                self.s_free = [sem(f"scatter_free{tag}_{b}") for b in range(2)]
                self.sel_ready = sem(f"select_ready{tag}")
                self.glu_ready = sem(f"glu_ready{tag}")
                self.tanh_ready = sem(f"tanh_ready{tag}")
                self.act_ready = sem(f"expert_act_ready{tag}")
                self.full = ring_full if tag == "" else [sem(f"ring_full{tag}_{i}") for i in range(RING)]
                self.step = sem(f"expert_step{tag}")
                self.done = sem(f"experts_done{tag}")

        moe = MoeSems("")
        again = MoeSems("_again")

        def cols(w, n0, n1):
            return w[:, n0:n1].rearrange("(k p) n -> p k n", p=P)

        def source(key):
            kind, s = (key, 0) if isinstance(key, str) else (key[0], key[-1])
            if kind == "ada":
                return cols(w_ada, BANK * s, BANK * s + BANK)
            if kind == "ada2":
                return cols(w_ada2[key[1]], BANK * s, BANK * s + BANK)
            if kind in QKV_COLS:
                return cols(w_qkv, *QKV_COLS[kind])
            if kind in ("wo0", "wo1"):
                n = int(kind[2])
                return cols(w_o, BANK * n, BANK * n + BANK)
            if kind in ("rq", "rk", "rv", "rg"):
                n = {"rq": 0, "rk": 2, "rv": 4, "rg": 8}[kind] + s
                return cols(w_ret, BANK * n, BANK * n + BANK)
            if kind == "rout":
                return w_rout[s]
            if kind == "up":
                return cols(w_up[key[1]], BANK * s, BANK * s + BANK)
            if kind == "down":
                return w_down[key[1], s]
            if kind == "s5in":
                return cols(w_s5in, BANK * s, BANK * s + BANK)
            assert kind == "glu"
            return cols(w_glu, BANK * s, BANK * s + BANK)

        QKV_COLS = {"qa": (0, 512), "kva": (512, 768), "qb": (768, 1280), "kb": (1280, 1792),
                    "vb": (1792, 2304)}

        def in_ring(slot, src):
            a, b = src.shape[1], src.shape[2]
            return ring[:, slot, 0:a * b].rearrange("p (a b) -> p a b", b=b)

        def slab(key):
            return in_ring(slab_number(key) % RING, source(key))

        def bank(key):
            return psum[:, CHUNK[key] % 4, :]

        def half(key, m):
            return psum[:, CHUNK[key] % 4, T * m:T * m + T]

        def two(ap):
            return ap.rearrange("p (a b) -> p a b", a=2)

        def over_tiles(ap, n):
            return ap.unsqueeze(1).to_broadcast([P, n, ap.shape[-1]])

        def read_ready(eng, key):
            eng.wait_ge(acc_ready, CHUNK[key] + 1)

        def read_done(ins, key):
            ins.then_inc(acc_free[CHUNK[key] % 4], 1)

        def copied(eng, key):
            eng.wait_ge(acc_free[CHUNK[key] % 4], CHUNK[key] // 4 + 1)

        MAPS = []
        for j in range(8):
            for b in range(2):
                MAPS.append((j // 2, HD * (j % 2), 0, b))
        for j in range(4):
            for b in range(2):
                for c in range(2):
                    MAPS.append((4 + j, HD * c, 1 + j, b))

        TURN_OF = [u if u < 16 else 16 + (u - 16) // 2 for u in range(32)]
        NEW_MAPS = [[n + 2] if n < 16 else [u for u in (2 * n - 14, 2 * n - 13) if u < 32] for n in range(24)]

        X_READY = {2: 1, 3: 2, 4: 3, 5: 4, 6: 5, 7: 6, 8: 7, "out": 8}
        NORMS = {
            0: (ctx_x, h_all[:, :, 0:T], 0, mod[:, 0:8, 1]),
            1: (x, h_all[:, :, T:N_KEYS], 1, mod[:, 0:8, 0]),
            2: (x, h_moe, 2, mod[:, 24:32, 0]),
            3: (x, x, None, None),
            4: (x, h2, 3, mod2[:, 0, 0:8]),
            5: (x, h2, 4, mod2[:, 0, 24:32]),
            6: (x, h2, 5, mod2[:, 1, 0:8]),
            7: (x, h2, 6, mod2[:, 1, 24:32]),
            8: (x, x, None, None),
        }
        G_ONLY = {3: "g_final", 8: "g_final2"}
        H_BASE = {0: 0, 1: 8, 2: 16, 4: 24, 5: 32, 6: 40, 7: 48}
        AFFINE = {0: 1, 1: 1, 2: 2, 4: 3, 5: 3, 6: 4, 7: 4}

        block = ctx.enter_context(nc.Block())

        @block.sync
        def _(sp):
            sp.dma_start(smalls[:], small).then_inc(small_in, 16)

            def load(n, src):
                sp.dma_start(in_ring(n % RING, src), src).then_inc(ring_full[n % RING], 16)

            def expert_source(e, j):
                if j < 8:
                    w = w_in[bass.ds(e + j // 4, 1)].rearrange("a k n -> (a k) n")
                    return cols(w, BANK * (j % 4), BANK * (j % 4) + BANK)
                w = w_out[bass.ds(e + (j - 8) // 2, 1)].rearrange("a k n -> (a k) n")
                return cols(w, BANK * (j % 2), BANK * (j % 2) + BANK)

            for n, key in enumerate(SLAB_KEYS[:SLABS_1]):
                if n >= RING:
                    sp.wait_ge(acc_ready, SLABS[SLAB_KEYS[n - RING]])
                load(n, source(key))
                if n == 0:
                    sp.dma_start(consts[:], const).then_inc(const_in, 16)
                    sp.dma_start(ctx_x, cT.rearrange("(k p) t -> p k t", p=P)).then_inc(ctx_in, 16)
                    sp.dma_start(x[:], xT.rearrange("(k p) t -> p k t", p=P)).then_inc(x_in, 16)
            for j in range(12):
                if j < RING:
                    sp.wait_ge(acc_ready, SLABS[SLAB_KEYS[SLABS_1 + j - RING]])
                else:
                    sp.wait_ge(moe.g_ready, j - RING + 1)
                load(SLABS_1 + j, expert_source(0, j))
            with sp.Fori(1, PAIRS) as i:
                for j in range(12):
                    sp.wait_ge(moe.g_ready, i * 12 + (j - RING + 1))
                    load(SLABS_1 + j, expert_source(i * 2, j))

            sp.wait_ge(over_ready, 1)
            flag = sp.value_load(over[0:1, 0:1], min_val=0, max_val=1)
            with sp.If(flag > 0):
                sp.wait_ge(moe.g_ready, MOE_SLABS)
                with sp.Fori(0, PAIRS * (PASSES - 1)) as i:
                    for j in range(12):
                        if j < RING:
                            sp.wait_ge(again.g_ready, i * 12)
                        else:
                            sp.wait_ge(again.g_ready, i * 12 + (j - RING + 1))
                        src = expert_source((i % PAIRS) * 2, j)
                        slot = (SLABS_1 + j) % RING
                        sp.dma_start(in_ring(slot, src), src).then_inc(again.full[slot], 16)
                sp.wait_ge(again.done, 1)

            for n, key in enumerate(SLAB_KEYS[SLABS_1:]):
                if n < RING:
                    sp.wait_ge(moe.g_ready, MOE_SLABS - RING + n + 1)
                else:
                    sp.wait_ge(acc_ready, SLABS[SLAB_KEYS[SLABS_1 + n - RING]])
                load(slab_number(key), source(key))
            sp.wait_ge(x_ready, X_READY["out"])
            sp.dma_start(outT.rearrange("(k p) t -> p k t", p=P), x[:]).then_inc(stored, 16)
            sp.wait_ge(stored, 16)

        @block.tensor
        def _(pe):
            order = {"next": 0, "loop": False}

            def begin(key):
                c = CHUNK[key]
                assert c == order["next"], (key, c, order["next"])
                order["next"] += 1
                if c >= 4:
                    pe.wait_ge(acc_free[c % 4], c // 4)

            def end(ins):
                ins.then_inc(acc_ready, 1)

            def arrived(key):
                n = slab_number(key)
                pe.wait_ge(ring_full[n % RING], 16 * (n // RING + 1))

            def features(key, rhs, per_chunk, k_tiles=KD, m_tiles=4, first=None):
                arrived(key)
                w = slab(key)
                for m in range(m_tiles):
                    c = (key, m // per_chunk)
                    if m % per_chunk == 0:
                        begin(c)
                    width = BANK // per_chunk if per_chunk < 4 else 2
                    for k in range(k_tiles):
                        if m == 0 and first:
                            first(k)
                        r = rhs(k)
                        n = r.shape[-1]
                        at = (m % per_chunk) * width if per_chunk < 4 else (m % per_chunk) * n
                        ins = nc.tensor.matmul(bank(c)[:, at:at + n], w[:, k, m * P:m * P + P], r,
                                               start=(k == 0), stop=(k == k_tiles - 1))
                    if m % per_chunk == per_chunk - 1:
                        end(ins)

            def tokens(key, lhs, n_tok, width, at=0, first_chunk=0):
                w = slab(key)
                for t in range(n_tok):
                    begin((key, first_chunk + t))
                    for k in range(KD):
                        ins = nc.tensor.matmul(bank((key, first_chunk + t))[:, 0:width], lhs(k, t),
                                               w[:, k, at:at + width], start=(k == 0), stop=(k == KD - 1))
                    end(ins)

            def norm(i):
                begin(("norm", i))
                pe.wait_ge(squares_ready, i + 1)
                for k in range(KD):
                    ins = nc.tensor.matmul(half(("norm", i), 0), con("ones"), sq[:, k, :],
                                           start=(k == 0), stop=(k == KD - 1))
                end(ins)

            def h_tiles(i):
                return lambda k: pe.wait_ge(h_ready, H_BASE[i] + k + 1)

            cond = sml("cond").rearrange("p (k c) -> p k c", c=2)
            pe.wait_ge(cond_ready, 1)
            for s in range(4):
                features(("ada", s), lambda k: cond[:, k, :], 4)
            pe.wait_ge(const_in, 16)
            norm(0)
            norm(1)
            pe.wait_ge(h_ready, 8)
            features("qa", lambda k: h_all[:, k, T:N_KEYS], 2, first=h_tiles(1))
            arrived("kva")
            w = slab("kva")
            begin(("kva", 0))
            for k in range(KD):
                ins = nc.tensor.matmul(bank(("kva", 0)), w[:, k, 0:P], h_all[:, k, :],
                                       start=(k == 0), stop=(k == KD - 1))
            end(ins)
            begin(("kva", 1))
            for t in range(KEY_TILES):
                for k in range(KD):
                    ins = nc.tensor.matmul(bank(("kva", 1))[:, t * P:t * P + P],
                                           h_all[:, k, t * P:t * P + P], w[:, k, P:2 * P],
                                           start=(k == 0), stop=(k == KD - 1))
            end(ins)
            features("qb", lambda k: h_all[:, k, T:N_KEYS], 2)
            features("kb", lambda k: h_all[:, k, :], 1)
            arrived("vb")
            tokens("vb", lambda k, t: h_all[:, k, t * P:t * P + P], KEY_TILES, BANK)
            for i in range(5):
                begin(("qknorm", i))
                pe.wait_ge(qk_square, i + 1)
                width = T if i < 4 else N_KEYS
                end(nc.tensor.matmul(bank(("qknorm", i))[:, 0:width], con("head_ones"),
                                     sq[:, 2 * (i % 2):2 * (i % 2) + 2, :].rearrange("p a b -> p (a b)")[:, 0:width],
                                     start=True, stop=True))
            for i in range(9):
                begin(("rope", i))
                if i == 0:
                    pe.wait_ge(q_ready, 1)
                if i < 4:
                    src = q_all[:, 2 * i:2 * i + 2, :].rearrange("p a b -> p (a b)")
                else:
                    src = k_all[:, i - 4, T:N_KEYS]
                end(nc.tensor.matmul(bank(("rope", i))[:, 0:src.shape[-1]], con("rope_perm"), src,
                                     start=True, stop=True))

            def scores(u):
                if u >= 2:
                    pe.wait_ge(probs_ready, u - 1)
                if u == 0:
                    pe.wait_ge(q_ready, 1 + 9)
                tile, part, kt, b = MAPS[u]
                nc.tensor.matmul(psum[:, 4 + u % 2, :], q_all[part:part + HD, tile, b * P:b * P + P],
                                 k_all[part:part + HD, kt, :], start=True, stop=True
                                 ).then_inc(scores_ready, 1)

            def turn(n, maps):
                pe.wait_ge(diag_ready, maps[-1] + 1)
                if n >= 2:
                    pe.wait_ge(pt_ready, n - 1)
                for kt in range(KEY_TILES):
                    for u in maps:
                        ins = nc.tensor.matmul(psum[:, 6 + n % 2, kt * P:kt * P + P],
                                               probs[:, u % 4, kt * P:kt * P + P], diag[:, u % 4, :],
                                               start=(u == maps[0]), stop=(u == maps[-1]))
                ins.then_inc(pt_written, 1)

            ada = [("ada", s) for s in range(4, 12)] + [("ada2", 0, s) for s in range(12)]
            cond2 = sml("cond2").rearrange("p (k c) -> p k c", c=1)

            def ada_slab():
                key = ada.pop(0)
                rhs = (lambda k: cond[:, k, :]) if key[0] == "ada" else (lambda k: cond2[:, k, :])
                features(key, rhs, 4)

            scores(0)
            scores(1)
            for j in range(12):
                u0, n0 = (2 * j, 2 * j) if j < 8 else (16 + 4 * (j - 8), 16 + 2 * (j - 8))
                if j < 8:
                    for b in range(2):
                        u = 2 * j + b
                        turn(n0 + b, [u])
                        if u + 2 < 32:
                            scores(u + 2)
                    for _ in range(2):
                        ada_slab()
                    if j % 2:
                        begin(("oa", j // 2))
                        pe.wait_ge(pt_ready, n0 + 2)
                        for a in range(2):
                            for kt in range(KEY_TILES):
                                ins = nc.tensor.matmul(
                                    half(("oa", j // 2), 0)[a * HD:a * HD + HD],
                                    v_all[:, kt, a * HD:a * HD + HD],
                                    p_t[:, a, kt * T:kt * T + T], start=(kt == 0), stop=(kt == KEY_TILES - 1))
                        end(ins)
                else:
                    for b in range(2):
                        turn(n0 + b, [u0 + 2 * b, u0 + 2 * b + 1])
                        for c in range(2):
                            if u0 + 2 * b + c + 2 < 32:
                                scores(u0 + 2 * b + c + 2)
                    ada_slab()
                    begin(("ob", j - 8))
                    pe.wait_ge(pt_ready, n0 + 2)
                    for kt in range(KEY_TILES):
                        ins = nc.tensor.matmul(half(("ob", j - 8), 0),
                                               v_all[:, kt, P * (j - 7):P * (j - 7) + P],
                                               p_t[:, j % 2, kt * T:kt * T + T],
                                               start=(kt == 0), stop=(kt == KEY_TILES - 1))
                    end(ins)
            for i in range(2):
                begin(("onorm", i))
                pe.wait_ge(qk_square, 6 + i)
                end(nc.tensor.matmul(bank(("onorm", i)), con("ones"),
                                     sq[:, 2 * i:2 * i + 2, :].rearrange("p a b -> p (a b)"), start=True, stop=True))
            pe.wait_ge(mix_ready, 1)
            features("wo0", lambda k: mix[:, k, :], 2)
            features("wo1", lambda k: mix[:, k, :], 2)

            norm(2)
            begin(("router", 0))
            pe.wait_ge(router_in, 16)
            pe.wait_ge(h_ready, H_BASE[2] + 8)
            for t in range(TT):
                for k in range(KD):
                    ins = nc.tensor.matmul(bank(("router", 0))[:, t * E:t * E + E],
                                           h_moe[:, k, t * P:t * P + P], w_rt[:, k, :],
                                           start=(k == 0), stop=(k == KD - 1))
            end(ins)
            for c in range(4):
                begin(("htok", c))
                for m in range(4):
                    k = 4 * (c % 2) + m
                    ins = nc.tensor.matmul(bank(("htok", c))[:, m * P:m * P + P],
                                           h_moe[:, k, (c // 2) * P:(c // 2) * P + P], con("ident"),
                                           start=True, stop=True)
                end(ins)
            begin(("pos", 0))
            pe.wait_ge(mask_ready, 1)
            b = bank(("pos", 0))
            nc.tensor.matmul(b[:, 0:E], con("before"), mask[:, 0, :], start=True, stop=True)
            nc.tensor.matmul(b[:, E:2 * E], con("ones"), mask[:, 0, :], start=True, stop=False)
            nc.tensor.matmul(b[:, E:2 * E], con("before"), mask[:, 1, :], start=False, stop=True)
            nc.tensor.matmul(b[:, 2 * E:3 * E], con("ones"), mask[:, 0, :], start=True, stop=False)
            end(nc.tensor.matmul(b[:, 2 * E:3 * E], con("ones"), mask[:, 1, :], start=False, stop=True))
            begin(("gates", 0))
            for t in range(TT):
                ins = nc.tensor.matmul(bank(("gates", 0))[0:E, t * P:t * P + P], gate[:, t, :],
                                       con("ident"), start=True, stop=True)
            end(ins)
            for c in range(4):
                begin(("bout", c))
                if c == 0:
                    pe.wait_ge(bout_in, 16)
                    copied(pe, ("gates", 0))
                for m in range(2):
                    k = 2 * c + m
                    ins = nc.tensor.matmul(half(("bout", c), m), b_out_sb[0:E, k * P:k * P + P],
                                           gates_t[0:E, :], start=True, stop=True)
                end(ins)
            for c in range(4):
                copied(pe, ("bout", c))

            def gather(s, n, t0):
                pe.wait_ge(s.sel_ready, n)
                for c in range(4):
                    if isinstance(t0, int):
                        if c >= 2:
                            pe.wait_ge(s.t_free[c % 2], 1)
                    else:
                        pe.wait_ge(s.t_free[c % 2], t0 + c // 2)
                    for m in range(4):
                        k = 4 * (c % 2) + m
                        for t in range(TT):
                            ins = nc.tensor.matmul(psum[:, 4 + c % 2, m * CAP:m * CAP + CAP],
                                                   h_tok[:, t, k * P:k * P + P], sel[:, c // 2, t, :],
                                                   start=(t == 0), stop=(t == TT - 1))
                    ins.then_inc(s.t_ready, 1)

            def experts(s, i, full):
                def product(j, rhs):
                    full(j)
                    w = in_ring((SLABS_1 + j) % RING, source("wo0"))
                    pe.wait_ge(s.g_free[j % 4], i * 3 + j // 4)
                    for m in range(4):
                        for k in range(KD):
                            ins = nc.tensor.matmul(psum[:, j % 4, m * CAP:m * CAP + CAP],
                                                   w[:, k, m * P:m * P + P], rhs[:, k, :],
                                                   start=(k == 0), stop=(k == KD - 1))
                    ins.then_inc(s.g_ready, 1)

                for c in range(2):
                    pe.wait_ge(s.t_free[c], i * 5 + 2)
                for j in range(8):
                    product(j, x_e[:, j // 4])
                pe.wait_ge(s.act_ready, i * 2 + 1)
                for j in (8, 9):
                    product(j, lin[:, 0])
                pe.wait_ge(s.sel_ready, i + 2)
                for e in range(2):
                    pe.wait_ge(s.t_free[e], i * 5 + 2)
                    for t in range(TT):
                        ins = nc.tensor.matmul(psum[0:CAP, 4 + e, t * P:t * P + P], gsel[:, e, t, :],
                                               con("ident"), start=True, stop=True)
                    ins.then_inc(s.t_ready, 1)
                pe.wait_ge(s.act_ready, i * 2 + 2)
                for j in (10, 11):
                    product(j, lin[:, 1])
                for c in range(4):
                    e = c // 2
                    if c % 2 == 0:
                        pe.wait_ge(s.g_free[2 * e], i * 3 + 3)
                        pe.wait_ge(s.g_free[2 * e + 1], i * 3 + 3)
                    pe.wait_ge(s.t_free[c % 2], i * 5 + 3 + c // 2)
                    for m in range(4):
                        ins = nc.tensor.matmul(psum[0:CAP, 4 + c % 2, m * P:m * P + P],
                                               y_e[:, e, 4 * (c % 2) + m, :], con("ident"),
                                               start=True, stop=True)
                    ins.then_inc(s.t_ready, 1)
                gather(s, i + 2, i * 5 + 5)
                for c in range(4):
                    pe.wait_ge(s.s_free[c % 2], i * 2 + c // 2)
                    for m in range(2):
                        k = 2 * c + m
                        for e in range(2):
                            ins = nc.tensor.matmul(psum[:, 6 + c % 2, m * T:m * T + T],
                                                   y_slot[0:CAP, e, k * P:k * P + P], g_slot[0:CAP, e, :],
                                                   start=(e == 0), stop=(e == 1))
                    ins.then_inc(s.s_ready, 1)

            gather(moe, 1, 0)
            with pe.Fori(0, PAIRS) as i:
                def full(j):
                    n = SLABS_1 + j
                    pe.wait_ge(ring_full[n % RING], i * 32 + 16 * (n // RING + 1))
                experts(moe, i, full)
            pe.wait_ge(over_ready, 1)
            flag = pe.value_load(over[0:1, 0:1], min_val=0, max_val=1)
            with pe.If(flag > 0):
                gather(again, 1, 0)
                with pe.Fori(0, PAIRS * (PASSES - 1)) as i:
                    def full(j):
                        pe.wait_ge(again.full[(SLABS_1 + j) % RING], i * 32 + 16 * (j // RING + 1))
                    experts(again, i, full)
                pe.wait_ge(again.done, 1)

            norm(3)
            norm(4)
            for s in range(2):
                features(("rq", s), lambda k: h2[:, k, :], 2, first=h_tiles(4) if s == 0 else None)
            for s in range(2):
                features(("rk", s), lambda k: h2[:, k, :], 2)
            for s in range(4):
                arrived(("rv", s))
                tokens(("rv", s), lambda k, t: h2[:, k, t * P:t * P + P], TT, BANK)
            for s in range(4):
                features(("rg", s), lambda k: h2[:, k, :], 2)
            for h in range(RET_HEADS):
                begin(("rs", h))
                pe.wait_ge(ret_qk, 8)
                for m in range(TT):
                    for j in range(2):
                        ins = nc.tensor.matmul(half(("rs", h), m), rk[:, 2 * h + j, m * P:m * P + P],
                                               rq[:, 2 * h + j, :], start=(j == 0), stop=(j == 1))
                end(ins)
                for c in range(2):
                    begin(("ro", h, c))
                    if c == 0:
                        pe.wait_ge(ret_s, h + 1)
                        if h == 0:
                            for s in range(4):
                                for t in range(TT):
                                    copied(pe, (("rv", s), t))
                    for m in range(2):
                        for t in range(TT):
                            at = h * 512 + (2 * c + m) * P
                            ins = nc.tensor.matmul(half(("ro", h, c), m), rv[:, t, at:at + P],
                                                   rs[:, t * T:t * T + T], start=(t == 0), stop=(t == 1))
                    end(ins)
                begin(("rmean", h))
                copied(pe, ("ro", h, 0))
                copied(pe, ("ro", h, 1))
                for k in range(4):
                    ins = nc.tensor.matmul(half(("rmean", h), 0), con("ones"), ro[:, k, :],
                                           start=(k == 0), stop=(k == 3))
                end(ins)
                begin(("rvar", h))
                pe.wait_ge(ret_sq, h + 1)
                for k in range(4):
                    ins = nc.tensor.matmul(half(("rvar", h), 0), con("ones"), sq[:, k, :],
                                           start=(k == 0), stop=(k == 3))
                end(ins)
            pe.wait_ge(ret_done, RET_HEADS)
            for s in range(4):
                features(("rout", s), lambda k: rg[:, k, :], 2, k_tiles=16, m_tiles=2)

            def ffn(layer):
                norm(5 + 2 * layer)
                for s in range(11):
                    features(("up", layer, s), lambda k: h2[:, k, :], 2,
                             first=h_tiles(5 + 2 * layer) if s == 0 else None)
                for s in range(8):
                    features(("down", layer, s), lambda k: val[:, k, :], 1, k_tiles=KF, m_tiles=1,
                             first=(lambda k: pe.wait_ge(act_ready, 11 * layer + k // 2 + 1)) if s == 0 else None)

            ffn(0)
            for s in range(12):
                features(("ada2", 1, s), lambda k: cond2[:, k, :], 4)
            norm(6)
            for s in range(2):
                features(("s5in", s), lambda k: h2[:, k, :], 2, first=h_tiles(6) if s == 0 else None)
            pe.wait_ge(s5_bc, 1)
            for c in range(2):
                for s in range(2):
                    copied(pe, (("s5in", s), c))
            for j in range(8):
                for q in range(4):
                    key = ("bu", 4 * j + q)
                    begin(key)
                    for c in range(2):
                        ins = nc.tensor.matmul(half(key, c), b_bd[32 * q:32 * q + 32, c, j, :],
                                               u5[32 * q:32 * q + 32, j, :], start=True, stop=True)
                    end(ins)
                begin(("s5y", j))
                for q in range(4):
                    pe.wait_ge(s5_state, 4 * j + q + 1)
                    zz = z3 if q % 2 == 0 else z4
                    for c in range(2):
                        ins = nc.tensor.matmul(half(("s5y", j), 0)[32 * q:32 * q + 32],
                                               c_bd[:, c, 4 * j + q, :], zz[:, c, :],
                                               start=(c == 0), stop=(c == 1))
                    if q < 3:
                        ins.then_inc(s5_u, 1)
                end(ins)
            pe.wait_ge(s5_y, 8)
            for s in range(4):
                features(("glu", s), lambda k: y5[:, k, :], 2)
            ffn(1)
            norm(8)

        @block.scalar
        def _(act):
            own = Steps(act, act_step)

            def norm(i):
                src = NORMS[i][0]
                if i == 0:
                    act.wait_ge(ctx_in, 16)
                elif i == 1:
                    act.wait_ge(x_in, 16)
                    read_ready(act, ("norm", 0))
                else:
                    act.wait_ge(x_ready, X_READY[i])
                nc.scalar.activation(sq[:], src[:], ACT.Square).then_inc(squares_ready, 1)

            def guess(key, out, width, n, signal):
                read_ready(act, key)
                own.link(nc.scalar.activation(out, bank(key)[:, 0:width], ACT.Ln, scale=1.0 / n,
                                              bias=con("eps")))
                nc.scalar.activation(out, out, ACT.Exp, scale=-0.5).then_inc(signal, 1)

            def apply(i):
                guess(("norm", i), rstd[:, 0, :], T, D, guess_ready)
                _, out, row, shift = NORMS[i]
                act.wait_ge(normed_ready, i + 1)
                if row is None:
                    g = sml(G_ONLY[i])
                    for k in range(KD):
                        nc.scalar.activation(out[:, k, :], out[:, k, :], ACT.Copy, scale=g[:, k:k + 1]
                                             ).then_inc(act_g, 1)
                    return
                act.wait_ge(affine_ready, AFFINE[i])
                for k in range(KD):
                    nc.scalar.activation(out[:, k, :], out[:, k, :], ACT.Identity,
                                         scale=aff[:, row, k:k + 1], bias=shift[:, k:k + 1]
                                         ).then_inc(h_ready, 1)

            act.wait_ge(small_in, 16)
            for n, name in enumerate(("cond", "cond2")):
                w = SMALL[name][1]
                ins = nc.scalar.activation(tiny[:, 500 + 16 * n:500 + 16 * n + w], sml(name), ACT.Tanh, scale=0.5)
                ins.then_inc(cond_tanh, 1)
            act.wait_ge(const_in, 16)
            norm(0)
            norm(1)
            apply(0)
            apply(1)
            act.wait_ge(lam_sum, 1)
            nc.scalar.activation(lam[:, 2:4], lam[:, 0:2], ACT.Exp).then_inc(lam_exp, 1)

            def copy(key, out, width=BANK):
                read_ready(act, key)
                src = bank(key)[:, 0:width]
                if len(out.shape) == 3:
                    src = src.rearrange("p (a b) -> p a b", b=out.shape[2])
                read_done(nc.scalar.activation(out, src, ACT.Copy), key)

            copy(("qa", 0), q_all[:, 0:2, :])
            copy(("qa", 1), q_all[:, 2:4, :])
            copy(("kva", 0), k_all[:, 0, :])
            copy(("kva", 1), v_all[:, :, 0:P])
            copy(("qb", 0), q_all[:, 4:6, :])
            copy(("qb", 1), q_all[:, 6:8, :])
            for i in range(4):
                copy(("kb", i), k_all[:, 1 + i, :])
            for i in range(4):
                copy(("vb", i), v_all[:, i, P:P + BANK])
            for i in range(5):
                src = q_all[:, i, :] if i < 4 else k_all[:, 0, :]
                dst = sq[:, 2 * (i % 2):2 * (i % 2) + 2, :].rearrange("p a b -> p (a b)")[:, 0:src.shape[-1]]
                if i == 0:
                    for key in (("qa", 0), ("qa", 1), ("kva", 0)):
                        copied(act, key)
                if i >= 2:
                    read_ready(act, ("qknorm", i - 2))
                nc.scalar.activation(dst, src, ACT.Square).then_inc(qk_square, 1)
                if i >= 1:
                    g = i - 1
                    guess(("qknorm", g), rstd[:, 0, :] if g % 2 == 0 else rstd[:, 2, :], T, HD, qk_guess)
                    act.wait_ge(q_normed, g + 1)
            guess(("qknorm", 4), rstd[:, 0:2, :].rearrange("p a b -> p (a b)"), N_KEYS, HD, qk_guess)

            def probabilities(u):
                act.wait_ge(max_ready, u + 1)
                if u >= 4:
                    act.wait_ge(pt_written, TURN_OF[u - 4] + 1)
                nc.scalar.activation(probs[:, u % 4, :], psum[:, 4 + u % 2, :], ACT.Exp,
                                     bias=soft[:, u, 0:1], scale=ATT_SCALE, accum_out=soft[:, u, 1:2]
                                     ).then_inc(probs_ready, 1)

            def copy_turned(n):
                act.wait_ge(pt_written, n + 1)
                if n < 16:
                    pair, b = n // 2, n % 2
                    slot = pair % 2
                    if n >= 4 and b == 0 and slot == 0:
                        read_ready(act, ("oa", pair // 2 - 1))
                else:
                    pair, b = n // 2, n % 2
                    slot = pair % 2
                    if b == 0:
                        if pair - 8 >= 2:
                            read_ready(act, ("ob", pair - 8 - 2))
                        else:
                            read_ready(act, ("oa", 3))
                dst = p_t[:, slot, :].rearrange("p (k t) -> p k t", t=T)[:, :, b * P:b * P + P]
                src = psum[:, 6 + n % 2, :].rearrange("p (k t) -> p k t", t=P)
                nc.scalar.activation(dst, src, ACT.Copy).then_inc(pt_ready, 1)

            probabilities(0)
            probabilities(1)
            for n in range(24):
                copy_turned(n)
                for u in NEW_MAPS[n]:
                    probabilities(u)
                if n < 16 and n % 4 == 3:
                    copy(("oa", n // 4), mix[:, n // 4, :], T)
                if n >= 16 and n % 2:
                    copy(("ob", (n - 16) // 2), mix[:, 4 + (n - 16) // 2, :], T)
            for i in range(2):
                for j in range(2):
                    copied(act, ("ob", 2 * i + j))
                nc.scalar.activation(sq[:, 2 * i:2 * i + 2, :], mix[:, 4 + 2 * i:6 + 2 * i, :], ACT.Square
                                     ).then_inc(qk_square, 1)
            for i in range(2):
                guess(("onorm", i), rstd[:, 2 * i:2 * i + 2, :].rearrange("p a b -> p (a b)") if i == 0
                      else sq[:, 6:8, :].rearrange("p a b -> p (a b)"), BANK, P, qk_guess)

            norm(2)
            apply(2)
            for c in range(4):
                copy(("htok", c), h_tok[:, c // 2, BANK * (c % 2):BANK * (c % 2) + BANK])
            act.wait_ge(top_ready, 1)
            nc.scalar.activation(top_e[:, :, 0:TOP_K], top_e[:, :, 0:TOP_K], ACT.Exp).then_inc(top_exp, 1)
            read_ready(act, ("gates", 0))
            read_done(nc.scalar.activation(gates_t[0:E, :], bank(("gates", 0))[0:E, 0:T], ACT.Copy), ("gates", 0))

            def gathered(s, t0):
                for c in range(4):
                    act.wait_ge(s.t_ready, t0 + c + 1)
                    nc.scalar.activation(x_e[:, c // 2, 4 * (c % 2):4 * (c % 2) + 4, :],
                                         psum[:, 4 + c % 2, 0:4 * CAP].rearrange("p (a b) -> p a b", b=CAP),
                                         ACT.Copy).then_inc(s.t_free[c % 2], 1)

            def experts(s, i):
                for e in range(2):
                    act.wait_ge(s.glu_ready, i * 2 + (e + 1))
                    nc.scalar.activation(tanh_e[:, e], glu[:, e], ACT.Tanh, scale=ALPHA / 2
                                         ).then_inc(s.tanh_ready, 1)

                def outputs(e):
                    for c in range(2):
                        j = 8 + 2 * e + c
                        act.wait_ge(s.g_ready, i * 12 + (j + 1))
                        nc.scalar.activation(y_e[:, e, 4 * c:4 * c + 4, :],
                                             psum[:, j % 4, 0:4 * CAP].rearrange("p (a b) -> p a b", b=CAP),
                                             ACT.Copy).then_inc(s.g_free[j % 4], 1)

                outputs(0)
                for e in range(2):
                    act.wait_ge(s.t_ready, i * 10 + (4 + e + 1))
                    nc.scalar.activation(g_slot[0:CAP, e, :], psum[0:CAP, 4 + e, 0:T], ACT.Copy
                                         ).then_inc(s.t_free[e], 1)
                outputs(1)
                for c in range(4):
                    act.wait_ge(s.t_ready, i * 10 + (6 + c + 1))
                    nc.scalar.activation(y_slot[0:CAP, c // 2, BANK * (c % 2):BANK * (c % 2) + BANK],
                                         psum[0:CAP, 4 + c % 2, :], ACT.Copy).then_inc(s.t_free[c % 2], 1)
                gathered(s, i * 10 + 10)

            gathered(moe, 0)
            with act.Fori(0, PAIRS) as i:
                experts(moe, i)
            act.wait_ge(over_ready, 1)
            flag = act.value_load(over[0:1, 0:1], min_val=0, max_val=1)
            with act.If(flag > 0):
                gathered(again, 0)
                with act.Fori(0, PAIRS * (PASSES - 1)) as i:
                    experts(again, i)
                act.wait_ge(again.done, 1)
            for c in range(2):
                act.wait_ge(moe.t_free[c], 5 * PAIRS + 2)

            norm(3)
            apply(3)
            norm(4)
            apply(4)
            act.wait_ge(angle_ready, 1)
            for n, a in enumerate((cos2, sin2)):
                nc.scalar.activation(a, rot[:, 0, n * T:n * T + T], ACT.Sin).then_inc(sin_ready, 1)
            for s in range(4):
                for t in range(TT):
                    copy((("rv", s), t), rv[:, t, BANK * s:BANK * s + BANK])
            for s in range(4):
                for c in range(2):
                    key = (("rg", s), c)
                    read_ready(act, key)
                    n = 2 * s + c
                    if n == 0:
                        act.wait_ge(ret_qk, 8)
                    if n >= 2:
                        act.wait_ge(ret_gate, n - 1)
                    nc.scalar.activation(rot[:, n % 2, :], bank(key), ACT.Tanh, scale=0.5).then_inc(ret_tanh, 1)
            for h in range(RET_HEADS):
                for c in range(2):
                    if c == 0 and h:
                        act.wait_ge(ret_done, h)
                    copy(("ro", h, c), ro[:, 2 * c:2 * c + 2, :])
                act.wait_ge(ret_o, h + 1)
                if h:
                    read_ready(act, ("rvar", h - 1))
                nc.scalar.activation(sq[:, 0:4, :], ro[:], ACT.Square).then_inc(ret_sq, 1)
                guess(("rvar", h), rstd[:, 0, :], T, 512, ret_guess)

            def ffn(layer):
                norm(5 + 2 * layer)
                apply(5 + 2 * layer)
                w = sml("conv_w").rearrange("p (l c k) -> p l c k", l=2, c=3)[:, layer]
                b = sml("conv_b").rearrange("p (l k) -> p l k", l=2)[:, layer]
                for s in range(11):
                    for c in range(2):
                        n = 2 * s + c
                        key = (("up", layer, s), c)
                        if n < 11:
                            copy(key, val[:, 2 * n:2 * n + 2, :])
                            continue
                        m = n - 11
                        read_ready(act, key)
                        if m >= 2:
                            act.wait_ge(act_ready, 11 * layer + m - 1)
                        for a in range(2):
                            k = 2 * m + a
                            ins = nc.scalar.activation(conv[:, m % 2, a * T:a * T + T], half(key, a), ACT.Identity,
                                                       scale=w[:, 2, k:k + 1], bias=b[:, k:k + 1])
                            ins.then_inc(conv_start, 1)
                        if m >= 1:
                            tanh(layer, m - 1)
                tanh(layer, 10)

            def tanh(layer, m):
                act.wait_ge(conv_ready, 11 * layer + m + 1)
                nc.scalar.activation(conv_t[:, m % 2, :], conv[:, m % 2, :], ACT.Tanh, scale=0.5
                                     ).then_inc(conv_tanh, 1)

            ffn(0)
            norm(6)
            apply(6)
            act.wait_ge(s5_dt, 1)
            nc.scalar.activation(s5[:, 0, :], sml("log_dt"), ACT.Exp).then_inc(s5_exp, 1)
            act.wait_ge(s5_dt, 2)
            nc.scalar.activation(s5[:, 1, :], s5[:, 1, :], ACT.Exp).then_inc(s5_exp, 1)
            act.wait_ge(s5_angle, 1)
            for n in range(2):
                nc.scalar.activation(s5[:, 4 + n, :], s5[:, 2 + n, :], ACT.Sin).then_inc(s5_exp, 1)
            for s in range(2):
                for c in range(2):
                    copy((("s5in", s), c), u5[:, 4 * s + 2 * c:4 * s + 2 * c + 2, :])
            for j in range(8):
                act.wait_ge(s5_gelu_in, j + 1)
                nc.scalar.activation(gl[:, j % 8, :], gl[:, j % 8, :], ACT.Tanh, scale=GELU_C
                                     ).then_inc(s5_gelu_t, 1)
            for s in range(2):
                for c in range(2):
                    if s == 0 and c == 0:
                        act.wait_ge(s5_y, 8)
                    copy((("glu", s), c), gl[:, 4 * s + 2 * c:4 * s + 2 * c + 2, :])
            for s in range(2, 4):
                for c in range(2):
                    n = 2 * (s - 2) + c
                    key = (("glu", s), c)
                    read_ready(act, key)
                    nc.scalar.activation(u5[:, 2 * n:2 * n + 2, :], two(bank(key)), ACT.Tanh, scale=0.5)\
                        .then_inc(glu_tanh, 1)
            ffn(1)
            norm(8)
            apply(8)

        @block.vector
        def _(dve):
            own = Steps(dve, dve_step)
            V = nc.vector

            def refine(key, y, v, t, width, n, guess_sem, count):
                dve.wait_ge(guess_sem, count)
                own.link(V.tensor_scalar(v, bank(key)[:, 0:width], -0.5 / n, -0.5 * EPS, ALU.mult, ALU.add))
                own.link(V.tensor_tensor(t, y, y, ALU.mult))
                own.link(V.tensor_tensor(t, t, v, ALU.mult))
                ins = V.scalar_tensor_tensor(out=y, in0=t, scalar=1.5, in1=y, op0=ALU.add, op1=ALU.mult)
                return ins

            def norm(i):
                src, out, row, _ = NORMS[i]
                key = ("norm", i)
                read_ready(dve, key)
                read_done(refine(key, rstd[:, 0, :], rstd[:, 1, :], rstd[:, 2, :], T, D, guess_ready, i + 1), key)
                copied(dve, key)
                V.tensor_tensor(out[:], src[:], over_tiles(rstd[:, 0, :], KD), ALU.mult
                                ).then_inc(normed_ready, 1)

            for n, name in enumerate(("cond", "cond2")):
                w = SMALL[name][1]
                dve.wait_ge(cond_tanh, n + 1)
                t = tiny[:, 500 + 16 * n:500 + 16 * n + w]
                own.link(V.scalar_tensor_tensor(out=t, in0=t, scalar=1.0, in1=sml(name), op0=ALU.add, op1=ALU.mult))
                V.tensor_scalar(sml(name), t, 0.5, None, ALU.mult).then_inc(cond_ready, 1)
            dl = sml("dlam").rearrange("p (a b) -> p a b", b=HD)
            for j in range(2):
                own.link(V.tensor_tensor(lam_prod[:, j, :], dl[:, 2 * j, :], dl[:, 2 * j + 1, :], ALU.mult))
            V.tensor_reduce(lam[:, 0:2], lam_prod, AX_X, ALU.add).then_inc(lam_sum, 1)

            def modulation(s):
                key = (("ada", s), 0)
                read_ready(dve, key)
                b = sml("b_ada")[:, 4 * s:4 * s + 4].unsqueeze(2).to_broadcast([P, 4, 2])
                read_done(V.tensor_tensor(mod[:, 4 * s:4 * s + 4, :],
                                          bank(key)[:, 0:8].rearrange("p (a b) -> p a b", b=2), b, ALU.add), key)

            def modulation2(layer, s):
                key = (("ada2", layer, s), 0)
                read_ready(dve, key)
                read_done(V.tensor_tensor(mod2[:, layer, 4 * s:4 * s + 4], bank(key)[:, 0:4],
                                          sml("b_ada2")[:, 48 * layer + 4 * s:48 * layer + 4 * s + 4], ALU.add), key)

            for s in range(4):
                modulation(s)
            for s in range(4):
                copied(dve, (("ada", s), 0))
            own.mark(V.scalar_tensor_tensor(out=aff[:, 0, :], in0=mod[:, 8:16, 1], scalar=1.0, in1=sml("g_attn"),
                                            op0=ALU.add, op1=ALU.mult))
            V.scalar_tensor_tensor(out=aff[:, 1, :], in0=mod[:, 8:16, 0], scalar=1.0, in1=sml("g_attn"),
                                   op0=ALU.add, op1=ALU.mult).then_inc(affine_ready, 1)
            dve.wait_ge(const_in, 16)
            norm(0)
            norm(1)
            dve.wait_ge(lam_exp, 1)
            own.link(V.tensor_tensor(lam[:, 4:5], lam[:, 3:4], lam[:, 2:3], ALU.subtract))
            own.link(V.tensor_scalar(lam[:, 5:6], lam[:, 4:5], -LAMBDA_INIT, None, ALU.add))

            for i in range(5):
                key = ("qknorm", i)
                y = rstd[:, 0, :] if i % 2 == 0 else rstd[:, 2, :]
                width = T if i < 4 else N_KEYS
                if i == 4:
                    y = rstd[:, 0:2, :].rearrange("p a b -> p (a b)")
                read_ready(dve, key)
                v = rope_t[:, 0, 0:width]
                t = rope_t[:, 1, 0:width]
                ins = refine(key, y, v, t, width, HD, qk_guess, i + 1)
                read_done(ins, key)
                copied(dve, key)
                src = q_all[:, i, :] if i < 4 else k_all[:, 0, :]
                ins = V.scalar_tensor_tensor(out=src, in0=src, scalar=sml("g_q" if i < 4 else "g_k"), in1=y,
                                             op0=ALU.mult, op1=ALU.mult)
                if i < 4:
                    ins.then_inc(q_normed, 1)
                else:
                    own.link(ins)
            dve.wait_ge(q_normed, 4)
            for j in range(2):
                copied(dve, ("qb", j))
            for j in range(4):
                copied(dve, ("kb", j))
                copied(dve, ("vb", j))
            V.memset(tiny[:, 499:500], 0.0).then_inc(q_ready, 1)
            for i in range(9):
                key = ("rope", i)
                read_ready(dve, key)
                if i < 4:
                    dst, ps = q_all[:, 2 * i:2 * i + 2, :], two(bank(key))
                    n = 2
                else:
                    dst, ps = k_all[:, i - 4:i - 3, T:N_KEYS], bank(key)[:, 0:T].unsqueeze(1)
                    n = 1
                t = rope_t[:, 0, 0:n * T].rearrange("p (a b) -> p a b", b=T)
                own.mark(V.tensor_tensor(dst, dst, over_tiles(con("rope_cos"), n), ALU.mult))
                ins = V.tensor_tensor(t, ps, over_tiles(con("rope_sin"), n), ALU.mult)
                read_done(ins, key)
                dve.wait_ge(dve_step, own.n)
                copied(dve, key)
                V.tensor_tensor(dst, dst, t, ALU.add).then_inc(q_ready, 1)
                dve.wait_ge(q_ready, 2 + i)

            def maximum(u):
                dve.wait_ge(scores_ready, u + 1)
                own.link(V.tensor_reduce(soft[:, u, 2:3], psum[:, 4 + u % 2, :], AX_X, ALU.max))
                V.tensor_scalar(soft[:, u, 0:1], soft[:, u, 2:3], -ATT_SCALE, None, ALU.mult).then_inc(max_ready, 1)

            def factor(u):
                dve.wait_ge(probs_ready, u + 1)
                if u >= 4:
                    dve.wait_ge(pt_written, TURN_OF[u - 4] + 1)
                own.link(V.reciprocal(soft[:, u, 3:4], soft[:, u, 1:2]))
                if u >= 16 and u % 2:
                    own.link(V.tensor_tensor(soft[:, u, 3:4], soft[:, u, 3:4], lam[:, 5:6], ALU.mult))
                V.tensor_scalar(diag[:, u % 4, :], con("ident"), soft[:, u, 3:4], None, ALU.mult
                                ).then_inc(diag_ready, 1)

            ada = [("ada", s) for s in range(4, 12)] + [("ada2", 0, s) for s in range(12)]

            def next_modulation():
                key = ada.pop(0)
                modulation(key[1]) if key[0] == "ada" else modulation2(0, key[2])

            maximum(0)
            maximum(1)
            for j in range(12):
                maps = [[2 * j], [2 * j + 1]] if j < 8 else [[4 * j - 16, 4 * j - 15], [4 * j - 14, 4 * j - 13]]
                for turned in maps:
                    for u in turned:
                        factor(u)
                    for u in turned:
                        if u + 2 < 32:
                            maximum(u + 2)
                for _ in range(2 if j < 8 else 1):
                    next_modulation()
            copied(dve, (("ada", 11), 0))
            copied(dve, (("ada", 10), 0))
            for s in range(8):
                copied(dve, (("ada", 4 + s), 0))
            V.scalar_tensor_tensor(out=aff[:, 2, :], in0=mod[:, 32:40, 0], scalar=1.0, in1=sml("g_ffn"),
                                   op0=ALU.add, op1=ALU.mult).then_inc(affine_ready, 1)
            for s in range(12):
                copied(dve, (("ada2", 0, s), 0))
            own.mark(V.tensor_scalar(aff[:, 3, :], mod2[:, 0, 8:16], 1.0, None, ALU.add))
            V.tensor_scalar(aff[:, 4, :], mod2[:, 0, 32:40], 1.0, None, ALU.add).then_inc(affine_ready, 1)
            for i in range(2):
                key = ("onorm", i)
                read_ready(dve, key)
                y = (rstd[:, 0:2, :] if i == 0 else sq[:, 6:8, :]).rearrange("p a b -> p (a b)")
                ins = refine(key, y, rope_t[:, 0, :], rope_t[:, 1, :], BANK, P, qk_guess, 6 + i)
                read_done(ins, key)
                copied(dve, key)
                o = mix[:, 4 + 2 * i:6 + 2 * i, :]
                own.link(V.tensor_tensor(o, o, two(y), ALU.mult))
                ins = V.tensor_scalar(o, o, sml("g_sub"), 1.0 - LAMBDA_INIT, ALU.mult, ALU.mult)
                if i == 0:
                    own.link(ins)
                else:
                    ins.then_inc(mix_ready, 1)
                    dve.wait_ge(mix_ready, 1)

            def add_to_x(key, m0, gate_col, n=2, last=None):
                read_ready(dve, key)
                for m in range(n):
                    ins = V.scalar_tensor_tensor(out=x[:, m0 + m, :], in0=half(key, m),
                                                 scalar=gate_col[:, m0 + m:m0 + m + 1], in1=x[:, m0 + m, :],
                                                 op0=ALU.mult, op1=ALU.add)
                    if m < n - 1:
                        own.mark(ins)
                read_done(ins, key)

            def x_complete(keys):
                for key in keys:
                    copied(dve, key)
                V.memset(tiny[:, 499:500], 0.0).then_inc(x_ready, 1)

            keys = [("wo0", 0), ("wo0", 1), ("wo1", 0), ("wo1", 1)]
            for n, key in enumerate(keys):
                add_to_x(key, 2 * n, mod[:, 16:24, 0])
            dve.wait_ge(dve_step, own.n)
            x_complete(keys)
            norm(2)

            key = ("router", 0)
            read_ready(dve, key)
            read_done(V.tensor_tensor(logits, bank(key)[:, 0:TT * E].rearrange("p (a b) -> p a b", b=E),
                                      over_tiles(sml("b_router"), TT), ALU.add), key)
            copied(dve, key)
            for t in range(TT):
                own.link(V.max(top[:, t, :], logits[:, t, :]))
                own.link(V.max_index(top_i[:, t, :].bitcast(U32), top[:, t, :], logits[:, t, :]))
            own.link(V.tensor_copy(top_f, top_i.bitcast(U32)))
            V.tensor_tensor(top_e[:, :, 0:TOP_K], top[:, :, 0:TOP_K],
                            top[:, :, 0:1].to_broadcast([P, TT, TOP_K]), ALU.subtract).then_inc(top_ready, 1)
            dve.wait_ge(top_exp, 1)
            own.link(V.tensor_reduce(gate_sum[:, 0:2], top_e[:, :, 0:TOP_K], AX_X, ALU.add))
            own.link(V.reciprocal(gate_sum[:, 2:4], gate_sum[:, 0:2]))
            for t in range(TT):
                own.link(V.tensor_scalar(top_e[:, t, 0:TOP_K], top_e[:, t, 0:TOP_K], gate_sum[:, 2 + t:3 + t],
                                         None, ALU.mult))
            for t in range(TT):
                for r in range(TOP_K):
                    dst = mask[:, t, :] if r == 0 else onehot[:, 0, :]
                    dst_g = gate[:, t, :] if r == 0 else onehot[:, 1, :]
                    own.mark(V.tensor_scalar(dst, con("experts"), top_f[:, t, r:r + 1], None, ALU.is_equal))
                    own.link(V.tensor_scalar(dst_g, con("experts"), top_f[:, t, r:r + 1],
                                             top_e[:, t, r:r + 1], ALU.is_equal, ALU.mult))
                    if r:
                        own.mark(V.tensor_tensor(mask[:, t, :], mask[:, t, :], onehot[:, 0, :], ALU.add))
                        ins = V.tensor_tensor(gate[:, t, :], gate[:, t, :], onehot[:, 1, :], ALU.add)
                        if t == TT - 1 and r == TOP_K - 1:
                            ins.then_inc(mask_ready, 1)
                        else:
                            own.link(ins)
            key = ("pos", 0)
            read_ready(dve, key)
            dve.wait_ge(mask_ready, 1)
            b = bank(key)
            own.mark(V.tensor_copy(count, b[:, 2 * E:3 * E]))
            own.link(V.scalar_tensor_tensor(out=slot_of, in0=b[:, 0:2 * E].rearrange("p (a b) -> p a b", b=E),
                                            scalar=1.0, in1=mask, op0=ALU.add, op1=ALU.mult))
            own.link(V.tensor_reduce(max_count, count, AX_X, ALU.max))
            own.mark(V.tensor_scalar(over, max_count, float(CAP), None, ALU.is_gt))
            ins = V.tensor_scalar(slot_of, slot_of, -1.0, None, ALU.add)
            read_done(ins, key)
            copied(dve, key)
            dve.wait_ge(dve_step, own.n)
            V.memset(tiny[:, 498:499], 0.0).then_inc(over_ready, 1)
            for c in range(4):
                key = ("bout", c)
                read_ready(dve, key)
                read_done(V.tensor_copy(y_moe[:, 2 * c:2 * c + 2, :], two(bank(key))), key)
            for c in range(4):
                copied(dve, ("bout", c))

            def select(pair, first, last):
                slots = con("slots")[:, first] if not isinstance(first, int) else con("slots")[:, first:first + CAP]
                for e in range(2):
                    for t in range(TT):
                        ins = V.tensor_scalar(sel[:, e, t, :], slots, slot_of[:, t, bass.ds(pair + e, 1)],
                                              None, ALU.is_equal)
                        if e == 1 and t == TT - 1:
                            ins.then_inc(last, 1)
                return ins

            def select_gated(pair, first, step):
                slots = con("slots")[:, first] if not isinstance(first, int) else con("slots")[:, first:first + CAP]
                for e in range(2):
                    for t in range(TT):
                        step.mark(V.tensor_scalar(gsel[:, e, t, :], slots, slot_of[:, t, bass.ds(pair + e, 1)],
                                                  gate[:, t, bass.ds(pair + e, 1)], ALU.is_equal, ALU.mult))

            def experts(s, i, pair, next_pair, first, next_first):
                per = 10
                step = Steps(dve, s.step, i * per)
                bias = sml("b_in").rearrange("p (e k) -> p e k", k=16)
                for j in range(8):
                    e, c = j // 4, j % 4
                    dve.wait_ge(s.g_ready, i * 12 + (j + 1))
                    if j == 0:
                        select_gated(pair, first, step)
                        select(next_pair, next_first, s.sel_ready)
                    dst = (glu if c < 2 else lin)[:, e, 4 * (c % 2):4 * (c % 2) + 4, :]
                    bb = bias[:, bass.ds(pair + e, 1), 4 * c:4 * c + 4].rearrange("p a k -> p (a k)")
                    V.tensor_tensor(dst, psum[:, j % 4, 0:4 * CAP].rearrange("p (a b) -> p a b", b=CAP),
                                    bb.unsqueeze(2).to_broadcast([P, 4, CAP]), ALU.add
                                    ).then_inc(s.g_free[j % 4], 1)
                    if c == 1:
                        for b in (0, 1):
                            dve.wait_ge(s.g_free[b], i * 3 + (e + 1))
                        V.tensor_scalar(glu[:, e], glu[:, e], LIMIT, None, ALU.min).then_inc(s.glu_ready, 1)
                    if c == 3:
                        for b in (2, 3):
                            dve.wait_ge(s.g_free[b], i * 3 + (e + 1))
                        step.link(V.tensor_scalar(lin[:, e], lin[:, e], LIMIT, -LIMIT, ALU.min, ALU.max))
                        step.link(V.tensor_scalar(lin[:, e], lin[:, e], 0.5, 0.5, ALU.mult, ALU.add))
                        dve.wait_ge(s.tanh_ready, i * 2 + (e + 1))
                        step.link(V.scalar_tensor_tensor(out=flat(tanh_e[:, e]), in0=flat(tanh_e[:, e]), scalar=1.0,
                                                         in1=flat(glu[:, e]), op0=ALU.add, op1=ALU.mult))
                        V.tensor_tensor(lin[:, e], lin[:, e], tanh_e[:, e], ALU.mult).then_inc(s.act_ready, 1)
                for c in range(4):
                    dve.wait_ge(s.s_ready, i * 4 + (c + 1))
                    V.tensor_tensor(y_moe[:, 2 * c:2 * c + 2, :], y_moe[:, 2 * c:2 * c + 2, :],
                                    two(psum[:, 6 + c % 2, :]), ALU.add).then_inc(s.s_free[c % 2], 1)
                for c in range(2):
                    dve.wait_ge(s.s_free[c], i * 2 + 2)
                assert step.n == per

            select(0, 0, moe.sel_ready)
            with dve.Fori(0, PAIRS) as i:
                experts(moe, i, i * 2, ((i + 1) % PAIRS) * 2, 0, 0)
            dve.wait_ge(over_ready, 1)
            flag = dve.value_load(over[0:1, 0:1], min_val=0, max_val=1)
            with dve.If(flag > 0):
                select(0, CAP, again.sel_ready)
                with dve.Fori(0, PAIRS * (PASSES - 1)) as i:
                    n = (i + 1) % (PAIRS * (PASSES - 1))
                    experts(again, i, (i % PAIRS) * 2, (n % PAIRS) * 2,
                            bass.ds((i // PAIRS + 1) * CAP, CAP), bass.ds((n // PAIRS + 1) * CAP, CAP))
                V.memset(tiny[:, 498:499], 0.0).then_inc(again.done, 1)

            for k in range(KD):
                own.mark(V.scalar_tensor_tensor(out=x[:, k, :], in0=y_moe[:, k, :], scalar=mod[:, 40 + k, 0:1],
                                                in1=x[:, k, :], op0=ALU.mult, op1=ALU.add))
            dve.wait_ge(dve_step, own.n)
            V.memset(tiny[:, 499:500], 0.0).then_inc(x_ready, 1)

            norm(3)
            dve.wait_ge(act_g, KD)
            V.memset(tiny[:, 499:500], 0.0).then_inc(x_ready, 1)
            norm(4)

            def reduce_angle(a, n, sin_out, cos_out):
                own.link(V.tensor_scalar(n, a, float(1 / TWO_PI), ROUND, ALU.mult, ALU.add))
                own.link(V.tensor_scalar(n, n, ROUND, None, ALU.subtract))
                for part in (PI2_A, PI2_B, PI2_C):
                    own.link(V.scalar_tensor_tensor(out=a, in0=n, scalar=-part, in1=a, op0=ALU.mult, op1=ALU.add))
                own.link(V.tensor_scalar(sin_out, a, PI_IN, -PI_IN, ALU.min, ALU.max))
                own.link(V.tensor_scalar(n, sin_out, float(np.pi / 2), -TWO_PI, ALU.is_gt, ALU.mult))
                own.link(V.scalar_tensor_tensor(out=n, in0=n, scalar=float(np.pi / 2), in1=sin_out,
                                                op0=ALU.add, op1=ALU.add))
                return V.tensor_scalar(cos_out, n, PI_IN, -PI_IN, ALU.min, ALU.max)

            dve.wait_ge(pos_ready, 1)
            own.link(V.tensor_scalar(rs[:, 0:T], rs[:, 0:T], con("inv_freq"), None, ALU.mult))
            reduce_angle(rs[:, 0:T], rs[:, T:2 * T], rot[:, 0, T:2 * T], rot[:, 0, 0:T]).then_inc(angle_ready, 1)
            dve.wait_ge(sin_ready, 2)
            for n, (name, dst) in enumerate((("rq", rq), ("rk", rk))):
                for h in range(RET_HEADS):
                    key = ((name, h // 2), h % 2)
                    read_ready(dve, key)
                    a, b = two(rot[:, 0, :]), two(rot[:, 1, :])
                    own.mark(V.tensor_tensor(a, two(bank(key)), over_tiles(cos2, 2), ALU.mult))
                    read_done(V.tensor_tensor(b, two(bank(key)), over_tiles(sin2, 2), ALU.mult), key)
                    dve.wait_ge(dve_step, own.n)
                    copied(dve, key)
                    own.mark(V.tensor_tensor(dst[:, 2 * h, :], a[:, 0, :], b[:, 1, :], ALU.subtract))
                    V.tensor_tensor(dst[:, 2 * h + 1, :], a[:, 1, :], b[:, 0, :], ALU.add).then_inc(ret_qk, 1)
                    dve.wait_ge(dve_step, own.n)
                    dve.wait_ge(ret_qk, 4 * n + h + 1)
            for s in range(4):
                for c in range(2):
                    n = 2 * s + c
                    key = (("rg", s), c)
                    dve.wait_ge(ret_tanh, n + 1)
                    ins = V.scalar_tensor_tensor(out=rg[:, 2 * n:2 * n + 2, :].rearrange("p a b -> p (a b)"),
                                                 in0=rot[:, n % 2, :], scalar=1.0, in1=bank(key),
                                                 op0=ALU.add, op1=ALU.mult)
                    read_done(ins, key)
                    copied(dve, key)
                    V.memset(tiny[:, 499:500], 0.0).then_inc(ret_gate, 1)
            for h in range(RET_HEADS):
                key = ("rs", h)
                read_ready(dve, key)
                mask_h = con("decay")[:, 2 * T * h:2 * T * h + 2 * T]
                read_done(V.tensor_tensor(rs, bank(key), mask_h, ALU.mult), key)
                copied(dve, key)
                V.memset(tiny[:, 499:500], 0.0).then_inc(ret_s, 1)
                key = ("rmean", h)
                read_ready(dve, key)
                own.link(V.tensor_scalar(rstd[:, 3, :], half(key, 0), 1.0 / 512, None, ALU.mult))
                ins = V.tensor_tensor(ro, ro, over_tiles(rstd[:, 3, :], 4), ALU.subtract)
                read_done(ins, key)
                copied(dve, key)
                V.memset(tiny[:, 499:500], 0.0).then_inc(ret_o, 1)
                key = ("rvar", h)
                read_ready(dve, key)
                read_done(refine(key, rstd[:, 0, :], rstd[:, 1, :], rstd[:, 2, :], T, 512, ret_guess, h + 1), key)
                copied(dve, key)
                own.link(V.tensor_tensor(ro, ro, over_tiles(rstd[:, 0, :], 4), ALU.mult))
                g = rg[:, 4 * h:4 * h + 4, :]
                V.scalar_tensor_tensor(out=flat(g), in0=flat(ro), scalar=0.5, in1=flat(g), op0=ALU.mult,
                                       op1=ALU.mult).then_inc(ret_done, 1)
                dve.wait_ge(ret_done, h + 1)
            keys = [(("rout", s), 0) for s in range(4)]
            for s, key in enumerate(keys):
                add_to_x(key, 2 * s, mod2[:, 0, 16:24])
            dve.wait_ge(dve_step, own.n)
            x_complete(keys)

            def ffn(layer):
                norm(5 + 2 * layer)
                w = sml("conv_w").rearrange("p (l c k) -> p l c k", l=2, c=3)[:, layer]
                for m in range(11):
                    n = m + 11
                    key = (("up", layer, n // 2), n % 2)
                    dve.wait_ge(conv_start, 22 * layer + 2 * m + 2)
                    ps = two(bank(key))
                    cv = two(conv[:, m % 2, :])
                    for lag in (1, 2):
                        for a in range(2):
                            k = 2 * m + a
                            ins = V.scalar_tensor_tensor(out=cv[:, a, lag:T], in0=ps[:, a, 0:T - lag],
                                                         scalar=w[:, 2 - lag, k:k + 1], in1=cv[:, a, lag:T],
                                                         op0=ALU.mult, op1=ALU.add)
                            if lag == 2 and a == 1:
                                read_done(ins, key)
                            else:
                                own.mark(ins)
                        if lag == 1:
                            dve.wait_ge(dve_step, own.n)
                    dve.wait_ge(dve_step, own.n)
                    copied(dve, key)
                    V.memset(tiny[:, 499:500], 0.0).then_inc(conv_ready, 1)
                    if m >= 1:
                        finish(layer, m - 1)
                finish(layer, 10)
                keys = [(("down", layer, s), 0) for s in range(8)]
                for s, key in enumerate(keys):
                    add_to_x(key, s, mod2[:, layer, 40:48], n=1)
                x_complete(keys)

            def finish(layer, m):
                dve.wait_ge(conv_tanh, 11 * layer + m + 1)
                t, cv = conv_t[:, m % 2, :], conv[:, m % 2, :]
                n = m
                own.link(V.scalar_tensor_tensor(out=t, in0=t, scalar=1.0, in1=cv, op0=ALU.add, op1=ALU.mult))
                copied(dve, (("up", layer, n // 2), n % 2))
                v = flat(val[:, 2 * m:2 * m + 2, :])
                V.scalar_tensor_tensor(out=v, in0=t, scalar=0.5, in1=v, op0=ALU.mult, op1=ALU.mult
                                       ).then_inc(act_ready, 1)
                dve.wait_ge(act_ready, 11 * layer + m + 1)

            ffn(0)
            for s in range(12):
                modulation2(1, s)
            for s in range(12):
                copied(dve, (("ada2", 1, s), 0))
            own.mark(V.tensor_scalar(aff[:, 5, :], mod2[:, 1, 8:16], 1.0, None, ALU.add))
            V.tensor_scalar(aff[:, 6, :], mod2[:, 1, 32:40], 1.0, None, ALU.add).then_inc(affine_ready, 1)
            norm(6)

            row = lambda n: s5[:, n, :]
            re, im = sml("lam_re"), sml("lam_im")
            V.memset(tiny[:, 639:640], 0.0).then_inc(s5_dt, 1)
            dve.wait_ge(s5_exp, 1)
            own.link(V.tensor_tensor(row(10), im, row(0), ALU.mult))
            V.tensor_tensor(row(1), re, row(0), ALU.mult).then_inc(s5_dt, 1)
            reduce_angle(row(10), row(11), row(3), row(2)).then_inc(s5_angle, 1)
            dve.wait_ge(s5_exp, 4)
            own.mark(V.tensor_tensor(row(6), row(1), row(4), ALU.mult))
            own.link(V.tensor_tensor(row(7), row(1), row(5), ALU.mult))
            own.mark(V.tensor_scalar(row(10), row(6), -1.0, None, ALU.add))
            own.mark(V.tensor_tensor(row(11), re, re, ALU.mult))
            own.link(V.tensor_tensor(row(12), im, im, ALU.mult))
            own.link(V.tensor_tensor(row(11), row(11), row(12), ALU.add))
            own.link(V.reciprocal(row(11), row(11)))
            own.mark(V.tensor_tensor(row(12), row(10), re, ALU.mult))
            own.link(V.tensor_tensor(row(13), row(7), im, ALU.mult))
            own.link(V.tensor_tensor(row(12), row(12), row(13), ALU.add))
            own.link(V.tensor_tensor(row(8), row(12), row(11), ALU.mult))
            own.mark(V.tensor_tensor(row(12), row(7), re, ALU.mult))
            own.link(V.tensor_tensor(row(13), row(10), im, ALU.mult))
            own.link(V.tensor_tensor(row(12), row(12), row(13), ALU.subtract))
            own.link(V.tensor_tensor(row(9), row(12), row(11), ALU.mult))
            V.memset(tiny[:, 639:640], 0.0).then_inc(s5_ab, 1)
            dve.wait_ge(s5_in, 64)
            fr = row(8).unsqueeze(2).to_broadcast([P, S5_PAIRS, GROUP])
            fi = row(9).unsqueeze(2).to_broadcast([P, S5_PAIRS, GROUP])
            c_t = gl[:, 4:6, :].rearrange("p a b -> p (a b)").rearrange("p (a b) -> p a b", b=GROUP)
            own.mark(V.tensor_tensor(c_f[:, 0], c_in5[:, 0], fr, ALU.mult))
            own.link(V.tensor_tensor(c_t, c_in5[:, 1], fi, ALU.mult))
            own.link(V.tensor_tensor(c_f[:, 0], c_f[:, 0], c_t, ALU.subtract))
            own.mark(V.tensor_tensor(c_f[:, 1], c_in5[:, 0], fi, ALU.mult))
            own.link(V.tensor_tensor(c_t, c_in5[:, 1], fr, ALU.mult))
            own.link(V.scalar_tensor_tensor(out=flat(c_f[:, 1]), in0=flat(c_f[:, 1]), scalar=-1.0, in1=flat(c_t),
                                            op0=ALU.mult, op1=ALU.subtract))
            for c in range(2):
                for g in range(2):
                    own.mark(V.tensor_scalar(c_bd[:, c, :, GROUP * g:GROUP * g + GROUP], c_f[:, c],
                                             con("state_mask")[:, g:g + 1], None, ALU.mult))
                    own.mark(V.tensor_scalar(b_bd[:, c, :, STATE * g:STATE * g + STATE], b_in5[:, c],
                                             con("in_mask")[:, g:g + 1], None, ALU.mult))
            dve.wait_ge(dve_step, own.n)
            V.memset(tiny[:, 639:640], 0.0).then_inc(s5_bc, 1)
            for j in range(8):
                cos_t, sin_t = tab[j % 2]
                for q in range(4):
                    u = 4 * j + q
                    key = ("bu", u)
                    read_ready(dve, key)
                    if q == 0:
                        dve.wait_ge(s5_table, j + 1)
                    ct, st = over_tiles(cos_t[:, q, :], 2), over_tiles(sin_t[:, q, :], 2)
                    own.mark(V.tensor_tensor(z1, two(bank(key)), ct, ALU.mult))
                    read_done(V.tensor_tensor(z2, two(bank(key)), st, ALU.mult), key)
                    dve.wait_ge(dve_step, own.n)
                    copied(dve, key)
                    own.link(V.tensor_tensor(z1[:, 0, :], z1[:, 0, :], z2[:, 1, :], ALU.add))
                    own.link(V.tensor_tensor(z1[:, 1, :], z1[:, 1, :], z2[:, 0, :], ALU.subtract))
                    m = row(1)[:, u:u + 1].to_broadcast([P, T])
                    for c in range(2):
                        own.mark(V.tensor_tensor_scan(out=z2[:, c, :], data0=m, data1=z1[:, c, :], initial=0.0,
                                                      op0=ALU.mult, op1=ALU.add))
                    dve.wait_ge(dve_step, own.n)
                    zz = z3 if q % 2 == 0 else z4
                    if u >= 2:
                        v = u - 2
                        if v % 4 < 3:
                            dve.wait_ge(s5_u, 3 * (v // 4) + v % 4 + 1)
                        else:
                            read_ready(dve, ("s5y", v // 4))
                    own.mark(V.tensor_tensor(zz, z2, ct, ALU.mult))
                    own.link(V.tensor_tensor(z1, z2, st, ALU.mult))
                    own.mark(V.tensor_tensor(zz[:, 0, :], zz[:, 0, :], z1[:, 1, :], ALU.subtract))
                    V.tensor_tensor(zz[:, 1, :], zz[:, 1, :], z1[:, 0, :], ALU.add).then_inc(s5_state, 1)
                    dve.wait_ge(s5_state, u + 1)
                    dve.wait_ge(dve_step, own.n)
                key = ("s5y", j)
                read_ready(dve, key)
                ins = V.scalar_tensor_tensor(out=y5[:, j, :], in0=u5[:, j, :], scalar=sml("s5_d")[:, j:j + 1],
                                             in1=half(key, 0), op0=ALU.mult, op1=ALU.add)
                read_done(ins, key)
                copied(dve, key)
                g = gl[:, j, :]
                own.link(V.tensor_tensor(g, y5[:, j, :], y5[:, j, :], ALU.mult))
                own.link(V.tensor_scalar(g, g, 0.044715, 1.0, ALU.mult, ALU.add))
                V.tensor_tensor(g, g, y5[:, j, :], ALU.mult).then_inc(s5_gelu_in, 1)
            for j in range(8):
                dve.wait_ge(s5_gelu_t, j + 1)
                g = gl[:, j, :]
                own.link(V.scalar_tensor_tensor(out=g, in0=g, scalar=1.0, in1=y5[:, j, :], op0=ALU.add, op1=ALU.mult))
                V.tensor_scalar(y5[:, j, :], g, 0.5, None, ALU.mult).then_inc(s5_y, 1)
            dve.wait_ge(s5_y, 8)
            for n in range(4):
                dve.wait_ge(glu_tanh, n + 1)
                key = (("glu", n // 2), n % 2)
                copied(dve, key)
                a = flat(gl[:, 2 * n:2 * n + 2, :])
                t = flat(u5[:, 2 * n:2 * n + 2, :])
                own.link(V.scalar_tensor_tensor(out=a, in0=t, scalar=1.0, in1=a, op0=ALU.add, op1=ALU.mult))
                own.link(V.tensor_scalar(a, a, 0.5, None, ALU.mult))
                for m in range(2):
                    k = 2 * n + m
                    ins = V.scalar_tensor_tensor(out=x[:, k, :], in0=gl[:, k, :], scalar=mod2[:, 1, 16 + k:17 + k],
                                                 in1=x[:, k, :], op0=ALU.mult, op1=ALU.add)
                    if m == 0:
                        own.mark(ins)
                key = (("glu", 2 + n // 2), n % 2)
                read_done(ins, key)
            dve.wait_ge(dve_step, own.n)
            x_complete([(("glu", 2 + n // 2), n % 2) for n in range(4)])
            ffn(1)
            norm(8)
            dve.wait_ge(act_g, 2 * KD)
            V.memset(tiny[:, 499:500], 0.0).then_inc(x_ready, 1)

        @block.gpsimd
        def _(pool):
            own = Steps(pool, pool_step)
            G = nc.gpsimd
            pool.wait_ge(x_ready, 1)
            pool.dma_start(w_rt, w_router.rearrange("(k p) n -> p k n", p=P)).then_inc(router_in, 16)
            pool.dma_start(b_out_sb[0:E, :], b_out).then_inc(bout_in, 16)
            pool.wait_ge(x_ready, 2)
            pool.dma_start(rot[:, 0, 0:T].bitcast(I32), pos).then_inc(pos_in, 16)
            pool.wait_ge(pos_in, 16)
            G.tensor_copy(rs[:, 0:T], rot[:, 0, 0:T].bitcast(I32)).then_inc(pos_ready, 1)
            pool.wait_ge(x_ready, X_READY[6])
            for c in range(2):
                pool.dma_start(b_in5[:, c], s5_b[c]).then_inc(s5_in, 16)
                pool.dma_start(c_in5[:, c], s5_c[c]).then_inc(s5_in, 16)
            pool.wait_ge(s5_ab, 1)
            for j in range(8):
                cos_t, sin_t = tab[j % 2]
                if j >= 2:
                    pool.wait_ge(s5_state, 4 * (j - 1))
                own.mark(G.memset(cos_t[:, :, 0:1], 1.0))
                own.link(G.memset(sin_t[:, :, 0:1], 0.0))
                c1, s1 = s5[:, 4, 4 * j:4 * j + 4], s5[:, 5, 4 * j:4 * j + 4]
                own.mark(G.tensor_copy(cos_t[:, :, 1:2], c1.unsqueeze(2)))
                own.link(G.tensor_copy(sin_t[:, :, 1:2], s1.unsqueeze(2)))
                n = 2
                while n < T:
                    cn, sn = tab_t[:, :, P - 1:P], tab_u[:, :, P - 1:P]
                    ch, sh = cos_t[:, :, n // 2:n // 2 + 1], sin_t[:, :, n // 2:n // 2 + 1]
                    c_new, s_new = cos_t[:, :, n:n + 1], sin_t[:, :, n:n + 1]
                    own.mark(G.tensor_tensor(c_new, ch, ch, ALU.mult))
                    own.mark(G.tensor_tensor(cn, sh, sh, ALU.mult))
                    own.link(G.tensor_tensor(s_new, ch, sh, ALU.mult))
                    own.mark(G.tensor_tensor(c_new, c_new, cn, ALU.subtract))
                    own.link(G.tensor_tensor(s_new, s_new, s_new, ALU.add))
                    if n > 1:
                        w = n - 1
                        lo_c, lo_s = cos_t[:, :, 1:n], sin_t[:, :, 1:n]
                        hi_c, hi_s = cos_t[:, :, n + 1:2 * n], sin_t[:, :, n + 1:2 * n]
                        bc, bs = c_new.to_broadcast([P, 4, w]), s_new.to_broadcast([P, 4, w])
                        own.mark(G.tensor_tensor(hi_c, lo_c, bc, ALU.mult))
                        own.mark(G.tensor_tensor(tab_t[:, :, 0:w], lo_s, bs, ALU.mult))
                        own.mark(G.tensor_tensor(hi_s, lo_s, bc, ALU.mult))
                        own.link(G.tensor_tensor(tab_u[:, :, 0:w], lo_c, bs, ALU.mult))
                        own.mark(G.tensor_tensor(hi_c, hi_c, tab_t[:, :, 0:w], ALU.subtract))
                        own.link(G.tensor_tensor(hi_s, hi_s, tab_u[:, :, 0:w], ALU.add))
                    n *= 2
                G.memset(tab_t[:, 0, 0:1], 0.0).then_inc(s5_table, 1)
                pool.wait_ge(s5_table, j + 1)



def kernel(**inputs):
    import concourse.bacc as bacc
    from concourse.bass_utils import run_bass_kernel_spmd

    a = {k: np.asarray(v) for k, v in inputs.items()}

    def columns(v):
        return v.reshape(-1, P).T

    def lay(v):
        return np.ascontiguousarray(v)

    heads = np.arange(512).reshape(2, 4, HD).transpose(1, 0, 2).reshape(-1)
    w_qkv = a["w_qkv"][0]
    w_qkv = np.concatenate([w_qkv[:, heads], w_qkv[:, 512:]], 1)
    w_o = np.concatenate([a["w_o"][0][heads], a["w_o"][0][512:]], 0)

    def states(v):
        return v.reshape(S5_PAIRS, 2 * STATE).T

    log_dt = np.repeat(a["s5_log_dt_2"][0].reshape(S5_PAIRS, 2).T, STATE, axis=0)
    parts = {
        "cond": np.stack([columns(a["c"][0]), columns(a["c_ctx"])], 2).reshape(P, 16),
        "b_ada": columns(a["b_ada"][0]), "g_attn": columns(a["g_attn"][0]),
        "g_q": np.tile(a["gqa_q_norm"][0], 2)[:, None], "g_k": np.tile(a["gqa_k_norm"][0], 2)[:, None],
        "g_sub": a["diff_subln"][0][:, None], "g_ffn": columns(a["g_ffn"][0]),
        "g_final": columns(a["g_final"]),
        "b_in": a["b_in"][0].reshape(E, 16, P).transpose(2, 0, 1).reshape(P, E * 16),
        "cond2": columns(a["c_2"][0]),
        "b_ada2": a["ada_b_2"].reshape(2, 48, P).transpose(2, 0, 1).reshape(P, 96),
        "lam_re": states(a["s5_lam_re_2"][0]), "lam_im": states(a["s5_lam_im_2"][0]), "log_dt": log_dt,
        "s5_d": columns(a["s5_d_2"][0]),
        "conv_w": a["ffn_conv_w_2"][:, :, 0].reshape(2, 3, KF, P).transpose(3, 0, 1, 2).reshape(P, -1),
        "conv_b": a["ffn_conv_b_2"].reshape(2, KF, P).transpose(2, 0, 1).reshape(P, -1),
        "g_final2": columns(a["final_norm_g_2"]),
        "dlam": np.broadcast_to(a["diff_lambda"][0].reshape(1, 4 * HD), (P, 4 * HD)),
        "b_router": np.broadcast_to(a["b_router"][0][None], (P, E)),
    }
    small = np.concatenate([parts[name] for name in SMALL], 1)
    s5_b = np.stack([a[n][0].reshape(8, 4, 2, STATE, GROUP).transpose(1, 2, 4, 0, 3).reshape(P, 8, STATE)
                     for n in ("s5_b_re_2", "s5_b_im_2")])
    s5_c = np.stack([a[n][0].reshape(S5_PAIRS, 2, GROUP, STATE).transpose(1, 3, 0, 2).reshape(P, S5_PAIRS, GROUP)
                     for n in ("s5_c_re_2", "s5_c_im_2")])
    arrays = {
        "small": small, "const": constants(),
        "xT": a["x"][0].T, "cT": a["ctx"][0].T,
        "pos": np.broadcast_to(a["pos_2"], (P, T)),
        "w_ada": a["w_ada"][0], "w_qkv": w_qkv, "w_o": w_o, "w_router": a["w_router"][0],
        "w_in": a["w_in"][0], "w_out": a["w_out"][0], "b_out": a["b_out"][0],
        "w_ada2": a["ada_w_2"], "w_ret": a["ret_w_in_2"][0],
        "w_rout": a["ret_w_out_2"][0].reshape(16, P, 4, T).transpose(2, 1, 0, 3),
        "w_s5in": a["s5_w_in_2"][0], "s5_b": s5_b, "s5_c": s5_c, "w_glu": a["s5_w_glu_2"][0],
        "w_up": a["ffn_w_up_2"],
        "w_down": a["ffn_w_down_2"].reshape(2, KF, P, KD, P).transpose(0, 3, 2, 1, 4),
    }
    nc = bacc.Bacc("TRN2", target_bir_lowering=False, num_devices=1)
    feed, args = {}, []
    for name, v in arrays.items():
        v = lay(v)
        feed[f"in_{name}_dram"] = v
        args.append(nc.dram_tensor(f"in_{name}_dram", v.shape, mybir.dt.from_np(v.dtype), kind="ExternalInput").ap())
    out = nc.dram_tensor("out_dram", (D, T), F32, kind="ExternalOutput").ap()
    transformer_blocks_kernel(nc, *args, out)
    r = run_bass_kernel_spmd(nc, [feed], core_ids=[0])
    return np.ascontiguousarray(r.results[0]["out_dram"].T).reshape(1, T, D)
```

```python
from contextlib import ExitStack

import numpy as np

import concourse.bass as bass
from concourse import mybir

F32 = mybir.dt.float32
I32 = mybir.dt.int32
U32 = mybir.dt.uint32
ALU = mybir.AluOpType
ACT = mybir.ActivationFunctionType
AX_X = mybir.AxisListType.X

P = 128
T = 256
TT = T // P
D = 1024
KD = D // P
HD = 64
EPS = 1e-6
N_KEYS = 512
KEY_TILES = N_KEYS // P
QKV = 2304
HEADS = 8
ATT_SCALE = HD ** -0.5
LAMBDA_INIT = 0.2
E = 32
TOP_K = 4
CAP = 64
BLOCKS = T // CAP
PAIRS = E // 2
MAX_JOBS = T * TOP_K // CAP
ALPHA = 1.702
LIMIT = 7.0
RET_HEADS = 4
RET_DV_TILES = 4
FF = 2816
KF = FF // P
GROUPS = 64
STATE = 64
GROUP = 16
S5_PAIRS = GROUPS // 2
GELU_C = float(np.sqrt(2.0 / np.pi))
TWO_PI = 2.0 * np.pi
ROUND = 1.5 * 2.0 ** 23
PI2_A = 6.28125
PI2_B = float(np.float32(np.float32((TWO_PI - PI2_A) * 2 ** 20).round() / 2 ** 20))
PI2_C = float(TWO_PI - PI2_A - PI2_B)
PI_IN = 3.1415925
RING = 6
SLAB = 4096
BANK = 512
ARENA = 17100

SMALL = {}
_at = 0
for _name, _width in (
    ("cond", 16), ("b_ada", 48), ("g_attn", 8), ("g_q", 1), ("g_k", 1), ("g_sub", 1), ("g_ffn", 8),
    ("g_final", 8), ("b_in", E * 16), ("cond2", 8), ("b_ada2", 96), ("lam_re", S5_PAIRS),
    ("lam_im", S5_PAIRS), ("log_dt", S5_PAIRS), ("s5_d", 8), ("conv_w", 2 * 3 * KF),
    ("conv_b", 2 * KF), ("g_final2", 8), ("dlam", 4 * HD), ("b_router", E),
):
    SMALL[_name] = (_at, _width)
    _at += _width
N_SMALL = _at

CONST = {}
_at = 0
for _name, _width in (
    ("ident", P), ("ones", P), ("head_ones", P), ("rope_perm", P), ("rope_cos", T), ("rope_sin", T),
    ("before", P), ("pick", P), ("slots", (BLOCKS + 1) * CAP), ("experts", E), ("inv_freq", 1), ("in_mask", 2),
    ("state_mask", 2), ("eps", 1), ("decay", RET_HEADS * 2 * T),
):
    CONST[_name] = (_at, _width)
    _at += _width
N_CONST = _at


def constants():
    c = np.zeros((P, N_CONST), np.float32)

    def put(name, a):
        at, width = CONST[name]
        c[:, at:at + width] = np.asarray(a, np.float32).reshape(P, width)

    p = np.arange(P)
    put("ident", np.eye(P))
    put("ones", np.ones((P, P)))
    put("head_ones", (p[:, None] // HD) == (p[None, :] // HD))
    perm = np.zeros((P, P))
    for d in range(P):
        first = d % 32 < 16
        perm[d + 16 if first else d - 16, d] = -1.0 if first else 1.0
    put("rope_perm", perm)
    n_freq = HD // 4
    inv = (np.float32(10000.0) ** (-np.arange(n_freq, dtype=np.float32) / n_freq)).astype(np.float32)
    t = np.arange(T)
    place = np.where((p[:, None] % HD) < 32, t[None] // 64, t[None] % 64).astype(np.float32)
    ang = (place * inv[p % 16][:, None]).astype(np.float32).astype(np.float64)
    put("rope_cos", np.cos(ang))
    put("rope_sin", np.sin(ang))
    put("before", p[:, None] < p[None, :])
    put("pick", (p[:, None] % 32 == p[None, :]) & (p[None, :] < 2))
    put("slots", np.broadcast_to(np.arange((BLOCKS + 1) * CAP), (P, (BLOCKS + 1) * CAP)))
    put("experts", np.broadcast_to(np.arange(E), (P, E)))
    half = P
    put("inv_freq", np.float32(10000.0) ** (-np.arange(half, dtype=np.float32) / half))
    put("in_mask", np.stack([(p // GROUP) % 2 == g for g in range(2)], 1))
    put("state_mask", np.stack([p // STATE == g for g in range(2)], 1))
    put("eps", np.full((P, 1), EPS))
    lag = t[None, None, :] - (p[:, None, None] + P * np.arange(2)[None, :, None])
    decay = np.zeros((P, RET_HEADS, 2, T))
    for h in range(RET_HEADS):
        log_gamma = np.log1p(-2.0 ** (-5.0 - h))
        decay[:, h] = np.where(lag >= 0, np.exp(log_gamma * np.maximum(lag, 0)), 0.0) / 16.0
    put("decay", decay)
    return c



def plan():
    chunks, slabs = {}, {}

    def chunk(*keys):
        for k in keys:
            assert k not in chunks
            chunks[k] = len(chunks)

    def slab(key, n):
        for i in range(n):
            chunk((key, i))
        slabs[key] = len(chunks)

    def modulation(keys, first=None, flush=True):
        for i, key in enumerate(keys):
            slab(key, 1)
            before = keys[i - 1] if i else first
            if before:
                chunk(("cols", before))
        if flush:
            chunk(("cols", keys[-1]))

    modulation([("ada", s) for s in range(4)])
    chunk(("norm", 0), ("norm", 1))
    slab("qa", 2)
    slab("kva", 2)
    slab("qb", 2)
    slab("kb", 4)
    slab("vb", 4)
    for i in range(5):
        chunk(("qknorm", i))
    for i in range(9):
        chunk(("rope", i))
    ada = [("ada", s) for s in range(4, 12)] + [("ada2", 0, s) for s in range(12)]
    before = None
    for j in range(12):
        n = 2 if j < 8 else 1
        modulation(ada[:n], before, flush=False)
        before = ada[n - 1]
        del ada[:n]
        if j < 8:
            if j % 2:
                chunk(("oa", j // 2))
        else:
            chunk(("ob", j - 8))
    assert not ada
    chunk(("cols", before))
    chunk(*(("onorm", i) for i in range(2)))
    slab("wo0", 2)
    slab("wo1", 2)
    chunk(("norm", 2), ("router", 0), ("htok", 0), ("htok", 1), ("htok", 2), ("htok", 3), ("pos", 0),
          ("gates", 0), *(("bout", i) for i in range(4)))
    before_loop = (len(chunks), len(slabs))
    chunk(("norm", 3), ("norm", 4))
    for s in range(2):
        slab(("rq", s), 2)
    for s in range(2):
        slab(("rk", s), 2)
    for s in range(4):
        slab(("rv", s), 2)
    for s in range(4):
        slab(("rg", s), 2)
    for h in range(RET_HEADS):
        chunk(("rs", h), ("ro", h, 0), ("ro", h, 1), ("rmean", h), ("rvar", h))
    for s in range(4):
        slab(("rout", s), 1)

    def ffn(layer):
        chunk(("norm", 5 + 2 * layer))
        for s in range(11):
            slab(("up", layer, s), 2)
        for s in range(8):
            slab(("down", layer, s), 1)

    ffn(0)
    modulation([("ada2", 1, s) for s in range(12)])
    chunk(("norm", 6))
    for s in range(2):
        slab(("s5in", s), 2)
    for j in range(8):
        for q in range(4):
            chunk(("bu", 4 * j + q))
        chunk(("s5y", j))
    for s in range(4):
        slab(("glu", s), 2)
    ffn(1)
    chunk(("norm", 8))
    return chunks, slabs, before_loop


CHUNK, SLABS, (CHUNKS_1, SLABS_1) = plan()
SLAB_KEYS = list(SLABS)
MOE_SLABS = 12 * PAIRS


def slab_number(key):
    n = SLAB_KEYS.index(key)
    return n if n < SLABS_1 else n + MOE_SLABS


class Steps:

    def __init__(self, eng, sem, base=0):
        self.eng, self.sem, self.base, self.n = eng, sem, base, 0

    def mark(self, ins):
        ins.then_inc(self.sem, 1)
        self.n += 1

    def link(self, ins):
        self.mark(ins)
        self.eng.wait_ge(self.sem, self.base + self.n)


def transformer_blocks_kernel(nc, small, const, xT, cT, pos, w_ada, w_qkv, w_o, w_router, w_in,
                              w_out, b_out, w_ada2, w_ret, w_rout, w_s5in, s5_b, s5_c, w_glu, w_up,
                              w_down, outT):
    ctx = ExitStack()
    with ctx:
        def sb(name, shape, dt=F32):
            return ctx.enter_context(nc.sbuf_tensor(name, shape, dt))

        def sem(name):
            return ctx.enter_context(nc.semaphore(name))

        ring = sb("ring", [P, RING, SLAB])
        consts = sb("consts", [P, N_CONST])
        smalls = sb("smalls", [P, N_SMALL])
        x = sb("x", [P, KD, T])
        sq = sb("sq", [P, KD, T])
        rstd = sb("rstd", [P, 4, T])
        mod = sb("mod", [P, 48, 2])
        mod2 = sb("mod2", [P, 2, 48])
        aff = sb("aff", [P, 8, KD])
        tiny = sb("tiny", [P, 640])
        cond32 = sb("cond32", [P, KD, 32])
        cond32_2 = sb("cond32_2", [P, KD, 32])
        arena = sb("arena", [P, ARENA])
        psum = ctx.enter_context(nc.psum_tensor("psum", [P, 8, BANK], F32))

        def con(name, *dims):
            at, width = CONST[name]
            return consts[:, at:at + width]

        def sml(name):
            at, width = SMALL[name]
            return smalls[:, at:at + width]

        def flat(ap):
            return ap.rearrange("p a b -> p (a b)")

        class Carve:

            def __init__(self, at=0):
                self.at = at

            def __call__(self, *shape):
                n = int(np.prod(shape))
                a = arena[:, self.at:self.at + n]
                self.at += n
                assert self.at <= ARENA, self.at
                if len(shape) == 2:
                    return a.rearrange("p (a b) -> p a b", b=shape[1])
                if len(shape) == 3:
                    return a.rearrange("p (a b c) -> p a b c", b=shape[1], c=shape[2])
                return a

        cut = Carve()
        h_all = cut(KD, N_KEYS)
        q_all = cut(8, T)
        k_all = cut(5, N_KEYS)
        v_all = cut(KEY_TILES, 640)
        rope_t = cut(2, BANK)
        ctx_x = cut(KD, T)
        probs = ctx_x.rearrange("p k t -> p (k t)").rearrange("p (a b) -> p a b", b=N_KEYS)
        p_t = cut(2, KEY_TILES * T)
        diag = cut(4, P)
        rows = rope_t
        mix = h_all[:, :, 0:T]
        soft = tiny[:, 0:128].rearrange("p (a b) -> p a b", b=4)
        lam = tiny[:, 256:264]
        lam_prod = tiny[:, 264:392].rearrange("p (a b) -> p a b", b=HD)

        cut = Carve()
        h_moe = cut(KD, T)
        h_tok = cut(TT, D)
        y_moe = cut(KD, T)
        x_e = cut(KD, P)
        h_cat = cut(4, BANK)
        glu = cut(KD, P)
        lin = cut(KD, P)
        tanh_e = cut(KD, P)
        y_slot = cut(D)
        g_slot = cut(T)
        sel = cut(TT, P)
        gsel = cut(TT, P)
        bias = cut(2, 16)
        flags = cut(BLOCKS - 1, E)
        cum = cut((BLOCKS - 1) * E)
        jobs_f = cut(MAX_JOBS + 3)
        jobs = cut(MAX_JOBS + 3).bitcast(I32)
        w_rt = cut(KD, E)
        b_out_sb = cut(D)
        logits = cut(TT, E)
        top = cut(TT, 8)
        top_i = cut(TT, 8)
        top_f = cut(TT, 8)
        top_e = cut(TT, 8)
        onehot = cut(2, E)
        mask = cut(TT, E)
        gate = cut(TT, E)
        slot_of = cut(TT, E)
        gates_t = cut(T)
        count = tiny[:, 400:432]
        gate_sum = tiny[:, 434:438]

        cut = Carve()
        h2 = cut(KD, T)
        after_h2 = cut.at
        rq = cut(8, T)
        rk = cut(8, T)
        rv = cut(TT, 2048)
        rg = cut(16, T)
        cos2 = cut(T)
        sin2 = cut(T)
        rot = cut(2, 2 * T)
        rs = flat(sq[:, 4:6, :])
        ro = cut(4, T)
        cut = Carve(after_h2)
        val = cut(KF, T)
        conv = cut(2, 2 * T)
        conv_t = cut(2, 2 * T)
        cut = Carve(after_h2)
        u5 = cut(KD, T)
        y5 = cut(KD, T)
        gl = cut(KD, T)
        tab = [[cut(4, T) for _ in range(2)] for _ in range(2)]
        tab_t = flat(rstd[:, 0:2, :]).rearrange("p (a b) -> p a b", b=P)
        tab_u = cut(4, P)
        z1 = cut(2, T)
        z2 = cut(2, T)
        z3 = cut(2, T)
        z4 = cut(2, T)
        b_bd = cut(2, 8, P)
        c_bd = flat(sq[:]).rearrange("p (a b c) -> p a b c", a=2, b=S5_PAIRS)
        b_in5 = flat(y5)[:, 0:1024].rearrange("p (a b c) -> p a b c", a=2, b=8)
        c_in5 = flat(y5)[:, 1024:2048].rearrange("p (a b c) -> p a b c", a=2, b=S5_PAIRS)
        c_f = flat(gl)[:, 0:1024].rearrange("p (a b c) -> p a b c", a=2, b=S5_PAIRS)
        s5 = tiny[:, 0:16 * S5_PAIRS].rearrange("p (a b) -> p a b", b=S5_PAIRS)

        small_in = sem("small_in")
        const_in = sem("const_in")
        x_in = sem("x_in")
        ctx_in = sem("ctx_in")
        router_in = sem("router_in")
        bout_in = sem("bout_in")
        pos_in = sem("pos_in")
        s5_in = sem("s5_in")
        ring_full = [sem(f"ring_full{i}") for i in range(RING)]
        stored = sem("stored")
        acc_ready = sem("acc_ready")
        acc_free = [sem(f"acc_free{b}") for b in range(4)]
        cond_tanh = sem("cond_tanh")
        cond_ready = sem("cond_ready")
        affine_ready = sem("affine_ready")
        squares_ready = sem("squares_ready")
        guess_ready = sem("guess_ready")
        normed_ready = sem("normed_ready")
        h_ready = sem("h_ready")
        x_ready = sem("x_ready")
        act_g = sem("scaled_by_g")
        q_ready = sem("q_ready")
        qk_square = sem("qk_square")
        qk_guess = sem("qk_guess")
        q_normed = sem("q_normed")
        scores_ready = sem("scores_ready")
        max_ready = sem("max_ready")
        probs_ready = sem("probs_ready")
        diag_ready = sem("diag_ready")
        pt_written = sem("pt_written")
        pt_ready = sem("pt_ready")
        mix_ready = sem("mix_ready")
        lam_exp = sem("lam_exp")
        lam_sum = sem("lam_sum")
        top_ready = sem("top_ready")
        top_exp = sem("top_exp")
        mask_ready = sem("mask_ready")
        slots_ready = sem("slots_ready")
        y_init = sem("y_init")
        over_ready = sem("over_ready")
        pos_ready = sem("pos_ready")
        angle_ready = sem("angle_ready")
        sin_ready = sem("sin_ready")
        ret_tanh = sem("ret_tanh")
        ret_gate = sem("ret_gate")
        ret_qk = sem("ret_qk")
        ret_s = sem("ret_s")
        ret_o = sem("ret_o")
        ret_sq = sem("ret_sq")
        ret_guess = sem("ret_guess")
        ret_done = sem("ret_done")
        val_ready = sem("val_ready")
        conv_start = sem("conv_start")
        conv_ready = sem("conv_ready")
        conv_tanh = sem("conv_tanh")
        act_ready = sem("act_ready")
        s5_u = sem("s5_u")
        s5_dt = sem("s5_dt")
        s5_exp = sem("s5_exp")
        s5_angle = sem("s5_angle")
        s5_ab = sem("s5_ab")
        s5_table = sem("s5_table")
        s5_state = sem("s5_state")
        s5_bc = sem("s5_bc")
        s5_gelu_in = sem("s5_gelu_in")
        s5_gelu_t = sem("s5_gelu_t")
        s5_y = sem("s5_y")
        glu_tanh = sem("glu_tanh")
        dve_step = sem("dve_step")
        act_step = sem("act_step")
        pool_step = sem("pool_step")

        class ExpertSems:

            def __init__(self, tag, halves, base):
                self.halves, self.base = halves, base
                self.product_ready = sem(f"product_ready{tag}")
                self.h_copied = sem(f"h_copied{tag}")
                self.gather_ready = sem(f"gather_ready{tag}")
                self.x_copied = sem(f"x_copied{tag}")
                self.gates_turned = sem(f"gates_turned{tag}")
                self.gates_copied = sem(f"gates_copied{tag}")
                self.y_copied = sem(f"y_copied{tag}")
                self.x_ready = sem(f"turned_ready{tag}")
                self.x_free = [sem(f"turned_free{tag}_{b}") for b in range(2)]
                self.sel_ready = sem(f"select_ready{tag}")
                self.glu_ready = sem(f"glu_ready{tag}")
                self.tanh_ready = sem(f"tanh_ready{tag}")
                self.act_ready = sem(f"expert_act_ready{tag}")
                self.step = sem(f"expert_step{tag}")
                self.done = sem(f"experts_done{tag}")

        moe = ExpertSems("", 2, 0)
        again = ExpertSems("_again", 1, 6)
        again_full = [sem(f"ring_full_again{j}") for j in range(6)]

        def cols(w, n0, n1):
            return w[:, n0:n1].rearrange("(k p) n -> p k n", p=P)

        def source(key):
            kind, s = (key, 0) if isinstance(key, str) else (key[0], key[-1])
            if kind == "ada":
                return cols(w_ada, BANK * s, BANK * s + BANK)
            if kind == "ada2":
                return cols(w_ada2[key[1]], BANK * s, BANK * s + BANK)
            if kind in QKV_COLS:
                return cols(w_qkv, *QKV_COLS[kind])
            if kind in ("wo0", "wo1"):
                n = int(kind[2])
                return cols(w_o, BANK * n, BANK * n + BANK)
            if kind in ("rq", "rk", "rv", "rg"):
                n = {"rq": 0, "rk": 2, "rv": 4, "rg": 8}[kind] + s
                return cols(w_ret, BANK * n, BANK * n + BANK)
            if kind == "rout":
                return w_rout[s]
            if kind == "up":
                return cols(w_up[key[1]], BANK * s, BANK * s + BANK)
            if kind == "down":
                return w_down[key[1], s]
            if kind == "s5in":
                return cols(w_s5in, BANK * s, BANK * s + BANK)
            assert kind == "glu"
            return cols(w_glu, BANK * s, BANK * s + BANK)

        QKV_COLS = {"qa": (0, 512), "kva": (512, 768), "qb": (768, 1280), "kb": (1280, 1792),
                    "vb": (1792, 2304)}

        def in_ring(slot, src):
            a, b = src.shape[1], src.shape[2]
            return ring[:, slot, 0:a * b].rearrange("p (a b) -> p a b", b=b)

        def slab(key):
            return in_ring(slab_number(key) % RING, source(key))

        def bank(key):
            return psum[:, CHUNK[key] % 4, :]

        def half(key, m):
            return psum[:, CHUNK[key] % 4, T * m:T * m + T]

        def two(ap):
            return ap.rearrange("p (a b) -> p a b", a=2)

        def over_tiles(ap, n):
            return ap.unsqueeze(1).to_broadcast([P, n, ap.shape[-1]])

        def read_ready(eng, key):
            eng.wait_ge(acc_ready, CHUNK[key] + 1)

        def read_done(ins, key):
            ins.then_inc(acc_free[CHUNK[key] % 4], 1)

        def copied(eng, key):
            eng.wait_ge(acc_free[CHUNK[key] % 4], CHUNK[key] // 4 + 1)

        MAPS = []
        for j in range(8):
            for b in range(2):
                MAPS.append((j // 2, HD * (j % 2), 0, b))
        for j in range(4):
            for b in range(2):
                for c in range(2):
                    MAPS.append((4 + j, HD * c, 1 + j, b))

        TURN_OF = [u if u < 16 else 16 + (u - 16) // 2 for u in range(32)]
        NEW_MAPS = [[n + 2] if n < 16 else [u for u in (2 * n - 14, 2 * n - 13) if u < 32] for n in range(24)]

        X_READY = {2: 1, 3: 2, 4: 3, 5: 4, 6: 5, 7: 6, 8: 7, "out": 8}
        MOD_KEYS = ([("ada", s) for s in range(12)] + [("ada2", 0, s) for s in range(12)]
                    + [("ada2", 1, s) for s in range(12)])
        MOD_NUMBER = {key: n for n, key in enumerate(MOD_KEYS)}
        NORMS = {
            0: (ctx_x, h_all[:, :, 0:T], 0, mod[:, 0:8, 1]),
            1: (x, h_all[:, :, T:N_KEYS], 1, mod[:, 0:8, 0]),
            2: (x, h_moe, 2, mod[:, 24:32, 0]),
            3: (x, x, None, None),
            4: (x, h2, 3, mod2[:, 0, 0:8]),
            5: (x, h2, 4, mod2[:, 0, 24:32]),
            6: (x, h2, 5, mod2[:, 1, 0:8]),
            7: (x, h2, 6, mod2[:, 1, 24:32]),
            8: (x, x, None, None),
        }
        G_ONLY = {3: "g_final", 8: "g_final2"}
        H_BASE = {0: 0, 1: 8, 2: 16, 4: 24, 5: 32, 6: 40, 7: 48}
        AFFINE = {0: 1, 1: 1, 2: 2, 4: 3, 5: 3, 6: 4, 7: 4}

        block = ctx.enter_context(nc.Block())

        @block.sync
        def _(sp):
            sp.dma_start(smalls[:], small).then_inc(small_in, 16)

            def load(n, src):
                sp.dma_start(in_ring(n % RING, src), src).then_inc(ring_full[n % RING], 16)

            def expert_source(e, s):
                w, s = (w_in, s) if s < 4 else (w_out, s - 4)
                w = w[bass.ds(e, 1)].rearrange("a k n -> (a k) n")
                return cols(w, BANK * s, BANK * s + BANK)

            for n, key in enumerate(SLAB_KEYS[:SLABS_1]):
                if n >= RING:
                    sp.wait_ge(acc_ready, SLABS[SLAB_KEYS[n - RING]])
                load(n, source(key))
                if n == 0:
                    sp.dma_start(consts[:], const).then_inc(const_in, 16)
                    sp.dma_start(ctx_x, cT.rearrange("(k p) t -> p k t", p=P)).then_inc(ctx_in, 16)
                    sp.dma_start(x[:], xT.rearrange("(k p) t -> p k t", p=P)).then_inc(x_in, 16)
            for j in range(12):
                if j < RING:
                    sp.wait_ge(acc_ready, SLABS[SLAB_KEYS[SLABS_1 + j - RING]])
                else:
                    sp.wait_ge(moe.product_ready, (j - RING) // 2 + 1)
                load(SLABS_1 + j, expert_source(j % 2, j // 2))
            with sp.Fori(1, PAIRS) as i:
                for j in range(12):
                    sp.wait_ge(moe.product_ready, i * 6 + (j // 2 - 2))
                    load(SLABS_1 + j, expert_source(i * 2 + j % 2, j // 2))

            sp.wait_ge(over_ready, 1)
            n_jobs = sp.value_load(jobs[0:1, MAX_JOBS + 2:MAX_JOBS + 3], min_val=0, max_val=MAX_JOBS)
            with sp.If(n_jobs > 0):
                sp.wait_ge(moe.product_ready, 6 * PAIRS)
                with sp.Fori(0, n_jobs) as i:
                    job = sp.value_load(jobs[0:1, bass.ds(i, 1)], min_val=0, max_val=(BLOCKS - 1) * E)
                    for j in range(6):
                        sp.wait_ge(again.product_ready, i * 6 + (j + 1))
                        src = expert_source(job % E, j)
                        sp.dma_start(in_ring(j, src), src).then_inc(again_full[j], 16)
                sp.wait_ge(again.done, 1)

            for n, key in enumerate(SLAB_KEYS[SLABS_1:]):
                if n < RING:
                    sp.wait_ge(moe.product_ready, 6 * PAIRS - 3 + n // 2 + 1)
                else:
                    sp.wait_ge(acc_ready, SLABS[SLAB_KEYS[SLABS_1 + n - RING]])
                load(slab_number(key), source(key))
            sp.wait_ge(x_ready, X_READY["out"])
            sp.dma_start(outT.rearrange("(k p) t -> p k t", p=P), x[:]).then_inc(stored, 16)
            sp.wait_ge(stored, 16)

        @block.tensor
        def _(pe):
            order = {"next": 0, "loop": False}

            def begin(key):
                c = CHUNK[key]
                assert c == order["next"], (key, c, order["next"])
                order["next"] += 1
                if c >= 4:
                    pe.wait_ge(acc_free[c % 4], c // 4)

            def end(ins):
                ins.then_inc(acc_ready, 1)

            def arrived(key):
                n = slab_number(key)
                pe.wait_ge(ring_full[n % RING], 16 * (n // RING + 1))

            def features(key, rhs, per_chunk, k_tiles=KD, m_tiles=4, first=None):
                arrived(key)
                w = slab(key)
                for m in range(m_tiles):
                    c = (key, m // per_chunk)
                    if m % per_chunk == 0:
                        begin(c)
                    width = BANK // per_chunk
                    for k in range(k_tiles):
                        if m == 0 and first:
                            first(k)
                        r = rhs(k)
                        n, at = r.shape[-1], (m % per_chunk) * width
                        ins = nc.tensor.matmul(bank(c)[:, at:at + n], w[:, k, m * P:m * P + P], r,
                                               start=(k == 0), stop=(k == k_tiles - 1))
                    if m % per_chunk == per_chunk - 1:
                        end(ins)

            def tokens(key, lhs, n_tok, width, at=0, first_chunk=0):
                w = slab(key)
                for t in range(n_tok):
                    begin((key, first_chunk + t))
                    for k in range(KD):
                        ins = nc.tensor.matmul(bank((key, first_chunk + t))[:, 0:width], lhs(k, t),
                                               w[:, k, at:at + width], start=(k == 0), stop=(k == KD - 1))
                    end(ins)

            def norm(i):
                begin(("norm", i))
                pe.wait_ge(squares_ready, i + 1)
                for k in range(KD):
                    ins = nc.tensor.matmul(half(("norm", i), 0), con("ones"), sq[:, k, :],
                                           start=(k == 0), stop=(k == KD - 1))
                end(ins)

            def h_tiles(i):
                return lambda k: pe.wait_ge(h_ready, H_BASE[i] + k + 1)

            def modulation_rows(key, cond):
                arrived(key)
                w = slab(key)
                begin((key, 0))
                for k in range(KD):
                    q = k % 4
                    ins = nc.tensor.matmul(bank((key, 0))[32 * q:32 * q + 32], cond[:, k, :], w[:, k, :],
                                           start=(k < 4), stop=(k >= 4))
                end(ins)

            def modulation_cols(key):
                begin(("cols", key))
                copied(pe, (key, 0))
                for m in range(4):
                    ins = nc.tensor.matmul(bank(("cols", key))[:, m * P:m * P + P],
                                           rows[:, MOD_NUMBER[key] % 2, m * P:m * P + P], con("pick"),
                                           start=True, stop=True)
                end(ins)

            def modulation(keys, cond, before=None, flush=True):
                for key in keys:
                    modulation_rows(key, cond(key))
                    if before:
                        modulation_cols(before)
                    before = key
                if flush:
                    modulation_cols(before)
                return before

            conds = lambda key: cond32 if key[0] == "ada" else cond32_2
            pe.wait_ge(cond_ready, 2)
            pe.wait_ge(const_in, 16)
            modulation([("ada", s) for s in range(4)], conds)
            norm(0)
            norm(1)
            pe.wait_ge(h_ready, 8)
            features("qa", lambda k: h_all[:, k, T:N_KEYS], 2, first=h_tiles(1))
            arrived("kva")
            w = slab("kva")
            begin(("kva", 0))
            for k in range(KD):
                ins = nc.tensor.matmul(bank(("kva", 0)), w[:, k, 0:P], h_all[:, k, :],
                                       start=(k == 0), stop=(k == KD - 1))
            end(ins)
            begin(("kva", 1))
            for t in range(KEY_TILES):
                for k in range(KD):
                    ins = nc.tensor.matmul(bank(("kva", 1))[:, t * P:t * P + P],
                                           h_all[:, k, t * P:t * P + P], w[:, k, P:2 * P],
                                           start=(k == 0), stop=(k == KD - 1))
            end(ins)
            features("qb", lambda k: h_all[:, k, T:N_KEYS], 2)
            features("kb", lambda k: h_all[:, k, :], 1)
            arrived("vb")
            tokens("vb", lambda k, t: h_all[:, k, t * P:t * P + P], KEY_TILES, BANK)
            for i in range(5):
                begin(("qknorm", i))
                pe.wait_ge(qk_square, i + 1)
                width = T if i < 4 else N_KEYS
                end(nc.tensor.matmul(bank(("qknorm", i))[:, 0:width], con("head_ones"),
                                     sq[:, 2 * (i % 2):2 * (i % 2) + 2, :].rearrange("p a b -> p (a b)")[:, 0:width],
                                     start=True, stop=True))
            for i in range(9):
                begin(("rope", i))
                if i == 0:
                    pe.wait_ge(q_ready, 1)
                if i < 4:
                    src = q_all[:, 2 * i:2 * i + 2, :].rearrange("p a b -> p (a b)")
                else:
                    src = k_all[:, i - 4, T:N_KEYS]
                end(nc.tensor.matmul(bank(("rope", i))[:, 0:src.shape[-1]], con("rope_perm"), src,
                                     start=True, stop=True))

            def scores(u):
                if u >= 2:
                    pe.wait_ge(probs_ready, u - 1)
                if u == 0:
                    pe.wait_ge(q_ready, 1 + 9)
                tile, part, kt, b = MAPS[u]
                nc.tensor.matmul(psum[:, 4 + u % 2, :], q_all[part:part + HD, tile, b * P:b * P + P],
                                 k_all[part:part + HD, kt, :], start=True, stop=True
                                 ).then_inc(scores_ready, 1)

            def turn(n, maps):
                pe.wait_ge(diag_ready, maps[-1] + 1)
                if n >= 2:
                    pe.wait_ge(pt_ready, n - 1)
                for kt in range(KEY_TILES):
                    for u in maps:
                        ins = nc.tensor.matmul(psum[:, 6 + n % 2, kt * P:kt * P + P],
                                               probs[:, u % 4, kt * P:kt * P + P], diag[:, u % 4, :],
                                               start=(u == maps[0]), stop=(u == maps[-1]))
                ins.then_inc(pt_written, 1)

            ada = [("ada", s) for s in range(4, 12)] + [("ada2", 0, s) for s in range(12)]
            before = None

            scores(0)
            scores(1)
            for j in range(12):
                u0, n0 = (2 * j, 2 * j) if j < 8 else (16 + 4 * (j - 8), 16 + 2 * (j - 8))
                if j < 8:
                    for b in range(2):
                        u = 2 * j + b
                        turn(n0 + b, [u])
                        if u + 2 < 32:
                            scores(u + 2)
                    before = modulation(ada[:2], conds, before, flush=False)
                    del ada[:2]
                    if j % 2:
                        begin(("oa", j // 2))
                        pe.wait_ge(pt_ready, n0 + 2)
                        for a in range(2):
                            for kt in range(KEY_TILES):
                                ins = nc.tensor.matmul(
                                    half(("oa", j // 2), 0)[a * HD:a * HD + HD],
                                    v_all[:, kt, a * HD:a * HD + HD],
                                    p_t[:, a, kt * T:kt * T + T], start=(kt == 0), stop=(kt == KEY_TILES - 1))
                        end(ins)
                else:
                    for b in range(2):
                        turn(n0 + b, [u0 + 2 * b, u0 + 2 * b + 1])
                        for c in range(2):
                            if u0 + 2 * b + c + 2 < 32:
                                scores(u0 + 2 * b + c + 2)
                    before = modulation(ada[:1], conds, before, flush=False)
                    del ada[:1]
                    begin(("ob", j - 8))
                    pe.wait_ge(pt_ready, n0 + 2)
                    for kt in range(KEY_TILES):
                        ins = nc.tensor.matmul(half(("ob", j - 8), 0),
                                               v_all[:, kt, P * (j - 7):P * (j - 7) + P],
                                               p_t[:, j % 2, kt * T:kt * T + T],
                                               start=(kt == 0), stop=(kt == KEY_TILES - 1))
                    end(ins)
            modulation_cols(before)
            for i in range(2):
                begin(("onorm", i))
                pe.wait_ge(qk_square, 6 + i)
                end(nc.tensor.matmul(bank(("onorm", i)), con("ones"),
                                     sq[:, 2 * i:2 * i + 2, :].rearrange("p a b -> p (a b)"), start=True, stop=True))
            pe.wait_ge(mix_ready, 1)
            features("wo0", lambda k: mix[:, k, :], 2)
            features("wo1", lambda k: mix[:, k, :], 2)

            norm(2)
            begin(("router", 0))
            pe.wait_ge(router_in, 16)
            pe.wait_ge(h_ready, H_BASE[2] + 8)
            for t in range(TT):
                for k in range(KD):
                    ins = nc.tensor.matmul(bank(("router", 0))[:, t * E:t * E + E],
                                           h_moe[:, k, t * P:t * P + P], w_rt[:, k, :],
                                           start=(k == 0), stop=(k == KD - 1))
            end(ins)
            for c in range(4):
                begin(("htok", c))
                for m in range(4):
                    k = 4 * (c % 2) + m
                    ins = nc.tensor.matmul(bank(("htok", c))[:, m * P:m * P + P],
                                           h_moe[:, k, (c // 2) * P:(c // 2) * P + P], con("ident"),
                                           start=True, stop=True)
                end(ins)
            begin(("pos", 0))
            pe.wait_ge(mask_ready, 1)
            b = bank(("pos", 0))
            nc.tensor.matmul(b[:, 0:E], con("before"), mask[:, 0, :], start=True, stop=True)
            nc.tensor.matmul(b[:, E:2 * E], con("ones"), mask[:, 0, :], start=True, stop=False)
            nc.tensor.matmul(b[:, E:2 * E], con("before"), mask[:, 1, :], start=False, stop=True)
            nc.tensor.matmul(b[:, 2 * E:3 * E], con("ones"), mask[:, 0, :], start=True, stop=False)
            end(nc.tensor.matmul(b[:, 2 * E:3 * E], con("ones"), mask[:, 1, :], start=False, stop=True))
            begin(("gates", 0))
            for t in range(TT):
                ins = nc.tensor.matmul(bank(("gates", 0))[0:E, t * P:t * P + P], gate[:, t, :],
                                       con("ident"), start=True, stop=True)
            end(ins)
            for c in range(4):
                begin(("bout", c))
                if c == 0:
                    pe.wait_ge(bout_in, 16)
                    copied(pe, ("gates", 0))
                for m in range(2):
                    k = 2 * c + m
                    ins = nc.tensor.matmul(half(("bout", c), m), b_out_sb[0:E, k * P:k * P + P],
                                           gates_t[0:E, :], start=True, stop=True)
                end(ins)
            for c in range(4):
                copied(pe, ("bout", c))

            def gather(s, n):
                width = CAP * s.halves
                pe.wait_ge(s.sel_ready, n)
                for c in range(2):
                    for m in range(4):
                        k = 4 * c + m
                        for t in range(TT):
                            ins = nc.tensor.matmul(psum[:, c, m * P:m * P + width],
                                                   h_tok[:, t, k * P:k * P + P], sel[:, t, 0:width],
                                                   start=(t == 0), stop=(t == TT - 1))
                    ins.then_inc(s.gather_ready, 1)

            def scatter(s, at, free_at):
                width = CAP * s.halves
                for c in range(4):
                    pe.wait_ge(s.x_free[c % 2], free_at + c // 2)
                    for m in range(2):
                        k = 2 * c + m
                        ins = nc.tensor.matmul(psum[:, 6 + c % 2, m * T:m * T + T],
                                               y_slot[0:width, k * P:k * P + P], g_slot[0:width, :],
                                               start=True, stop=True)
                    ins.then_inc(s.x_ready, 1)

            def experts(s, i, full, ring_slot):
                width = CAP * s.halves

                def product(p, act):
                    for e in range(s.halves):
                        full(s.halves * p + e)
                    for k in range(KD):
                        for e in range(s.halves):
                            w = in_ring(ring_slot(s.halves * p + e), source("wo0"))
                            ins = nc.tensor.matmul(psum[CAP * e:CAP * e + CAP, p, :],
                                                   act[:, k, CAP * e:CAP * e + CAP], w[:, k, :],
                                                   start=(k == 0), stop=(k == KD - 1))
                    ins.then_inc(s.product_ready, 1)

                def turn_h(c):
                    pe.wait_ge(s.h_copied, i * 4 + (c + 1))
                    pe.wait_ge(s.x_free[c % 2], i * 4 + (c // 2 + 1))
                    for m in range(4):
                        ins = nc.tensor.matmul(psum[:, 6 + c % 2, m * P:m * P + width],
                                               h_cat[0:width, c, m * P:m * P + P],
                                               con("ident")[0:width, 0:width], start=True, stop=True)
                    ins.then_inc(s.x_ready, 1)

                pe.wait_ge(s.x_copied, i * 2 + 2)
                product(0, x_e)
                product(1, x_e)
                turn_h(0)
                product(2, x_e)
                turn_h(1)
                product(3, x_e)
                turn_h(2)
                turn_h(3)
                gather(s, i + 2)
                pe.wait_ge(s.y_copied, i * 2 + 2)
                scatter(s, 4, i * 4 + 3)
                for t in range(TT):
                    ins = nc.tensor.matmul(psum[0:width, 2, t * P:t * P + P], gsel[:, t, 0:width],
                                           con("ident"), start=True, stop=True)
                ins.then_inc(s.gates_turned, 1)
                pe.wait_ge(s.act_ready, i + 1)
                product(4, lin)
                pe.wait_ge(s.gates_copied, i + 1)
                product(5, lin)

            def last_scatter(s, n):
                pe.wait_ge(s.y_copied, n * 2 + 2)
                scatter(s, 0, n * 4 + 1)

            gather(moe, 1)
            with pe.Fori(0, PAIRS) as i:
                def full(j):
                    n = SLABS_1 + j
                    pe.wait_ge(ring_full[n % RING], i * 32 + 16 * (n // RING + 1))
                experts(moe, i, full, lambda j: (SLABS_1 + j) % RING)
            last_scatter(moe, PAIRS)
            pe.wait_ge(over_ready, 1)
            n_jobs = pe.value_load(jobs[0:1, MAX_JOBS + 2:MAX_JOBS + 3], min_val=0, max_val=MAX_JOBS)
            with pe.If(n_jobs > 0):
                gather(again, 1)
                with pe.Fori(0, n_jobs) as i:
                    experts(again, i, lambda j: pe.wait_ge(again_full[j], i * 16 + 16), lambda j: j)
                last_scatter(again, n_jobs)
                pe.wait_ge(again.done, 1)

            norm(3)
            norm(4)
            for s in range(2):
                features(("rq", s), lambda k: h2[:, k, :], 2, first=h_tiles(4) if s == 0 else None)
            for s in range(2):
                features(("rk", s), lambda k: h2[:, k, :], 2)
            for s in range(4):
                arrived(("rv", s))
                tokens(("rv", s), lambda k, t: h2[:, k, t * P:t * P + P], TT, BANK)
            for s in range(4):
                features(("rg", s), lambda k: h2[:, k, :], 2)
            for h in range(RET_HEADS):
                begin(("rs", h))
                pe.wait_ge(ret_qk, 8)
                for m in range(TT):
                    for j in range(2):
                        ins = nc.tensor.matmul(half(("rs", h), m), rk[:, 2 * h + j, m * P:m * P + P],
                                               rq[:, 2 * h + j, :], start=(j == 0), stop=(j == 1))
                end(ins)
                for c in range(2):
                    begin(("ro", h, c))
                    if c == 0:
                        pe.wait_ge(ret_s, h + 1)
                        if h == 0:
                            for s in range(4):
                                for t in range(TT):
                                    copied(pe, (("rv", s), t))
                    for m in range(2):
                        for t in range(TT):
                            at = h * 512 + (2 * c + m) * P
                            ins = nc.tensor.matmul(half(("ro", h, c), m), rv[:, t, at:at + P],
                                                   rs[:, t * T:t * T + T], start=(t == 0), stop=(t == 1))
                    end(ins)
                begin(("rmean", h))
                copied(pe, ("ro", h, 0))
                copied(pe, ("ro", h, 1))
                for k in range(4):
                    ins = nc.tensor.matmul(half(("rmean", h), 0), con("ones"), ro[:, k, :],
                                           start=(k == 0), stop=(k == 3))
                end(ins)
                begin(("rvar", h))
                pe.wait_ge(ret_sq, h + 1)
                for k in range(4):
                    ins = nc.tensor.matmul(half(("rvar", h), 0), con("ones"), sq[:, k, :],
                                           start=(k == 0), stop=(k == 3))
                end(ins)
            pe.wait_ge(ret_done, RET_HEADS)
            for s in range(4):
                features(("rout", s), lambda k: rg[:, k, :], 2, k_tiles=16, m_tiles=2)

            def ffn(layer):
                norm(5 + 2 * layer)
                for s in range(11):
                    features(("up", layer, s), lambda k: h2[:, k, :], 2,
                             first=h_tiles(5 + 2 * layer) if s == 0 else None)
                for s in range(8):
                    features(("down", layer, s), lambda k: val[:, k, :], 1, k_tiles=KF, m_tiles=1,
                             first=(lambda k: pe.wait_ge(act_ready, 11 * layer + k // 2 + 1)) if s == 0 else None)

            ffn(0)
            modulation([("ada2", 1, s) for s in range(12)], conds)
            norm(6)
            for s in range(2):
                features(("s5in", s), lambda k: h2[:, k, :], 2, first=h_tiles(6) if s == 0 else None)
            pe.wait_ge(s5_bc, 1)
            for c in range(2):
                for s in range(2):
                    copied(pe, (("s5in", s), c))
            for j in range(8):
                for q in range(4):
                    key = ("bu", 4 * j + q)
                    begin(key)
                    for c in range(2):
                        ins = nc.tensor.matmul(half(key, c), b_bd[32 * q:32 * q + 32, c, j, :],
                                               u5[32 * q:32 * q + 32, j, :], start=True, stop=True)
                    end(ins)
                begin(("s5y", j))
                for q in range(4):
                    pe.wait_ge(s5_state, 4 * j + q + 1)
                    zz = z3 if q % 2 == 0 else z4
                    for c in range(2):
                        ins = nc.tensor.matmul(half(("s5y", j), 0)[32 * q:32 * q + 32],
                                               c_bd[:, c, 4 * j + q, :], zz[:, c, :],
                                               start=(c == 0), stop=(c == 1))
                    if q < 3:
                        ins.then_inc(s5_u, 1)
                end(ins)
            pe.wait_ge(s5_y, 8)
            for s in range(4):
                features(("glu", s), lambda k: y5[:, k, :], 2)
            ffn(1)
            norm(8)

        @block.scalar
        def _(act):
            own = Steps(act, act_step)

            def norm(i):
                src = NORMS[i][0]
                if i == 0:
                    act.wait_ge(ctx_in, 16)
                elif i == 1:
                    act.wait_ge(x_in, 16)
                    read_ready(act, ("norm", 0))
                else:
                    act.wait_ge(x_ready, X_READY[i])
                nc.scalar.activation(sq[:], src[:], ACT.Square).then_inc(squares_ready, 1)

            def guess(key, out, width, n, signal):
                read_ready(act, key)
                own.link(nc.scalar.activation(out, bank(key)[:, 0:width], ACT.Ln, scale=1.0 / n,
                                              bias=con("eps")))
                nc.scalar.activation(out, out, ACT.Exp, scale=-0.5).then_inc(signal, 1)

            def apply(i):
                guess(("norm", i), rstd[:, 0, :], T, D, guess_ready)
                _, out, row, shift = NORMS[i]
                act.wait_ge(normed_ready, i + 1)
                if row is None:
                    g = sml(G_ONLY[i])
                    for k in range(KD):
                        nc.scalar.activation(out[:, k, :], out[:, k, :], ACT.Copy, scale=g[:, k:k + 1]
                                             ).then_inc(act_g, 1)
                    return
                act.wait_ge(affine_ready, AFFINE[i])
                for k in range(KD):
                    nc.scalar.activation(out[:, k, :], out[:, k, :], ACT.Identity,
                                         scale=aff[:, row, k:k + 1], bias=shift[:, k:k + 1]
                                         ).then_inc(h_ready, 1)

            def copy_rows(key):
                n = MOD_NUMBER[key]
                if n >= 2:
                    read_ready(act, ("cols", MOD_KEYS[n - 2]))
                read_ready(act, (key, 0))
                read_done(nc.scalar.activation(rows[:, n % 2, :], bank((key, 0)), ACT.Copy), (key, 0))

            act.wait_ge(small_in, 16)
            for n, name in enumerate(("cond", "cond2")):
                w = SMALL[name][1]
                ins = nc.scalar.activation(tiny[:, 500 + 16 * n:500 + 16 * n + w], sml(name), ACT.Tanh, scale=0.5)
                ins.then_inc(cond_tanh, 1)
            act.wait_ge(const_in, 16)
            norm(0)
            for s in range(4):
                copy_rows(("ada", s))
            norm(1)
            apply(0)
            apply(1)
            act.wait_ge(lam_sum, 1)
            nc.scalar.activation(lam[:, 2:4], lam[:, 0:2], ACT.Exp).then_inc(lam_exp, 1)

            def copy(key, out, width=BANK):
                read_ready(act, key)
                src = bank(key)[:, 0:width]
                if len(out.shape) == 3:
                    src = src.rearrange("p (a b) -> p a b", b=out.shape[2])
                read_done(nc.scalar.activation(out, src, ACT.Copy), key)

            copy(("qa", 0), q_all[:, 0:2, :])
            copy(("qa", 1), q_all[:, 2:4, :])
            copy(("kva", 0), k_all[:, 0, :])
            copy(("kva", 1), v_all[:, :, 0:P])
            copy(("qb", 0), q_all[:, 4:6, :])
            copy(("qb", 1), q_all[:, 6:8, :])
            for i in range(4):
                copy(("kb", i), k_all[:, 1 + i, :])
            for i in range(4):
                copy(("vb", i), v_all[:, i, P:P + BANK])
            for i in range(5):
                src = q_all[:, i, :] if i < 4 else k_all[:, 0, :]
                dst = sq[:, 2 * (i % 2):2 * (i % 2) + 2, :].rearrange("p a b -> p (a b)")[:, 0:src.shape[-1]]
                if i == 0:
                    for key in (("qa", 0), ("qa", 1), ("kva", 0)):
                        copied(act, key)
                if i >= 2:
                    read_ready(act, ("qknorm", i - 2))
                nc.scalar.activation(dst, src, ACT.Square).then_inc(qk_square, 1)
                if i >= 1:
                    g = i - 1
                    guess(("qknorm", g), rstd[:, 0, :] if g % 2 == 0 else rstd[:, 2, :], T, HD, qk_guess)
                    act.wait_ge(q_normed, g + 1)
            guess(("qknorm", 4), rstd[:, 0:2, :].rearrange("p a b -> p (a b)"), N_KEYS, HD, qk_guess)

            def probabilities(u):
                act.wait_ge(max_ready, u + 1)
                if u >= 4:
                    act.wait_ge(pt_written, TURN_OF[u - 4] + 1)
                nc.scalar.activation(probs[:, u % 4, :], psum[:, 4 + u % 2, :], ACT.Exp,
                                     bias=soft[:, u, 0:1], scale=ATT_SCALE, accum_out=soft[:, u, 1:2]
                                     ).then_inc(probs_ready, 1)

            def copy_turned(n):
                act.wait_ge(pt_written, n + 1)
                if n < 16:
                    pair, b = n // 2, n % 2
                    slot = pair % 2
                    if n >= 4 and b == 0 and slot == 0:
                        read_ready(act, ("oa", pair // 2 - 1))
                else:
                    pair, b = n // 2, n % 2
                    slot = pair % 2
                    if b == 0:
                        if pair - 8 >= 2:
                            read_ready(act, ("ob", pair - 8 - 2))
                        else:
                            read_ready(act, ("oa", 3))
                dst = p_t[:, slot, :].rearrange("p (k t) -> p k t", t=T)[:, :, b * P:b * P + P]
                src = psum[:, 6 + n % 2, :].rearrange("p (k t) -> p k t", t=P)
                nc.scalar.activation(dst, src, ACT.Copy).then_inc(pt_ready, 1)

            probabilities(0)
            probabilities(1)
            ada = MOD_KEYS[4:24]
            for n in range(24):
                copy_turned(n)
                for u in NEW_MAPS[n]:
                    probabilities(u)
                if n % 2:
                    for key in ada[:2 if n < 16 else 1]:
                        copy_rows(key)
                    del ada[:2 if n < 16 else 1]
                if n < 16 and n % 4 == 3:
                    copy(("oa", n // 4), mix[:, n // 4, :], T)
                if n >= 16 and n % 2:
                    copy(("ob", (n - 16) // 2), mix[:, 4 + (n - 16) // 2, :], T)
            for i in range(2):
                for j in range(2):
                    copied(act, ("ob", 2 * i + j))
                nc.scalar.activation(sq[:, 2 * i:2 * i + 2, :], mix[:, 4 + 2 * i:6 + 2 * i, :], ACT.Square
                                     ).then_inc(qk_square, 1)
            for i in range(2):
                guess(("onorm", i), rstd[:, 2 * i:2 * i + 2, :].rearrange("p a b -> p (a b)") if i == 0
                      else sq[:, 6:8, :].rearrange("p a b -> p (a b)"), BANK, P, qk_guess)

            norm(2)
            apply(2)
            for c in range(4):
                copy(("htok", c), h_tok[:, c // 2, BANK * (c % 2):BANK * (c % 2) + BANK])
            act.wait_ge(top_ready, 1)
            nc.scalar.activation(top_e[:, :, 0:TOP_K], top_e[:, :, 0:TOP_K], ACT.Exp).then_inc(top_exp, 1)
            read_ready(act, ("gates", 0))
            read_done(nc.scalar.activation(gates_t[0:E, :], bank(("gates", 0))[0:E, 0:T], ACT.Copy), ("gates", 0))

            def copy_bank(s, out, src, signal):
                nc.scalar.activation(out, src, ACT.Copy).then_inc(signal, 1)

            def gathered(s, base):
                width = CAP * s.halves
                for c in range(2):
                    act.wait_ge(s.gather_ready, base + (c + 1))
                    copy_bank(s, x_e[:, 4 * c:4 * c + 4, 0:width],
                              psum[:, c, :].rearrange("p (a b) -> p a b", b=P)[:, :, 0:width], s.x_copied)

            def experts(s, i):
                width = CAP * s.halves
                for c in range(4):
                    act.wait_ge(s.product_ready, i * 6 + (s.base + c + 1))
                    copy_bank(s, h_cat[0:width, c, :], psum[0:width, c, :], s.h_copied)
                act.wait_ge(s.glu_ready, i + 1)
                nc.scalar.activation(tanh_e[:, :, 0:width], glu[:, :, 0:width], ACT.Tanh, scale=ALPHA / 2
                                     ).then_inc(s.tanh_ready, 1)
                gathered(s, i * 2 + 2)
                act.wait_ge(s.gates_turned, i + 1)
                copy_bank(s, g_slot[0:width, :], psum[0:width, 2, 0:T], s.gates_copied)
                for c in range(2):
                    act.wait_ge(s.product_ready, i * 6 + (s.base + 4 + c + 1))
                    copy_bank(s, y_slot[0:width, BANK * c:BANK * c + BANK], psum[0:width, 4 + c, :], s.y_copied)

            gathered(moe, 0)
            with act.Fori(0, PAIRS) as i:
                experts(moe, i)
            act.wait_ge(over_ready, 1)
            n_jobs = act.value_load(jobs[0:1, MAX_JOBS + 2:MAX_JOBS + 3], min_val=0, max_val=MAX_JOBS)
            with act.If(n_jobs > 0):
                gathered(again, 0)
                with act.Fori(0, n_jobs) as i:
                    experts(again, i)
                act.wait_ge(again.done, 1)
            act.wait_ge(moe.x_copied, 2 * PAIRS + 2)

            norm(3)
            apply(3)
            norm(4)
            apply(4)
            act.wait_ge(angle_ready, 1)
            for n, a in enumerate((cos2, sin2)):
                nc.scalar.activation(a, rot[:, 0, n * T:n * T + T], ACT.Sin).then_inc(sin_ready, 1)
            for s in range(4):
                for t in range(TT):
                    copy((("rv", s), t), rv[:, t, BANK * s:BANK * s + BANK])
            for s in range(4):
                for c in range(2):
                    key = (("rg", s), c)
                    read_ready(act, key)
                    n = 2 * s + c
                    if n == 0:
                        act.wait_ge(ret_qk, 8)
                    if n >= 2:
                        act.wait_ge(ret_gate, n - 1)
                    nc.scalar.activation(rot[:, n % 2, :], bank(key), ACT.Tanh, scale=0.5).then_inc(ret_tanh, 1)
            for h in range(RET_HEADS):
                for c in range(2):
                    if c == 0 and h:
                        act.wait_ge(ret_done, h)
                    copy(("ro", h, c), ro[:, 2 * c:2 * c + 2, :])
                act.wait_ge(ret_o, h + 1)
                if h:
                    read_ready(act, ("rvar", h - 1))
                nc.scalar.activation(sq[:, 0:4, :], ro[:], ACT.Square).then_inc(ret_sq, 1)
                guess(("rvar", h), rstd[:, 0, :], T, 512, ret_guess)

            def ffn(layer):
                norm(5 + 2 * layer)
                apply(5 + 2 * layer)
                w = sml("conv_w").rearrange("p (l c k) -> p l c k", l=2, c=3)[:, layer]
                b = sml("conv_b").rearrange("p (l k) -> p l k", l=2)[:, layer]
                for s in range(11):
                    for c in range(2):
                        n = 2 * s + c
                        key = (("up", layer, s), c)
                        if n < 11:
                            copy(key, val[:, 2 * n:2 * n + 2, :])
                            continue
                        m = n - 11
                        read_ready(act, key)
                        if m >= 2:
                            act.wait_ge(act_ready, 11 * layer + m - 1)
                        for a in range(2):
                            k = 2 * m + a
                            ins = nc.scalar.activation(conv[:, m % 2, a * T:a * T + T], half(key, a), ACT.Identity,
                                                       scale=w[:, 2, k:k + 1], bias=b[:, k:k + 1])
                            ins.then_inc(conv_start, 1)
                        if m >= 1:
                            tanh(layer, m - 1)
                tanh(layer, 10)

            def tanh(layer, m):
                act.wait_ge(conv_ready, 11 * layer + m + 1)
                nc.scalar.activation(conv_t[:, m % 2, :], conv[:, m % 2, :], ACT.Tanh, scale=0.5
                                     ).then_inc(conv_tanh, 1)

            ffn(0)
            for s in range(12):
                copy_rows(("ada2", 1, s))
            norm(6)
            apply(6)
            act.wait_ge(s5_dt, 1)
            nc.scalar.activation(s5[:, 0, :], sml("log_dt"), ACT.Exp).then_inc(s5_exp, 1)
            act.wait_ge(s5_dt, 2)
            nc.scalar.activation(s5[:, 1, :], s5[:, 1, :], ACT.Exp).then_inc(s5_exp, 1)
            act.wait_ge(s5_angle, 1)
            for n in range(2):
                nc.scalar.activation(s5[:, 4 + n, :], s5[:, 2 + n, :], ACT.Sin).then_inc(s5_exp, 1)
            for s in range(2):
                for c in range(2):
                    copy((("s5in", s), c), u5[:, 4 * s + 2 * c:4 * s + 2 * c + 2, :])
            for j in range(8):
                act.wait_ge(s5_gelu_in, j + 1)
                nc.scalar.activation(gl[:, j % 8, :], gl[:, j % 8, :], ACT.Tanh, scale=GELU_C
                                     ).then_inc(s5_gelu_t, 1)
            for s in range(2):
                for c in range(2):
                    if s == 0 and c == 0:
                        act.wait_ge(s5_y, 8)
                    copy((("glu", s), c), gl[:, 4 * s + 2 * c:4 * s + 2 * c + 2, :])
            for s in range(2, 4):
                for c in range(2):
                    n = 2 * (s - 2) + c
                    key = (("glu", s), c)
                    read_ready(act, key)
                    nc.scalar.activation(u5[:, 2 * n:2 * n + 2, :], two(bank(key)), ACT.Tanh, scale=0.5)\
                        .then_inc(glu_tanh, 1)
            ffn(1)
            norm(8)
            apply(8)

        @block.vector
        def _(dve):
            own = Steps(dve, dve_step)
            V = nc.vector

            def refine(key, y, v, t, width, n, guess_sem, count):
                dve.wait_ge(guess_sem, count)
                own.link(V.tensor_scalar(v, bank(key)[:, 0:width], -0.5 / n, -0.5 * EPS, ALU.mult, ALU.add))
                own.link(V.tensor_tensor(t, y, y, ALU.mult))
                own.link(V.tensor_tensor(t, t, v, ALU.mult))
                ins = V.scalar_tensor_tensor(out=y, in0=t, scalar=1.5, in1=y, op0=ALU.add, op1=ALU.mult)
                return ins

            def norm(i):
                src, out, row, _ = NORMS[i]
                key = ("norm", i)
                read_ready(dve, key)
                read_done(refine(key, rstd[:, 0, :], rstd[:, 1, :], rstd[:, 2, :], T, D, guess_ready, i + 1), key)
                copied(dve, key)
                V.tensor_tensor(out[:], src[:], over_tiles(rstd[:, 0, :], KD), ALU.mult
                                ).then_inc(normed_ready, 1)

            own.mark(V.memset(cond32[:], 0.0))
            own.link(V.memset(cond32_2[:], 0.0))
            for n, (name, dst, w) in enumerate((("cond", cond32, 2), ("cond2", cond32_2, 1))):
                dve.wait_ge(cond_tanh, n + 1)
                t = tiny[:, 500 + 16 * n:500 + 16 * n + KD * w]
                own.link(V.scalar_tensor_tensor(out=t, in0=t, scalar=1.0, in1=sml(name), op0=ALU.add, op1=ALU.mult))
                V.tensor_scalar(dst[:, :, 0:w], t.rearrange("p (k c) -> p k c", c=w), 0.5, None, ALU.mult
                                ).then_inc(cond_ready, 1)
            dl = sml("dlam").rearrange("p (a b) -> p a b", b=HD)
            for j in range(2):
                own.link(V.tensor_tensor(lam_prod[:, j, :], dl[:, 2 * j, :], dl[:, 2 * j + 1, :], ALU.mult))
            V.tensor_reduce(lam[:, 0:2], lam_prod, AX_X, ALU.add).then_inc(lam_sum, 1)

            def modulation(key):
                s = key[-1]
                read_ready(dve, ("cols", key))
                src = bank(("cols", key)).rearrange("p (m c) -> p m c", c=P)
                if key[0] == "ada":
                    b = sml("b_ada")[:, 4 * s:4 * s + 4].unsqueeze(2).to_broadcast([P, 4, 2])
                    ins = V.tensor_tensor(mod[:, 4 * s:4 * s + 4, :], src[:, :, 0:2], b, ALU.add)
                else:
                    at = 48 * key[1] + 4 * s
                    ins = V.tensor_tensor(mod2[:, key[1], 4 * s:4 * s + 4], src[:, :, 0],
                                          sml("b_ada2")[:, at:at + 4], ALU.add)
                read_done(ins, ("cols", key))

            for s in range(4):
                modulation(("ada", s))
            for s in range(4):
                copied(dve, ("cols", ("ada", s)))
            dve.wait_ge(dve_step, own.n)
            own.mark(V.scalar_tensor_tensor(out=aff[:, 0, :], in0=mod[:, 8:16, 1], scalar=1.0, in1=sml("g_attn"),
                                            op0=ALU.add, op1=ALU.mult))
            V.scalar_tensor_tensor(out=aff[:, 1, :], in0=mod[:, 8:16, 0], scalar=1.0, in1=sml("g_attn"),
                                   op0=ALU.add, op1=ALU.mult).then_inc(affine_ready, 1)
            dve.wait_ge(const_in, 16)
            norm(0)
            norm(1)
            dve.wait_ge(lam_exp, 1)
            own.link(V.tensor_tensor(lam[:, 4:5], lam[:, 3:4], lam[:, 2:3], ALU.subtract))
            own.link(V.tensor_scalar(lam[:, 5:6], lam[:, 4:5], -LAMBDA_INIT, None, ALU.add))

            for i in range(5):
                key = ("qknorm", i)
                y = rstd[:, 0, :] if i % 2 == 0 else rstd[:, 2, :]
                width = T if i < 4 else N_KEYS
                if i == 4:
                    y = rstd[:, 0:2, :].rearrange("p a b -> p (a b)")
                read_ready(dve, key)
                v = rope_t[:, 0, 0:width]
                t = rope_t[:, 1, 0:width]
                ins = refine(key, y, v, t, width, HD, qk_guess, i + 1)
                read_done(ins, key)
                copied(dve, key)
                src = q_all[:, i, :] if i < 4 else k_all[:, 0, :]
                ins = V.scalar_tensor_tensor(out=src, in0=src, scalar=sml("g_q" if i < 4 else "g_k"), in1=y,
                                             op0=ALU.mult, op1=ALU.mult)
                if i < 4:
                    ins.then_inc(q_normed, 1)
                else:
                    own.link(ins)
            dve.wait_ge(q_normed, 4)
            for j in range(2):
                copied(dve, ("qb", j))
            for j in range(4):
                copied(dve, ("kb", j))
                copied(dve, ("vb", j))
            V.memset(tiny[:, 499:500], 0.0).then_inc(q_ready, 1)
            for i in range(9):
                key = ("rope", i)
                read_ready(dve, key)
                if i < 4:
                    dst, ps = q_all[:, 2 * i:2 * i + 2, :], two(bank(key))
                    n = 2
                else:
                    dst, ps = k_all[:, i - 4:i - 3, T:N_KEYS], bank(key)[:, 0:T].unsqueeze(1)
                    n = 1
                t = rope_t[:, 0, 0:n * T].rearrange("p (a b) -> p a b", b=T)
                own.mark(V.tensor_tensor(dst, dst, over_tiles(con("rope_cos"), n), ALU.mult))
                ins = V.tensor_tensor(t, ps, over_tiles(con("rope_sin"), n), ALU.mult)
                read_done(ins, key)
                dve.wait_ge(dve_step, own.n)
                copied(dve, key)
                V.tensor_tensor(dst, dst, t, ALU.add).then_inc(q_ready, 1)
                dve.wait_ge(q_ready, 2 + i)

            def maximum(u):
                dve.wait_ge(scores_ready, u + 1)
                own.link(V.tensor_reduce(soft[:, u, 2:3], psum[:, 4 + u % 2, :], AX_X, ALU.max))
                V.tensor_scalar(soft[:, u, 0:1], soft[:, u, 2:3], -ATT_SCALE, None, ALU.mult).then_inc(max_ready, 1)

            def factor(u):
                dve.wait_ge(probs_ready, u + 1)
                if u >= 4:
                    dve.wait_ge(pt_written, TURN_OF[u - 4] + 1)
                own.link(V.reciprocal(soft[:, u, 3:4], soft[:, u, 1:2]))
                if u >= 16 and u % 2:
                    own.link(V.tensor_tensor(soft[:, u, 3:4], soft[:, u, 3:4], lam[:, 5:6], ALU.mult))
                V.tensor_scalar(diag[:, u % 4, :], con("ident"), soft[:, u, 3:4], None, ALU.mult
                                ).then_inc(diag_ready, 1)

            ada = MOD_KEYS[4:24]

            maximum(0)
            maximum(1)
            for j in range(12):
                maps = [[2 * j], [2 * j + 1]] if j < 8 else [[4 * j - 16, 4 * j - 15], [4 * j - 14, 4 * j - 13]]
                for turned in maps:
                    for u in turned:
                        factor(u)
                    for u in turned:
                        if u + 2 < 32:
                            maximum(u + 2)
                n = (2 if j < 8 else 1) - (j == 0)
                for key in ada[:n]:
                    modulation(key)
                del ada[:n]
            modulation(ada.pop(0))
            assert not ada
            for key in MOD_KEYS[4:24]:
                copied(dve, ("cols", key))
            V.scalar_tensor_tensor(out=aff[:, 2, :], in0=mod[:, 32:40, 0], scalar=1.0, in1=sml("g_ffn"),
                                   op0=ALU.add, op1=ALU.mult).then_inc(affine_ready, 1)
            own.mark(V.tensor_scalar(aff[:, 3, :], mod2[:, 0, 8:16], 1.0, None, ALU.add))
            V.tensor_scalar(aff[:, 4, :], mod2[:, 0, 32:40], 1.0, None, ALU.add).then_inc(affine_ready, 1)
            for i in range(2):
                key = ("onorm", i)
                read_ready(dve, key)
                y = (rstd[:, 0:2, :] if i == 0 else sq[:, 6:8, :]).rearrange("p a b -> p (a b)")
                ins = refine(key, y, rope_t[:, 0, :], rope_t[:, 1, :], BANK, P, qk_guess, 6 + i)
                read_done(ins, key)
                copied(dve, key)
                o = mix[:, 4 + 2 * i:6 + 2 * i, :]
                own.link(V.tensor_tensor(o, o, two(y), ALU.mult))
                ins = V.tensor_scalar(o, o, sml("g_sub"), 1.0 - LAMBDA_INIT, ALU.mult, ALU.mult)
                if i == 0:
                    own.link(ins)
                else:
                    ins.then_inc(mix_ready, 1)
                    dve.wait_ge(mix_ready, 1)

            def add_to_x(key, m0, gate_col, n=2, last=None):
                read_ready(dve, key)
                for m in range(n):
                    ins = V.scalar_tensor_tensor(out=x[:, m0 + m, :], in0=half(key, m),
                                                 scalar=gate_col[:, m0 + m:m0 + m + 1], in1=x[:, m0 + m, :],
                                                 op0=ALU.mult, op1=ALU.add)
                    if m < n - 1:
                        own.mark(ins)
                read_done(ins, key)

            def x_complete(keys):
                for key in keys:
                    copied(dve, key)
                V.memset(tiny[:, 499:500], 0.0).then_inc(x_ready, 1)

            keys = [("wo0", 0), ("wo0", 1), ("wo1", 0), ("wo1", 1)]
            for n, key in enumerate(keys):
                add_to_x(key, 2 * n, mod[:, 16:24, 0])
            dve.wait_ge(dve_step, own.n)
            x_complete(keys)
            norm(2)

            key = ("router", 0)
            read_ready(dve, key)
            read_done(V.tensor_tensor(logits, bank(key)[:, 0:TT * E].rearrange("p (a b) -> p a b", b=E),
                                      over_tiles(sml("b_router"), TT), ALU.add), key)
            copied(dve, key)
            for t in range(TT):
                own.link(V.max(top[:, t, :], logits[:, t, :]))
                own.link(V.max_index(top_i[:, t, :].bitcast(U32), top[:, t, :], logits[:, t, :]))
            own.link(V.tensor_copy(top_f, top_i.bitcast(U32)))
            V.tensor_tensor(top_e[:, :, 0:TOP_K], top[:, :, 0:TOP_K],
                            top[:, :, 0:1].to_broadcast([P, TT, TOP_K]), ALU.subtract).then_inc(top_ready, 1)
            dve.wait_ge(top_exp, 1)
            own.link(V.tensor_reduce(gate_sum[:, 0:2], top_e[:, :, 0:TOP_K], AX_X, ALU.add))
            own.link(V.reciprocal(gate_sum[:, 2:4], gate_sum[:, 0:2]))
            for t in range(TT):
                own.link(V.tensor_scalar(top_e[:, t, 0:TOP_K], top_e[:, t, 0:TOP_K], gate_sum[:, 2 + t:3 + t],
                                         None, ALU.mult))
            for t in range(TT):
                for r in range(TOP_K):
                    dst = mask[:, t, :] if r == 0 else onehot[:, 0, :]
                    dst_g = gate[:, t, :] if r == 0 else onehot[:, 1, :]
                    own.mark(V.tensor_scalar(dst, con("experts"), top_f[:, t, r:r + 1], None, ALU.is_equal))
                    own.link(V.tensor_scalar(dst_g, con("experts"), top_f[:, t, r:r + 1],
                                             top_e[:, t, r:r + 1], ALU.is_equal, ALU.mult))
                    if r:
                        own.mark(V.tensor_tensor(mask[:, t, :], mask[:, t, :], onehot[:, 0, :], ALU.add))
                        ins = V.tensor_tensor(gate[:, t, :], gate[:, t, :], onehot[:, 1, :], ALU.add)
                        if t == TT - 1 and r == TOP_K - 1:
                            ins.then_inc(mask_ready, 1)
                        else:
                            own.link(ins)
            key = ("pos", 0)
            read_ready(dve, key)
            dve.wait_ge(mask_ready, 1)
            b = bank(key)
            own.mark(V.tensor_copy(count, b[:, 2 * E:3 * E]))
            own.link(V.scalar_tensor_tensor(out=slot_of, in0=b[:, 0:2 * E].rearrange("p (a b) -> p a b", b=E),
                                            scalar=1.0, in1=mask, op0=ALU.add, op1=ALU.mult))
            ins = V.tensor_scalar(slot_of, slot_of, -1.0, None, ALU.add)
            read_done(ins, key)
            copied(dve, key)
            for c in range(4):
                key = ("bout", c)
                read_ready(dve, key)
                read_done(V.tensor_copy(y_moe[:, 2 * c:2 * c + 2, :], two(bank(key))), key)
            for c in range(4):
                copied(dve, ("bout", c))

            def one(e):
                return slice(e, e + 1) if isinstance(e, int) else bass.ds(e, 1)

            def block_slots(b):
                at = b * CAP
                return con("slots")[:, at:at + CAP] if isinstance(b, int) else con("slots")[:, bass.ds(at, CAP)]

            def select(s, experts_of, b):
                for h in range(s.halves):
                    for t in range(TT):
                        ins = V.tensor_scalar(sel[:, t, CAP * h:CAP * h + CAP], block_slots(b),
                                              slot_of[:, t, one(experts_of[h])], None, ALU.is_equal)
                ins.then_inc(s.sel_ready, 1)

            def add_scattered(s, base):
                for c in range(4):
                    dve.wait_ge(s.x_ready, base + (c + 1))
                    V.tensor_tensor(y_moe[:, 2 * c:2 * c + 2, :], y_moe[:, 2 * c:2 * c + 2, :],
                                    two(psum[:, 6 + c % 2, :]), ALU.add).then_inc(s.x_free[c % 2], 1)

            def experts(s, i, experts_of, b, next_experts, next_b):
                width = CAP * s.halves
                step = Steps(dve, s.step, i * STEPS_OF[s.halves])
                dve.wait_ge(s.product_ready, i * 6 + (s.base + 1))
                for h in range(s.halves):
                    for t in range(TT):
                        step.mark(V.tensor_scalar(gsel[:, t, CAP * h:CAP * h + CAP], block_slots(b),
                                                  slot_of[:, t, one(experts_of[h])],
                                                  gate[:, t, one(experts_of[h])], ALU.is_equal, ALU.mult))
                for h in range(s.halves):
                    ins = V.tensor_copy(bias[:, h, :], sml("b_in").rearrange("p (e k) -> p e k", k=16)
                                        [:, one(experts_of[h]), :].rearrange("p a k -> p (a k)"))
                    step.mark(ins)
                dve.wait_ge(s.step, step.base + step.n)
                select(s, next_experts, next_b)
                for c in range(4):
                    dve.wait_ge(s.x_ready, i * 8 + (c + 1))
                    dst = (glu if c < 2 else lin)[:, 4 * (c % 2):4 * (c % 2) + 4, 0:width]
                    src = psum[:, 6 + c % 2, :].rearrange("p (a b) -> p a b", b=P)[:, :, 0:width]
                    bb = bias[:, 0:s.halves, 4 * c:4 * c + 4].rearrange("p e k -> p k e")
                    V.tensor_tensor(dst.rearrange("p k (e n) -> p k e n", n=CAP),
                                    src.rearrange("p k (e n) -> p k e n", n=CAP),
                                    bb.unsqueeze(3).to_broadcast([P, 4, s.halves, CAP]), ALU.add
                                    ).then_inc(s.x_free[c % 2], 1)
                    if c % 2 == 0:
                        continue
                    for bank_free in s.x_free:
                        dve.wait_ge(bank_free, i * 4 + (c // 2 + 2))
                    if c == 1:
                        V.tensor_scalar(glu[:, :, 0:width], glu[:, :, 0:width], LIMIT, None, ALU.min
                                        ).then_inc(s.glu_ready, 1)
                t_e, g_e, l_e = tanh_e[:, :, 0:width], glu[:, :, 0:width], lin[:, :, 0:width]
                step.link(V.tensor_scalar(l_e, l_e, LIMIT, -LIMIT, ALU.min, ALU.max))
                step.link(V.tensor_scalar(l_e, l_e, 0.5, 0.5, ALU.mult, ALU.add))
                dve.wait_ge(s.tanh_ready, i + 1)
                step.link(V.scalar_tensor_tensor(out=t_e, in0=t_e, scalar=1.0, in1=g_e, op0=ALU.add, op1=ALU.mult))
                V.tensor_tensor(l_e, l_e, t_e, ALU.mult).then_inc(s.act_ready, 1)
                add_scattered(s, i * 8 + 4)
                assert step.n == STEPS_OF[s.halves]

            def last_scattered(s, n):
                for c in range(2):
                    dve.wait_ge(s.x_free[c], n * 4 + 1)
                add_scattered(s, n * 8)
                for c in range(2):
                    dve.wait_ge(s.x_free[c], n * 4 + 3)

            STEPS_OF = {2: 9, 1: 6}

            def start(s):
                ins = V.memset(g_slot, 0.0)
                own.link(ins)
                for c in range(2):
                    dve.sem_inc(s.x_free[c], 1)
                if s.base:
                    dve.sem_inc(s.product_ready, s.base)
                for c in range(2):
                    dve.sem_inc(s.y_copied, 1)

            own.link(V.memset(y_slot, 0.0))
            start(moe)
            select(moe, (0, 1), 0)
            for b in range(1, BLOCKS):
                own.mark(V.tensor_scalar(flags[:, b - 1, :], count, float(CAP * b), None, ALU.is_gt))
            dve.wait_ge(dve_step, own.n)
            n_flags = (BLOCKS - 1) * E
            own.link(V.tensor_tensor_scan(out=cum, data0=con("ones")[:, 0:n_flags], data1=flat(flags), initial=0.0,
                                          op0=ALU.mult, op1=ALU.add))
            n_list = MAX_JOBS + 2
            cmp = flat(h_moe)[:, 0:n_list * n_flags].rearrange("p (a b) -> p a b", b=n_flags)
            own.link(V.tensor_tensor(cmp, over_tiles(cum, n_list),
                                     con("slots")[:, 0:n_list].unsqueeze(2).to_broadcast([P, n_list, n_flags]),
                                     ALU.is_le))
            own.mark(V.tensor_reduce(jobs_f[:, 0:n_list], cmp, AX_X, ALU.add))
            own.link(V.tensor_copy(jobs_f[:, n_list:n_list + 1], cum[:, n_flags - 1:n_flags]))
            V.tensor_copy(jobs, jobs_f).then_inc(over_ready, 1)
            with dve.Fori(0, PAIRS) as i:
                n = ((i + 1) % PAIRS) * 2
                experts(moe, i, (i * 2, i * 2 + 1), 0, (n, n + 1), 0)
            last_scattered(moe, PAIRS)
            dve.wait_ge(over_ready, 1)
            n_jobs = dve.value_load(jobs[0:1, MAX_JOBS + 2:MAX_JOBS + 3], min_val=0, max_val=MAX_JOBS)
            with dve.If(n_jobs > 0):
                def job_at(i):
                    job = dve.value_load(jobs[0:1, bass.ds(i, 1)], min_val=0, max_val=(BLOCKS - 1) * E)
                    return (job % E,), job // E + 1

                start(again)
                select(again, *job_at(0))
                with dve.Fori(0, n_jobs) as i:
                    experts(again, i, *job_at(i), *job_at(i + 1))
                last_scattered(again, n_jobs)
                V.memset(tiny[:, 498:499], 0.0).then_inc(again.done, 1)

            for k in range(KD):
                own.mark(V.scalar_tensor_tensor(out=x[:, k, :], in0=y_moe[:, k, :], scalar=mod[:, 40 + k, 0:1],
                                                in1=x[:, k, :], op0=ALU.mult, op1=ALU.add))
            dve.wait_ge(dve_step, own.n)
            V.memset(tiny[:, 499:500], 0.0).then_inc(x_ready, 1)

            norm(3)
            dve.wait_ge(act_g, KD)
            V.memset(tiny[:, 499:500], 0.0).then_inc(x_ready, 1)
            norm(4)

            def reduce_angle(a, n, sin_out, cos_out):
                own.link(V.tensor_scalar(n, a, float(1 / TWO_PI), ROUND, ALU.mult, ALU.add))
                own.link(V.tensor_scalar(n, n, ROUND, None, ALU.subtract))
                for part in (PI2_A, PI2_B, PI2_C):
                    own.link(V.scalar_tensor_tensor(out=a, in0=n, scalar=-part, in1=a, op0=ALU.mult, op1=ALU.add))
                own.link(V.tensor_scalar(sin_out, a, PI_IN, -PI_IN, ALU.min, ALU.max))
                own.link(V.tensor_scalar(n, sin_out, float(np.pi / 2), -TWO_PI, ALU.is_gt, ALU.mult))
                own.link(V.scalar_tensor_tensor(out=n, in0=n, scalar=float(np.pi / 2), in1=sin_out,
                                                op0=ALU.add, op1=ALU.add))
                return V.tensor_scalar(cos_out, n, PI_IN, -PI_IN, ALU.min, ALU.max)

            dve.wait_ge(pos_ready, 1)
            own.link(V.tensor_scalar(rk[:, 0, :], rk[:, 0, :], con("inv_freq"), None, ALU.mult))
            reduce_angle(rk[:, 0, :], rk[:, 1, :], rot[:, 0, T:2 * T], rot[:, 0, 0:T]).then_inc(angle_ready, 1)
            dve.wait_ge(sin_ready, 2)
            for n, (name, dst) in enumerate((("rq", rq), ("rk", rk))):
                for h in range(RET_HEADS):
                    key = ((name, h // 2), h % 2)
                    read_ready(dve, key)
                    a, b = two(rot[:, 0, :]), two(rot[:, 1, :])
                    own.mark(V.tensor_tensor(a, two(bank(key)), over_tiles(cos2, 2), ALU.mult))
                    read_done(V.tensor_tensor(b, two(bank(key)), over_tiles(sin2, 2), ALU.mult), key)
                    dve.wait_ge(dve_step, own.n)
                    copied(dve, key)
                    own.mark(V.tensor_tensor(dst[:, 2 * h, :], a[:, 0, :], b[:, 1, :], ALU.subtract))
                    V.tensor_tensor(dst[:, 2 * h + 1, :], a[:, 1, :], b[:, 0, :], ALU.add).then_inc(ret_qk, 1)
                    dve.wait_ge(dve_step, own.n)
                    dve.wait_ge(ret_qk, 4 * n + h + 1)
            for s in range(4):
                for c in range(2):
                    n = 2 * s + c
                    key = (("rg", s), c)
                    dve.wait_ge(ret_tanh, n + 1)
                    ins = V.scalar_tensor_tensor(out=rg[:, 2 * n:2 * n + 2, :].rearrange("p a b -> p (a b)"),
                                                 in0=rot[:, n % 2, :], scalar=1.0, in1=bank(key),
                                                 op0=ALU.add, op1=ALU.mult)
                    read_done(ins, key)
                    copied(dve, key)
                    V.memset(tiny[:, 499:500], 0.0).then_inc(ret_gate, 1)
            for h in range(RET_HEADS):
                key = ("rs", h)
                read_ready(dve, key)
                mask_h = con("decay")[:, 2 * T * h:2 * T * h + 2 * T]
                read_done(V.tensor_tensor(rs, bank(key), mask_h, ALU.mult), key)
                copied(dve, key)
                V.memset(tiny[:, 499:500], 0.0).then_inc(ret_s, 1)
                key = ("rmean", h)
                read_ready(dve, key)
                own.link(V.tensor_scalar(rstd[:, 3, :], half(key, 0), 1.0 / 512, None, ALU.mult))
                ins = V.tensor_tensor(ro, ro, over_tiles(rstd[:, 3, :], 4), ALU.subtract)
                read_done(ins, key)
                copied(dve, key)
                V.memset(tiny[:, 499:500], 0.0).then_inc(ret_o, 1)
                key = ("rvar", h)
                read_ready(dve, key)
                read_done(refine(key, rstd[:, 0, :], rstd[:, 1, :], rstd[:, 2, :], T, 512, ret_guess, h + 1), key)
                copied(dve, key)
                own.link(V.tensor_tensor(ro, ro, over_tiles(rstd[:, 0, :], 4), ALU.mult))
                g = rg[:, 4 * h:4 * h + 4, :]
                V.scalar_tensor_tensor(out=flat(g), in0=flat(ro), scalar=0.5, in1=flat(g), op0=ALU.mult,
                                       op1=ALU.mult).then_inc(ret_done, 1)
                dve.wait_ge(ret_done, h + 1)
            keys = [(("rout", s), 0) for s in range(4)]
            for s, key in enumerate(keys):
                add_to_x(key, 2 * s, mod2[:, 0, 16:24])
            dve.wait_ge(dve_step, own.n)
            x_complete(keys)

            def ffn(layer):
                norm(5 + 2 * layer)
                w = sml("conv_w").rearrange("p (l c k) -> p l c k", l=2, c=3)[:, layer]
                for m in range(11):
                    n = m + 11
                    key = (("up", layer, n // 2), n % 2)
                    dve.wait_ge(conv_start, 22 * layer + 2 * m + 2)
                    ps = two(bank(key))
                    cv = two(conv[:, m % 2, :])
                    for lag in (1, 2):
                        for a in range(2):
                            k = 2 * m + a
                            ins = V.scalar_tensor_tensor(out=cv[:, a, lag:T], in0=ps[:, a, 0:T - lag],
                                                         scalar=w[:, 2 - lag, k:k + 1], in1=cv[:, a, lag:T],
                                                         op0=ALU.mult, op1=ALU.add)
                            if lag == 2 and a == 1:
                                read_done(ins, key)
                            else:
                                own.mark(ins)
                        if lag == 1:
                            dve.wait_ge(dve_step, own.n)
                    dve.wait_ge(dve_step, own.n)
                    copied(dve, key)
                    V.memset(tiny[:, 499:500], 0.0).then_inc(conv_ready, 1)
                    if m >= 1:
                        finish(layer, m - 1)
                finish(layer, 10)
                keys = [(("down", layer, s), 0) for s in range(8)]
                for s, key in enumerate(keys):
                    add_to_x(key, s, mod2[:, layer, 40:48], n=1)
                x_complete(keys)

            def finish(layer, m):
                dve.wait_ge(conv_tanh, 11 * layer + m + 1)
                t, cv = conv_t[:, m % 2, :], conv[:, m % 2, :]
                n = m
                own.link(V.scalar_tensor_tensor(out=t, in0=t, scalar=1.0, in1=cv, op0=ALU.add, op1=ALU.mult))
                copied(dve, (("up", layer, n // 2), n % 2))
                v = flat(val[:, 2 * m:2 * m + 2, :])
                V.scalar_tensor_tensor(out=v, in0=t, scalar=0.5, in1=v, op0=ALU.mult, op1=ALU.mult
                                       ).then_inc(act_ready, 1)
                dve.wait_ge(act_ready, 11 * layer + m + 1)

            ffn(0)
            for s in range(12):
                modulation(("ada2", 1, s))
            for s in range(12):
                copied(dve, ("cols", ("ada2", 1, s)))
            own.mark(V.tensor_scalar(aff[:, 5, :], mod2[:, 1, 8:16], 1.0, None, ALU.add))
            V.tensor_scalar(aff[:, 6, :], mod2[:, 1, 32:40], 1.0, None, ALU.add).then_inc(affine_ready, 1)
            norm(6)

            row = lambda n: s5[:, n, :]
            re, im = sml("lam_re"), sml("lam_im")
            V.memset(tiny[:, 639:640], 0.0).then_inc(s5_dt, 1)
            dve.wait_ge(s5_exp, 1)
            own.link(V.tensor_tensor(row(10), im, row(0), ALU.mult))
            V.tensor_tensor(row(1), re, row(0), ALU.mult).then_inc(s5_dt, 1)
            reduce_angle(row(10), row(11), row(3), row(2)).then_inc(s5_angle, 1)
            dve.wait_ge(s5_exp, 4)
            own.mark(V.tensor_tensor(row(6), row(1), row(4), ALU.mult))
            own.link(V.tensor_tensor(row(7), row(1), row(5), ALU.mult))
            own.mark(V.tensor_scalar(row(10), row(6), -1.0, None, ALU.add))
            own.mark(V.tensor_tensor(row(11), re, re, ALU.mult))
            own.link(V.tensor_tensor(row(12), im, im, ALU.mult))
            own.link(V.tensor_tensor(row(11), row(11), row(12), ALU.add))
            own.link(V.reciprocal(row(11), row(11)))
            own.mark(V.tensor_tensor(row(12), row(10), re, ALU.mult))
            own.link(V.tensor_tensor(row(13), row(7), im, ALU.mult))
            own.link(V.tensor_tensor(row(12), row(12), row(13), ALU.add))
            own.link(V.tensor_tensor(row(8), row(12), row(11), ALU.mult))
            own.mark(V.tensor_tensor(row(12), row(7), re, ALU.mult))
            own.link(V.tensor_tensor(row(13), row(10), im, ALU.mult))
            own.link(V.tensor_tensor(row(12), row(12), row(13), ALU.subtract))
            own.link(V.tensor_tensor(row(9), row(12), row(11), ALU.mult))
            V.memset(tiny[:, 639:640], 0.0).then_inc(s5_ab, 1)
            dve.wait_ge(s5_in, 64)
            fr = row(8).unsqueeze(2).to_broadcast([P, S5_PAIRS, GROUP])
            fi = row(9).unsqueeze(2).to_broadcast([P, S5_PAIRS, GROUP])
            c_t = gl[:, 4:6, :].rearrange("p a b -> p (a b)").rearrange("p (a b) -> p a b", b=GROUP)
            own.mark(V.tensor_tensor(c_f[:, 0], c_in5[:, 0], fr, ALU.mult))
            own.link(V.tensor_tensor(c_t, c_in5[:, 1], fi, ALU.mult))
            own.link(V.tensor_tensor(c_f[:, 0], c_f[:, 0], c_t, ALU.subtract))
            own.mark(V.tensor_tensor(c_f[:, 1], c_in5[:, 0], fi, ALU.mult))
            own.link(V.tensor_tensor(c_t, c_in5[:, 1], fr, ALU.mult))
            own.link(V.scalar_tensor_tensor(out=flat(c_f[:, 1]), in0=flat(c_f[:, 1]), scalar=-1.0, in1=flat(c_t),
                                            op0=ALU.mult, op1=ALU.subtract))
            for c in range(2):
                for g in range(2):
                    own.mark(V.tensor_scalar(c_bd[:, c, :, GROUP * g:GROUP * g + GROUP], c_f[:, c],
                                             con("state_mask")[:, g:g + 1], None, ALU.mult))
                    own.mark(V.tensor_scalar(b_bd[:, c, :, STATE * g:STATE * g + STATE], b_in5[:, c],
                                             con("in_mask")[:, g:g + 1], None, ALU.mult))
            dve.wait_ge(dve_step, own.n)
            V.memset(tiny[:, 639:640], 0.0).then_inc(s5_bc, 1)
            for j in range(8):
                cos_t, sin_t = tab[j % 2]
                for q in range(4):
                    u = 4 * j + q
                    key = ("bu", u)
                    read_ready(dve, key)
                    if q == 0:
                        dve.wait_ge(s5_table, j + 1)
                    ct, st = over_tiles(cos_t[:, q, :], 2), over_tiles(sin_t[:, q, :], 2)
                    own.mark(V.tensor_tensor(z1, two(bank(key)), ct, ALU.mult))
                    read_done(V.tensor_tensor(z2, two(bank(key)), st, ALU.mult), key)
                    dve.wait_ge(dve_step, own.n)
                    copied(dve, key)
                    own.link(V.tensor_tensor(z1[:, 0, :], z1[:, 0, :], z2[:, 1, :], ALU.add))
                    own.link(V.tensor_tensor(z1[:, 1, :], z1[:, 1, :], z2[:, 0, :], ALU.subtract))
                    m = row(1)[:, u:u + 1].to_broadcast([P, T])
                    for c in range(2):
                        own.mark(V.tensor_tensor_scan(out=z2[:, c, :], data0=m, data1=z1[:, c, :], initial=0.0,
                                                      op0=ALU.mult, op1=ALU.add))
                    dve.wait_ge(dve_step, own.n)
                    zz = z3 if q % 2 == 0 else z4
                    if u >= 2:
                        v = u - 2
                        if v % 4 < 3:
                            dve.wait_ge(s5_u, 3 * (v // 4) + v % 4 + 1)
                        else:
                            read_ready(dve, ("s5y", v // 4))
                    own.mark(V.tensor_tensor(zz, z2, ct, ALU.mult))
                    own.link(V.tensor_tensor(z1, z2, st, ALU.mult))
                    own.mark(V.tensor_tensor(zz[:, 0, :], zz[:, 0, :], z1[:, 1, :], ALU.subtract))
                    V.tensor_tensor(zz[:, 1, :], zz[:, 1, :], z1[:, 0, :], ALU.add).then_inc(s5_state, 1)
                    dve.wait_ge(s5_state, u + 1)
                    dve.wait_ge(dve_step, own.n)
                key = ("s5y", j)
                read_ready(dve, key)
                ins = V.scalar_tensor_tensor(out=y5[:, j, :], in0=u5[:, j, :], scalar=sml("s5_d")[:, j:j + 1],
                                             in1=half(key, 0), op0=ALU.mult, op1=ALU.add)
                read_done(ins, key)
                copied(dve, key)
                g = gl[:, j, :]
                own.link(V.tensor_tensor(g, y5[:, j, :], y5[:, j, :], ALU.mult))
                own.link(V.tensor_scalar(g, g, 0.044715, 1.0, ALU.mult, ALU.add))
                V.tensor_tensor(g, g, y5[:, j, :], ALU.mult).then_inc(s5_gelu_in, 1)
            for j in range(8):
                dve.wait_ge(s5_gelu_t, j + 1)
                g = gl[:, j, :]
                own.link(V.scalar_tensor_tensor(out=g, in0=g, scalar=1.0, in1=y5[:, j, :], op0=ALU.add, op1=ALU.mult))
                V.tensor_scalar(y5[:, j, :], g, 0.5, None, ALU.mult).then_inc(s5_y, 1)
            dve.wait_ge(s5_y, 8)
            for n in range(4):
                dve.wait_ge(glu_tanh, n + 1)
                key = (("glu", n // 2), n % 2)
                copied(dve, key)
                a = flat(gl[:, 2 * n:2 * n + 2, :])
                t = flat(u5[:, 2 * n:2 * n + 2, :])
                own.link(V.scalar_tensor_tensor(out=a, in0=t, scalar=1.0, in1=a, op0=ALU.add, op1=ALU.mult))
                own.link(V.tensor_scalar(a, a, 0.5, None, ALU.mult))
                for m in range(2):
                    k = 2 * n + m
                    ins = V.scalar_tensor_tensor(out=x[:, k, :], in0=gl[:, k, :], scalar=mod2[:, 1, 16 + k:17 + k],
                                                 in1=x[:, k, :], op0=ALU.mult, op1=ALU.add)
                    if m == 0:
                        own.mark(ins)
                key = (("glu", 2 + n // 2), n % 2)
                read_done(ins, key)
            dve.wait_ge(dve_step, own.n)
            x_complete([(("glu", 2 + n // 2), n % 2) for n in range(4)])
            ffn(1)
            norm(8)
            dve.wait_ge(act_g, 2 * KD)
            V.memset(tiny[:, 499:500], 0.0).then_inc(x_ready, 1)

        @block.gpsimd
        def _(pool):
            own = Steps(pool, pool_step)
            G = nc.gpsimd
            pool.wait_ge(x_ready, 1)
            pool.dma_start(w_rt, w_router.rearrange("(k p) n -> p k n", p=P)).then_inc(router_in, 16)
            pool.dma_start(b_out_sb[0:E, :], b_out).then_inc(bout_in, 16)
            pool.wait_ge(x_ready, 2)
            pool.dma_start(rot[:, 0, 0:T].bitcast(I32), pos).then_inc(pos_in, 16)
            pool.wait_ge(pos_in, 16)
            G.tensor_copy(rk[:, 0, :], rot[:, 0, 0:T].bitcast(I32)).then_inc(pos_ready, 1)
            pool.wait_ge(x_ready, X_READY[6])
            for c in range(2):
                pool.dma_start(b_in5[:, c], s5_b[c]).then_inc(s5_in, 16)
                pool.dma_start(c_in5[:, c], s5_c[c]).then_inc(s5_in, 16)
            pool.wait_ge(s5_ab, 1)
            for j in range(8):
                cos_t, sin_t = tab[j % 2]
                if j >= 2:
                    pool.wait_ge(s5_state, 4 * (j - 1))
                own.mark(G.memset(cos_t[:, :, 0:1], 1.0))
                own.link(G.memset(sin_t[:, :, 0:1], 0.0))
                c1, s1 = s5[:, 4, 4 * j:4 * j + 4], s5[:, 5, 4 * j:4 * j + 4]
                own.mark(G.tensor_copy(cos_t[:, :, 1:2], c1.unsqueeze(2)))
                own.link(G.tensor_copy(sin_t[:, :, 1:2], s1.unsqueeze(2)))
                n = 2
                while n < T:
                    cn, sn = tab_t[:, :, P - 1:P], tab_u[:, :, P - 1:P]
                    ch, sh = cos_t[:, :, n // 2:n // 2 + 1], sin_t[:, :, n // 2:n // 2 + 1]
                    c_new, s_new = cos_t[:, :, n:n + 1], sin_t[:, :, n:n + 1]
                    own.mark(G.tensor_tensor(c_new, ch, ch, ALU.mult))
                    own.mark(G.tensor_tensor(cn, sh, sh, ALU.mult))
                    own.link(G.tensor_tensor(s_new, ch, sh, ALU.mult))
                    own.mark(G.tensor_tensor(c_new, c_new, cn, ALU.subtract))
                    own.link(G.tensor_tensor(s_new, s_new, s_new, ALU.add))
                    if n > 1:
                        w = n - 1
                        lo_c, lo_s = cos_t[:, :, 1:n], sin_t[:, :, 1:n]
                        hi_c, hi_s = cos_t[:, :, n + 1:2 * n], sin_t[:, :, n + 1:2 * n]
                        bc, bs = c_new.to_broadcast([P, 4, w]), s_new.to_broadcast([P, 4, w])
                        own.mark(G.tensor_tensor(hi_c, lo_c, bc, ALU.mult))
                        own.mark(G.tensor_tensor(tab_t[:, :, 0:w], lo_s, bs, ALU.mult))
                        own.mark(G.tensor_tensor(hi_s, lo_s, bc, ALU.mult))
                        own.link(G.tensor_tensor(tab_u[:, :, 0:w], lo_c, bs, ALU.mult))
                        own.mark(G.tensor_tensor(hi_c, hi_c, tab_t[:, :, 0:w], ALU.subtract))
                        own.link(G.tensor_tensor(hi_s, hi_s, tab_u[:, :, 0:w], ALU.add))
                    n *= 2
                G.memset(tab_t[:, 0, 0:1], 0.0).then_inc(s5_table, 1)
                pool.wait_ge(s5_table, j + 1)



def kernel(**inputs):
    import concourse.bacc as bacc
    from concourse.bass_utils import run_bass_kernel_spmd

    a = {k: np.asarray(v) for k, v in inputs.items()}

    def columns(v):
        return v.reshape(-1, P).T

    def lay(v):
        return np.ascontiguousarray(v)

    heads = np.arange(512).reshape(2, 4, HD).transpose(1, 0, 2).reshape(-1)
    w_qkv = a["w_qkv"][0]
    w_qkv = np.concatenate([w_qkv[:, heads], w_qkv[:, 512:]], 1)
    w_o = np.concatenate([a["w_o"][0][heads], a["w_o"][0][512:]], 0)

    def states(v):
        return v.reshape(S5_PAIRS, 2 * STATE).T

    log_dt = np.repeat(a["s5_log_dt_2"][0].reshape(S5_PAIRS, 2).T, STATE, axis=0)
    parts = {
        "cond": np.stack([columns(a["c"][0]), columns(a["c_ctx"])], 2).reshape(P, 16),
        "b_ada": columns(a["b_ada"][0]), "g_attn": columns(a["g_attn"][0]),
        "g_q": np.tile(a["gqa_q_norm"][0], 2)[:, None], "g_k": np.tile(a["gqa_k_norm"][0], 2)[:, None],
        "g_sub": a["diff_subln"][0][:, None], "g_ffn": columns(a["g_ffn"][0]),
        "g_final": columns(a["g_final"]),
        "b_in": a["b_in"][0].reshape(E, 16, P).transpose(2, 0, 1).reshape(P, E * 16),
        "cond2": columns(a["c_2"][0]),
        "b_ada2": a["ada_b_2"].reshape(2, 48, P).transpose(2, 0, 1).reshape(P, 96),
        "lam_re": states(a["s5_lam_re_2"][0]), "lam_im": states(a["s5_lam_im_2"][0]), "log_dt": log_dt,
        "s5_d": columns(a["s5_d_2"][0]),
        "conv_w": a["ffn_conv_w_2"][:, :, 0].reshape(2, 3, KF, P).transpose(3, 0, 1, 2).reshape(P, -1),
        "conv_b": a["ffn_conv_b_2"].reshape(2, KF, P).transpose(2, 0, 1).reshape(P, -1),
        "g_final2": columns(a["final_norm_g_2"]),
        "dlam": np.broadcast_to(a["diff_lambda"][0].reshape(1, 4 * HD), (P, 4 * HD)),
        "b_router": np.broadcast_to(a["b_router"][0][None], (P, E)),
    }
    small = np.concatenate([parts[name] for name in SMALL], 1)
    s5_b = np.stack([a[n][0].reshape(8, 4, 2, STATE, GROUP).transpose(1, 2, 4, 0, 3).reshape(P, 8, STATE)
                     for n in ("s5_b_re_2", "s5_b_im_2")])
    s5_c = np.stack([a[n][0].reshape(S5_PAIRS, 2, GROUP, STATE).transpose(1, 3, 0, 2).reshape(P, S5_PAIRS, GROUP)
                     for n in ("s5_c_re_2", "s5_c_im_2")])
    arrays = {
        "small": small, "const": constants(),
        "xT": a["x"][0].T, "cT": a["ctx"][0].T,
        "pos": np.broadcast_to(a["pos_2"], (P, T)),
        "w_ada": a["w_ada"][0], "w_qkv": w_qkv, "w_o": w_o, "w_router": a["w_router"][0],
        "w_in": a["w_in"][0], "w_out": a["w_out"][0], "b_out": a["b_out"][0],
        "w_ada2": a["ada_w_2"], "w_ret": a["ret_w_in_2"][0],
        "w_rout": a["ret_w_out_2"][0].reshape(16, P, 4, T).transpose(2, 1, 0, 3),
        "w_s5in": a["s5_w_in_2"][0], "s5_b": s5_b, "s5_c": s5_c, "w_glu": a["s5_w_glu_2"][0],
        "w_up": a["ffn_w_up_2"],
        "w_down": a["ffn_w_down_2"].reshape(2, KF, P, KD, P).transpose(0, 3, 2, 1, 4),
    }
    nc = bacc.Bacc("TRN2", target_bir_lowering=False, num_devices=1)
    feed, args = {}, []
    for name, v in arrays.items():
        v = lay(v)
        feed[f"in_{name}_dram"] = v
        args.append(nc.dram_tensor(f"in_{name}_dram", v.shape, mybir.dt.from_np(v.dtype), kind="ExternalInput").ap())
    out = nc.dram_tensor("out_dram", (D, T), F32, kind="ExternalOutput").ap()
    transformer_blocks_kernel(nc, *args, out)
    r = run_bass_kernel_spmd(nc, [feed], core_ids=[0])
    return np.ascontiguousarray(r.results[0]["out_dram"].T).reshape(1, T, D)
```

```python
from contextlib import ExitStack

import numpy as np

import concourse.bass as bass
from concourse import mybir

F32 = mybir.dt.float32
I32 = mybir.dt.int32
U32 = mybir.dt.uint32
ALU = mybir.AluOpType
ACT = mybir.ActivationFunctionType
AX_X = mybir.AxisListType.X

P = 128
T = 256
TT = T // P
D = 1024
KD = D // P
HD = 64
EPS = 1e-6
N_KEYS = 512
KEY_TILES = N_KEYS // P
QKV = 2304
HEADS = 8
ATT_SCALE = HD ** -0.5
LAMBDA_INIT = 0.2
E = 32
TOP_K = 4
CAP = 64
BLOCKS = T // CAP
PAIRS = E // 2
MAX_JOBS = T * TOP_K // CAP
ALPHA = 1.702
LIMIT = 7.0
RET_HEADS = 4
RET_DV_TILES = 4
FF = 2816
KF = FF // P
GROUPS = 64
STATE = 64
GROUP = 16
S5_PAIRS = GROUPS // 2
GELU_C = float(np.sqrt(2.0 / np.pi))
TWO_PI = 2.0 * np.pi
ROUND = 1.5 * 2.0 ** 23
PI2_A = 6.28125
PI2_B = float(np.float32(np.float32((TWO_PI - PI2_A) * 2 ** 20).round() / 2 ** 20))
PI2_C = float(TWO_PI - PI2_A - PI2_B)
PI_IN = 3.1415925
RING = 6
SLAB = 4096
BANK = 512
ARENA = 17040

SMALL = {}
_at = 0
for _name, _width in (
    ("cond", 16), ("b_ada", 48), ("g_attn", 8), ("g_q", 1), ("g_k", 1), ("g_sub", 1), ("g_ffn", 8),
    ("g_final", 8), ("b_in", E * 16), ("cond2", 8), ("b_ada2", 96), ("lam_re", S5_PAIRS),
    ("lam_im", S5_PAIRS), ("log_dt", S5_PAIRS), ("s5_d", 8), ("conv_w", 2 * 3 * KF),
    ("conv_b", 2 * KF), ("g_final2", 8), ("dlam", 4 * HD), ("b_router", E),
):
    SMALL[_name] = (_at, _width)
    _at += _width
N_SMALL = _at

CONST = {}
_at = 0
for _name, _width in (
    ("ident", P), ("ones", P), ("head_ones", P), ("rope_perm", P), ("rope_cos", T), ("rope_sin", T),
    ("before", P), ("pick", P), ("slots", (BLOCKS + 1) * CAP), ("experts", E),
    ("fold", CAP), ("inv_freq", 1), ("in_mask", 2),
    ("state_mask", 2), ("eps", 1), ("decay", RET_HEADS * 2 * T),
):
    CONST[_name] = (_at, _width)
    _at += _width
N_CONST = _at


def constants():
    c = np.zeros((P, N_CONST), np.float32)

    def put(name, a):
        at, width = CONST[name]
        c[:, at:at + width] = np.asarray(a, np.float32).reshape(P, width)

    p = np.arange(P)
    put("ident", np.eye(P))
    put("ones", np.ones((P, P)))
    put("head_ones", (p[:, None] // HD) == (p[None, :] // HD))
    perm = np.zeros((P, P))
    for d in range(P):
        first = d % 32 < 16
        perm[d + 16 if first else d - 16, d] = -1.0 if first else 1.0
    put("rope_perm", perm)
    n_freq = HD // 4
    inv = (np.float32(10000.0) ** (-np.arange(n_freq, dtype=np.float32) / n_freq)).astype(np.float32)
    t = np.arange(T)
    place = np.where((p[:, None] % HD) < 32, t[None] // 64, t[None] % 64).astype(np.float32)
    ang = (place * inv[p % 16][:, None]).astype(np.float32).astype(np.float64)
    put("rope_cos", np.cos(ang))
    put("rope_sin", np.sin(ang))
    put("before", p[:, None] < p[None, :])
    put("pick", (p[:, None] % 32 == p[None, :]) & (p[None, :] < 2))
    put("slots", np.broadcast_to(np.arange((BLOCKS + 1) * CAP), (P, (BLOCKS + 1) * CAP)))
    put("experts", np.broadcast_to(np.arange(E), (P, E)))
    put("fold", p[:, None] % CAP == np.arange(CAP)[None])
    half = P
    put("inv_freq", np.float32(10000.0) ** (-np.arange(half, dtype=np.float32) / half))
    put("in_mask", np.stack([(p // GROUP) % 2 == g for g in range(2)], 1))
    put("state_mask", np.stack([p // STATE == g for g in range(2)], 1))
    put("eps", np.full((P, 1), EPS))
    lag = t[None, None, :] - (p[:, None, None] + P * np.arange(2)[None, :, None])
    decay = np.zeros((P, RET_HEADS, 2, T))
    for h in range(RET_HEADS):
        log_gamma = np.log1p(-2.0 ** (-5.0 - h))
        decay[:, h] = np.where(lag >= 0, np.exp(log_gamma * np.maximum(lag, 0)), 0.0) / 16.0
    put("decay", decay)
    return c



ROPES_AFTER = [(2, 3), (5, 6), (7, 8), (0, 1, 4)]


def retention_steps():
    steps = [("rs", 0), "ada2"]
    for h in range(RET_HEADS):
        steps += [("ro", h, 0), ("ro", h, 1), "ada2", ("rmean", h)]
        if h < RET_HEADS - 1:
            steps += [("rs", h + 1)]
        steps += ["ada2", ("rvar", h)]
        if h < RET_HEADS - 1:
            steps += ["ada2"]
    s = iter(range(12))
    steps = [("ada2", 1, next(s)) if step == "ada2" else step for step in steps]
    assert next(s, None) is None
    return steps


RET_STEPS = retention_steps()


def plan():
    chunks, slabs = {}, {}

    def chunk(*keys):
        for k in keys:
            assert k not in chunks
            chunks[k] = len(chunks)

    def slab(key, n):
        for i in range(n):
            chunk((key, i))
        slabs[key] = len(chunks)

    def modulation(keys, first=None, flush=True):
        for i, key in enumerate(keys):
            slab(key, 1)
            before = keys[i - 1] if i else first
            if before:
                chunk(("cols", before))
        if flush:
            chunk(("cols", keys[-1]))

    chunk(("norm", 0), ("norm", 1))
    modulation([("ada", s) for s in range(4)])
    slab("qa", 2)
    slab("kva", 2)
    slab("qb", 2)
    slab("kb", 4)
    chunk(*(("qknorm", i) for i in range(3)))
    for t in range(KEY_TILES):
        chunk(("vb", t), *(("rope", i) for i in ROPES_AFTER[t]))
    slabs["vb"] = len(chunks)
    ada = [("ada", s) for s in range(4, 12)] + [("ada2", 0, s) for s in range(12)]
    before = None
    for j in range(12):
        n = 2 if j < 8 else 1
        modulation(ada[:n], before, flush=False)
        before = ada[n - 1]
        del ada[:n]
        if j < 8:
            if j % 2:
                chunk(("oa", j // 2))
        else:
            chunk(("ob", j - 8))
    assert not ada
    chunk(("cols", before))
    slab("wo0", 2)
    slab("wo1", 2)
    chunk(("norm", 2), ("router", 0), ("htok", 0), ("htok", 1), ("htok", 2), ("htok", 3), ("pos", 0),
          ("gates", 0), *(("bout", i) for i in range(4)))
    before_loop = (len(chunks), len(slabs))
    chunk(("norm", 3), ("norm", 4))
    for s in range(2):
        slab(("rq", s), 2)
    for s in range(2):
        slab(("rk", s), 2)
    for s in range(4):
        slab(("rv", s), 2)
    for s in range(4):
        slab(("rg", s), 2)
    before = None
    for step in RET_STEPS:
        if step[0] == "ada2":
            modulation([step], before, flush=False)
            before = step
        else:
            chunk(step)
    chunk(("cols", before))
    for s in range(4):
        slab(("rout", s), 1)

    def ffn(layer):
        chunk(("norm", 5 + 2 * layer))
        for s in range(11):
            slab(("up", layer, s), 2)
        for s in range(8):
            slab(("down", layer, s), 1)

    ffn(0)
    chunk(("norm", 6))
    for s in range(2):
        slab(("s5in", s), 2)
    chunk(*(("bu", u) for u in range(S5_PAIRS)))
    for s in range(4):
        slab(("glu", s), 2)
    ffn(1)
    chunk(("norm", 8))
    return chunks, slabs, before_loop


CHUNK, SLABS, (CHUNKS_1, SLABS_1) = plan()
SLAB_KEYS = list(SLABS)
MOE_SLABS = 12 * PAIRS


def slab_number(key):
    n = SLAB_KEYS.index(key)
    return n if n < SLABS_1 else n + MOE_SLABS


class Steps:

    def __init__(self, eng, sem, base=0):
        self.eng, self.sem, self.base, self.n = eng, sem, base, 0

    def mark(self, ins):
        ins.then_inc(self.sem, 1)
        self.n += 1

    def link(self, ins):
        self.mark(ins)
        self.eng.wait_ge(self.sem, self.base + self.n)


def transformer_blocks_kernel(nc, small, const, xT, cT, pos, w_ada, w_qkv, w_o, w_router, w_in,
                              w_out, b_out, w_ada2, w_ret, w_rout, w_s5in, s5_b, s5_c, w_glu, w_up,
                              w_down, outT):
    ctx = ExitStack()
    with ctx:
        def sb(name, shape, dt=F32):
            return ctx.enter_context(nc.sbuf_tensor(name, shape, dt))

        def sem(name):
            return ctx.enter_context(nc.semaphore(name))

        ring = sb("ring", [P, RING, SLAB])
        consts = sb("consts", [P, N_CONST])
        smalls = sb("smalls", [P, N_SMALL])
        x = sb("x", [P, KD, T])
        sq = sb("sq", [P, KD, T])
        rstd = sb("rstd", [P, 4, T])
        mod = sb("mod", [P, 48, 2])
        mod2 = sb("mod2", [P, 2, 48])
        aff = sb("aff", [P, 8, KD])
        tiny = sb("tiny", [P, 640])
        cond32 = sb("cond32", [P, KD, 32])
        cond32_2 = sb("cond32_2", [P, KD, 32])
        arena = sb("arena", [P, ARENA])
        psum = ctx.enter_context(nc.psum_tensor("psum", [P, 8, BANK], F32))

        def con(name, *dims):
            at, width = CONST[name]
            return consts[:, at:at + width]

        def sml(name):
            at, width = SMALL[name]
            return smalls[:, at:at + width]

        def flat(ap):
            return ap.rearrange("p a b -> p (a b)")

        class Carve:

            def __init__(self, at=0):
                self.at = at

            def __call__(self, *shape):
                n = int(np.prod(shape))
                a = arena[:, self.at:self.at + n]
                self.at += n
                assert self.at <= ARENA, self.at
                if len(shape) == 2:
                    return a.rearrange("p (a b) -> p a b", b=shape[1])
                if len(shape) == 3:
                    return a.rearrange("p (a b c) -> p a b c", b=shape[1], c=shape[2])
                return a

        cut = Carve()
        h_all = cut(KD, N_KEYS)
        q_all = cut(8, T)
        k_all = cut(5, N_KEYS)
        v_all = cut(KEY_TILES, 640)
        rope_t = cut(2, BANK)
        ctx_x = cut(KD, T)
        probs = ctx_x.rearrange("p k t -> p (k t)").rearrange("p (a b) -> p a b", b=N_KEYS)
        p_t = cut(2, KEY_TILES * T)
        diag = cut(4, P)
        rows = rope_t
        mix = h_all[:, :, 0:T]
        soft = tiny[:, 0:128].rearrange("p (a b) -> p a b", b=4)
        lam = tiny[:, 256:264]
        lam_prod = tiny[:, 264:392].rearrange("p (a b) -> p a b", b=HD)

        cut = Carve()
        h_moe = cut(KD, T)
        h_tok = cut(TT, D)
        y_moe = cut(KD, T)
        x_e = cut(KD, P)
        h_cat = cut(4, BANK)
        glu = cut(KD, P)
        lin = cut(KD, P)
        tanh_e = cut(KD, P)
        y_slot = cut(D)
        g_slot = cut(T)
        sel = cut(TT, P)
        gsel = cut(TT, P)
        bias = cut(2, 16)
        flags = cut(BLOCKS - 1, E)
        cum = cut((BLOCKS - 1) * E)
        jobs_f = cut(MAX_JOBS + 3)
        jobs = cut(MAX_JOBS + 3).bitcast(I32)
        w_rt = cut(KD, E)
        b_out_sb = cut(D)
        logits = cut(TT, E)
        top = cut(TT, 8)
        top_i = cut(TT, 8)
        top_f = cut(TT, 8)
        top_e = cut(TT, 8)
        onehot = [rstd[:, n, :].rearrange("p (t r e) -> p t r e", t=TT, r=TOP_K) for n in range(2)]
        mask = cut(TT, E)
        gate = cut(TT, E)
        slot_of = cut(TT, E)
        gates_t = cut(T)
        count = tiny[:, 400:432]
        gate_sum = tiny[:, 434:438]

        cut = Carve()
        h2 = cut(KD, T)
        after_h2 = cut.at
        rq = cut(8, T)
        rk = cut(8, T)
        rv = cut(TT, 2048)
        rg = cut(16, T)
        cos2 = cut(T)
        sin2 = cut(T)
        rot = cut(2, 2 * T)
        rs = flat(sq[:, 4:6, :])
        ro = cut(4, T)
        rows2 = rot
        after_decay = con("decay")
        cut = Carve(after_h2)
        val = cut(KF, T)
        after_val = cut.at
        conv = after_decay[:, 0:4 * T].rearrange("p (a b) -> p a b", b=2 * T)
        conv_t = after_decay[:, 4 * T:8 * T].rearrange("p (a b) -> p a b", b=2 * T)
        cut = Carve(after_val)
        cos_t = cut(S5_PAIRS, P)
        sin_t = cut(S5_PAIRS, P)
        tab_t = cut(BANK)
        tab_u = cut(BANK)
        cut = Carve(after_h2)
        u5 = cut(KD, T)
        gl = cut(KD, T)
        z_place = cut(3, BANK)
        assert cut.at <= after_val
        y5 = h2
        z1 = z_place[:, 0, :]
        z2 = flat(rstd[:]).rearrange("p (a b) -> p a b", b=BANK)
        z_cos = [z_place[:, 1, :], z_place[:, 2, :]]
        z_sin = [tab_t, tab_u]
        b_bd = after_decay.rearrange("p (a b c) -> p a b c", a=2, b=8)
        c_bd = flat(sq[:]).rearrange("p (a b c) -> p a b c", a=2, b=S5_PAIRS)
        at = CONST["rope_perm"][0]
        assert CONST["inv_freq"][0] - at >= S5_PAIRS * 32
        c_neg = consts[:, at:at + S5_PAIRS * 32].rearrange("p (a b) -> p a b", b=32)
        b_in5 = flat(gl)[:, 0:1024].rearrange("p (a b c) -> p a b c", a=2, b=8)
        c_in5 = flat(gl)[:, 1024:2048].rearrange("p (a b c) -> p a b c", a=2, b=S5_PAIRS)
        c_f = flat(z_place)[:, 0:1024].rearrange("p (a b c) -> p a b c", a=2, b=S5_PAIRS)
        c_t = z_place[:, 2, :].rearrange("p (a b) -> p a b", b=GROUP)
        s5 = tiny[:, 0:14 * S5_PAIRS].rearrange("p (a b) -> p a b", b=S5_PAIRS)
        carry = tiny[:, 520:524]

        small_in = sem("small_in")
        const_in = sem("const_in")
        decay_in = sem("decay_in")
        x_in = sem("x_in")
        ctx_in = sem("ctx_in")
        router_in = sem("router_in")
        bout_in = sem("bout_in")
        pos_in = sem("pos_in")
        s5_in = sem("s5_in")
        ring_full = [sem(f"ring_full{i}") for i in range(RING)]
        stored = sem("stored")
        acc_ready = sem("acc_ready")
        acc_free = [sem(f"acc_free{b}") for b in range(4)]
        cond_tanh = sem("cond_tanh")
        cond_ready = sem("cond_ready")
        affine_ready = sem("affine_ready")
        squares_ready = sem("squares_ready")
        guess_ready = sem("guess_ready")
        normed_ready = sem("normed_ready")
        h_ready = sem("h_ready")
        x_ready = sem("x_ready")
        act_g = sem("scaled_by_g")
        q_ready = sem("q_ready")
        qk_square = sem("qk_square")
        qk_guess = sem("qk_guess")
        q_normed = sem("q_normed")
        onorm_ready = sem("onorm_ready")
        scores_ready = sem("scores_ready")
        max_ready = sem("max_ready")
        probs_ready = sem("probs_ready")
        diag_ready = sem("diag_ready")
        pt_written = sem("pt_written")
        pt_ready = sem("pt_ready")
        mix_ready = sem("mix_ready")
        lam_exp = sem("lam_exp")
        lam_sum = sem("lam_sum")
        top_ready = sem("top_ready")
        top_exp = sem("top_exp")
        mask_ready = sem("mask_ready")
        slots_ready = sem("slots_ready")
        y_init = sem("y_init")
        over_ready = sem("over_ready")
        pos_ready = sem("pos_ready")
        angle_ready = sem("angle_ready")
        sin_ready = sem("sin_ready")
        ret_tanh = sem("ret_tanh")
        ret_gate = sem("ret_gate")
        ret_qk = sem("ret_qk")
        ret_s = sem("ret_s")
        ret_o = sem("ret_o")
        ret_sq = sem("ret_sq")
        ret_guess = sem("ret_guess")
        ret_done = sem("ret_done")
        val_ready = sem("val_ready")
        conv_start = sem("conv_start")
        conv_ready = sem("conv_ready")
        conv_tanh = sem("conv_tanh")
        act_ready = sem("act_ready")
        s5_turned = sem("s5_turned")
        s5_used = sem("s5_used")
        s5_y_read = sem("s5_y_read")
        s5_sq = sem("s5_sq")
        s5_dt = sem("s5_dt")
        s5_exp = sem("s5_exp")
        s5_angle = sem("s5_angle")
        s5_ab = sem("s5_ab")
        s5_table = sem("s5_table")
        s5_state = sem("s5_state")
        s5_bc = sem("s5_bc")
        s5_gelu_in = sem("s5_gelu_in")
        s5_gelu_t = sem("s5_gelu_t")
        s5_y = sem("s5_y")
        glu_tanh = sem("glu_tanh")
        dve_step = sem("dve_step")
        act_step = sem("act_step")
        pool_step = sem("pool_step")

        class ExpertSems:

            def __init__(self, tag, halves, base):
                self.halves, self.base = halves, base
                self.product_ready = sem(f"product_ready{tag}")
                self.h_copied = sem(f"h_copied{tag}")
                self.gather_ready = sem(f"gather_ready{tag}")
                self.x_copied = sem(f"x_copied{tag}")
                self.gates_turned = sem(f"gates_turned{tag}")
                self.gates_copied = sem(f"gates_copied{tag}")
                self.y_copied = sem(f"y_copied{tag}")
                self.x_ready = sem(f"turned_ready{tag}")
                self.x_free = [sem(f"turned_free{tag}_{b}") for b in range(2)]
                self.sel_ready = sem(f"select_ready{tag}")
                self.glu_ready = sem(f"glu_ready{tag}")
                self.tanh_ready = sem(f"tanh_ready{tag}")
                self.act_ready = sem(f"expert_act_ready{tag}")
                self.step = sem(f"expert_step{tag}")
                self.done = sem(f"experts_done{tag}")

        moe = ExpertSems("", 2, 0)
        again = ExpertSems("_again", 1, 6)
        again_full = [sem(f"ring_full_again{j}") for j in range(6)]

        def cols(w, n0, n1):
            return w[:, n0:n1].rearrange("(k p) n -> p k n", p=P)

        def source(key):
            kind, s = (key, 0) if isinstance(key, str) else (key[0], key[-1])
            if kind == "ada":
                return cols(w_ada, BANK * s, BANK * s + BANK)
            if kind == "ada2":
                return cols(w_ada2[key[1]], BANK * s, BANK * s + BANK)
            if kind in QKV_COLS:
                return cols(w_qkv, *QKV_COLS[kind])
            if kind in ("wo0", "wo1"):
                n = int(kind[2])
                return cols(w_o, BANK * n, BANK * n + BANK)
            if kind in ("rq", "rk", "rv", "rg"):
                n = {"rq": 0, "rk": 2, "rv": 4, "rg": 8}[kind] + s
                return cols(w_ret, BANK * n, BANK * n + BANK)
            if kind == "rout":
                return w_rout[s]
            if kind == "up":
                return cols(w_up[key[1]], BANK * s, BANK * s + BANK)
            if kind == "down":
                return w_down[key[1], s]
            if kind == "s5in":
                return cols(w_s5in, BANK * s, BANK * s + BANK)
            assert kind == "glu"
            return cols(w_glu, BANK * s, BANK * s + BANK)

        QKV_COLS = {"qa": (0, 512), "kva": (512, 768), "qb": (768, 1280), "kb": (1280, 1792),
                    "vb": (1792, 2304)}

        def in_ring(slot, src):
            a, b = src.shape[1], src.shape[2]
            return ring[:, slot, 0:a * b].rearrange("p (a b) -> p a b", b=b)

        def slab(key):
            return in_ring(slab_number(key) % RING, source(key))

        def bank(key):
            return psum[:, CHUNK[key] % 4, :]

        def half(key, m):
            return psum[:, CHUNK[key] % 4, T * m:T * m + T]

        def two(ap):
            return ap.rearrange("p (a b) -> p a b", a=2)

        def over_tiles(ap, n):
            return ap.unsqueeze(1).to_broadcast([P, n, ap.shape[-1]])

        def read_ready(eng, key):
            eng.wait_ge(acc_ready, CHUNK[key] + 1)

        def read_done(ins, key):
            ins.then_inc(acc_free[CHUNK[key] % 4], 1)

        def copied(eng, key):
            eng.wait_ge(acc_free[CHUNK[key] % 4], CHUNK[key] // 4 + 1)

        MAPS = []
        for j in range(8):
            for b in range(2):
                MAPS.append((j // 2, HD * (j % 2), 0, b))
        for j in range(4):
            for b in range(2):
                for c in range(2):
                    MAPS.append((4 + j, HD * c, 1 + j, b))

        TURN_OF = [u if u < 16 else 16 + (u - 16) // 2 for u in range(32)]
        NEW_MAPS = [[n + 2] if n < 16 else [u for u in (2 * n - 14, 2 * n - 13) if u < 32] for n in range(24)]

        QK_RSTD = [flat(rstd[:, 0:2, :]), flat(rstd[:, 2:4, :]), flat(sq[:, 6:8, :])]
        X_READY = {2: 1, 3: 2, 4: 3, 5: 4, 6: 5, 7: 6, 8: 7}
        MOD_KEYS = ([("ada", s) for s in range(12)] + [("ada2", 0, s) for s in range(12)]
                    + [("ada2", 1, s) for s in range(12)])
        MOD_NUMBER = {key: n for n, key in enumerate(MOD_KEYS)}
        NORMS = {
            0: (ctx_x, h_all[:, :, 0:T], 0, mod[:, 0:8, 1]),
            1: (x, h_all[:, :, T:N_KEYS], 1, mod[:, 0:8, 0]),
            2: (x, h_moe, 2, mod[:, 24:32, 0]),
            3: (x, x, None, None),
            4: (x, h2, 3, mod2[:, 0, 0:8]),
            5: (x, h2, 4, mod2[:, 0, 24:32]),
            6: (x, h2, 5, mod2[:, 1, 0:8]),
            7: (x, h2, 6, mod2[:, 1, 24:32]),
            8: (x, x, None, None),
        }
        G_ONLY = {3: "g_final", 8: "g_final2"}
        H_BASE = {0: 0, 1: 8, 2: 16, 4: 24, 5: 32, 6: 40, 7: 48}
        NORM_AFTER = {
            2: [[("wo0", 0)], [("wo0", 1)], [("wo1", 0)], [("wo1", 1)]],
            5: [[(("rout", s), 0)] for s in range(4)],
            6: [[(("down", 0, 2 * s + a), 0) for a in range(2)] for s in range(4)],
            7: [[(("glu", 2 + s // 2), s % 2)] for s in range(4)],
            8: [[(("down", 1, 2 * s + a), 0) for a in range(2)] for s in range(4)],
        }

        def squares(i, k):
            return i + 1 if i < 2 else 2 + 4 * (i - 2) + k // 2 + 1

        AFFINE = {0: 1, 1: 1, 2: 2, 4: 3, 5: 3, 6: 4, 7: 4}

        def rows_of(key):
            return (rows2 if key[:2] == ("ada2", 1) else rows)[:, MOD_NUMBER[key] % 2, :]

        block = ctx.enter_context(nc.Block())

        @block.sync
        def _(sp):
            at_decay = CONST["decay"][0]
            sp.dma_start(smalls[:], small).then_inc(small_in, 16)
            sp.dma_start(consts[:, 0:at_decay], const[:, 0:at_decay]).then_inc(const_in, 16)
            sp.dma_start(ctx_x, cT.rearrange("(k p) t -> p k t", p=P)).then_inc(ctx_in, 16)
            sp.dma_start(x[:], xT.rearrange("(k p) t -> p k t", p=P)).then_inc(x_in, 16)

            def load(n, src):
                sp.dma_start(in_ring(n % RING, src), src).then_inc(ring_full[n % RING], 16)

            def expert_source(e, s):
                w, s = (w_in, s) if s < 4 else (w_out, s - 4)
                w = w[bass.ds(e, 1)].rearrange("a k n -> (a k) n")
                return cols(w, BANK * s, BANK * s + BANK)

            for n, key in enumerate(SLAB_KEYS[:SLABS_1]):
                if n >= RING:
                    sp.wait_ge(acc_ready, SLABS[SLAB_KEYS[n - RING]])
                load(n, source(key))
                if n == RING - 1:
                    sp.dma_start(consts[:, at_decay:], const[:, at_decay:]).then_inc(decay_in, 16)
            for j in range(12):
                if j < RING:
                    sp.wait_ge(acc_ready, SLABS[SLAB_KEYS[SLABS_1 + j - RING]])
                else:
                    sp.wait_ge(moe.product_ready, (j - RING) // 2 + 1)
                load(SLABS_1 + j, expert_source(j % 2, j // 2))
            with sp.Fori(1, PAIRS) as i:
                for j in range(12):
                    sp.wait_ge(moe.product_ready, i * 6 + (j // 2 - 2))
                    load(SLABS_1 + j, expert_source(i * 2 + j % 2, j // 2))

            sp.wait_ge(over_ready, 1)
            n_jobs = sp.value_load(jobs[0:1, MAX_JOBS + 2:MAX_JOBS + 3], min_val=0, max_val=MAX_JOBS)
            with sp.If(n_jobs > 0):
                sp.wait_ge(moe.product_ready, 6 * PAIRS)
                with sp.Fori(0, n_jobs) as i:
                    job = sp.value_load(jobs[0:1, bass.ds(i, 1)], min_val=0, max_val=(BLOCKS - 1) * E)
                    for j in range(6):
                        sp.wait_ge(again.product_ready, i * 6 + (j + 1))
                        src = expert_source(job % E, j)
                        sp.dma_start(in_ring(j, src), src).then_inc(again_full[j], 16)
                sp.wait_ge(again.done, 1)

            for n, key in enumerate(SLAB_KEYS[SLABS_1:]):
                if n < RING:
                    sp.wait_ge(moe.product_ready, 6 * PAIRS - 3 + n // 2 + 1)
                else:
                    sp.wait_ge(acc_ready, SLABS[SLAB_KEYS[SLABS_1 + n - RING]])
                load(slab_number(key), source(key))
            for n in range(4):
                sp.wait_ge(act_g, KD + 2 * n + 2)
                sp.dma_start(outT.rearrange("(k p) t -> p k t", p=P)[:, 2 * n:2 * n + 2, :],
                             x[:, 2 * n:2 * n + 2, :]).then_inc(stored, 16)
            sp.wait_ge(stored, 64)

        @block.tensor
        def _(pe):
            order = {"next": 0, "loop": False}

            def begin(key):
                c = CHUNK[key]
                assert c == order["next"], (key, c, order["next"])
                order["next"] += 1
                if c >= 4:
                    pe.wait_ge(acc_free[c % 4], c // 4)

            def end(ins):
                ins.then_inc(acc_ready, 1)

            def arrived(key):
                n = slab_number(key)
                pe.wait_ge(ring_full[n % RING], 16 * (n // RING + 1))

            def features(key, rhs, per_chunk, k_tiles=KD, m_tiles=4, first=None):
                arrived(key)
                w = slab(key)
                for m in range(m_tiles):
                    c = (key, m // per_chunk)
                    if m % per_chunk == 0:
                        begin(c)
                    width = BANK // per_chunk
                    for k in range(k_tiles):
                        if m == 0 and first:
                            first(k)
                        r = rhs(k)
                        n, at = r.shape[-1], (m % per_chunk) * width
                        ins = nc.tensor.matmul(bank(c)[:, at:at + n], w[:, k, m * P:m * P + P], r,
                                               start=(k == 0), stop=(k == k_tiles - 1))
                    if m % per_chunk == per_chunk - 1:
                        end(ins)

            def tokens(key, lhs, n_tok, width, at=0, first_chunk=0):
                w = slab(key)
                for t in range(n_tok):
                    begin((key, first_chunk + t))
                    for k in range(KD):
                        ins = nc.tensor.matmul(bank((key, first_chunk + t))[:, 0:width], lhs(k, t),
                                               w[:, k, at:at + width], start=(k == 0), stop=(k == KD - 1))
                    end(ins)

            def norm(i):
                begin(("norm", i))
                for k in range(KD):
                    pe.wait_ge(squares_ready, squares(i, k))
                    ins = nc.tensor.matmul(half(("norm", i), 0), con("ones"), sq[:, k, :],
                                           start=(k == 0), stop=(k == KD - 1))
                end(ins)

            def h_tiles(i):
                return lambda k: pe.wait_ge(h_ready, H_BASE[i] + k + 1)

            def modulation_rows(key, cond):
                arrived(key)
                w = slab(key)
                begin((key, 0))
                for k in range(KD):
                    q = k % 4
                    ins = nc.tensor.matmul(bank((key, 0))[32 * q:32 * q + 32], cond[:, k, :], w[:, k, :],
                                           start=(k < 4), stop=(k >= 4))
                end(ins)

            def modulation_cols(key):
                begin(("cols", key))
                copied(pe, (key, 0))
                for m in range(4):
                    ins = nc.tensor.matmul(bank(("cols", key))[:, m * P:m * P + P],
                                           rows_of(key)[:, m * P:m * P + P], con("pick"),
                                           start=True, stop=True)
                end(ins)

            def modulation(keys, cond, before=None, flush=True):
                for key in keys:
                    modulation_rows(key, cond(key))
                    if before:
                        modulation_cols(before)
                    before = key
                if flush:
                    modulation_cols(before)
                return before

            conds = lambda key: cond32 if key[0] == "ada" else cond32_2
            pe.wait_ge(const_in, 16)
            norm(0)
            norm(1)
            pe.wait_ge(cond_ready, 2)
            modulation([("ada", s) for s in range(4)], conds)
            pe.wait_ge(h_ready, 8)
            features("qa", lambda k: h_all[:, k, T:N_KEYS], 2, first=h_tiles(1))
            arrived("kva")
            w = slab("kva")
            begin(("kva", 0))
            for k in range(KD):
                ins = nc.tensor.matmul(bank(("kva", 0)), w[:, k, 0:P], h_all[:, k, :],
                                       start=(k == 0), stop=(k == KD - 1))
            end(ins)
            begin(("kva", 1))
            for t in range(KEY_TILES):
                for k in range(KD):
                    ins = nc.tensor.matmul(bank(("kva", 1))[:, t * P:t * P + P],
                                           h_all[:, k, t * P:t * P + P], w[:, k, P:2 * P],
                                           start=(k == 0), stop=(k == KD - 1))
            end(ins)
            features("qb", lambda k: h_all[:, k, T:N_KEYS], 2)
            features("kb", lambda k: h_all[:, k, :], 1)
            for i in range(3):
                begin(("qknorm", i))
                pe.wait_ge(qk_square, 1 if i < 2 else 2)
                end(nc.tensor.matmul(bank(("qknorm", i)), con("head_ones"), flat(sq[:, 2 * i:2 * i + 2, :]),
                                     start=True, stop=True))
            arrived("vb")
            w = slab("vb")
            for t in range(KEY_TILES):
                begin(("vb", t))
                for k in range(KD):
                    ins = nc.tensor.matmul(bank(("vb", t)), h_all[:, k, t * P:t * P + P], w[:, k, :],
                                           start=(k == 0), stop=(k == KD - 1))
                end(ins)
                for i in ROPES_AFTER[t]:
                    begin(("rope", i))
                    if i in (0, 1, 4):
                        pe.wait_ge(q_normed, 3)
                    elif i < 4:
                        copied(pe, ("qb", i - 2))
                    else:
                        copied(pe, ("kb", i - 5))
                    src = flat(q_all[:, 2 * i:2 * i + 2, :]) if i < 4 else k_all[:, i - 4, T:N_KEYS]
                    end(nc.tensor.matmul(bank(("rope", i))[:, 0:src.shape[-1]], con("rope_perm"), src,
                                         start=True, stop=True))
            for i in range(4):
                copied(pe, ("kb", i))
                copied(pe, ("vb", i))
            copied(pe, ("kva", 1))

            def scores(u):
                if u >= 2:
                    pe.wait_ge(probs_ready, u - 1)
                if u == 0:
                    pe.wait_ge(q_ready, 9)
                tile, part, kt, b = MAPS[u]
                nc.tensor.matmul(psum[:, 4 + u % 2, :], q_all[part:part + HD, tile, b * P:b * P + P],
                                 k_all[part:part + HD, kt, :], start=True, stop=True
                                 ).then_inc(scores_ready, 1)

            def turn(n, maps):
                pe.wait_ge(diag_ready, maps[-1] + 1)
                if n >= 2:
                    pe.wait_ge(pt_ready, n - 1)
                for kt in range(KEY_TILES):
                    for u in maps:
                        ins = nc.tensor.matmul(psum[:, 6 + n % 2, kt * P:kt * P + P],
                                               probs[:, u % 4, kt * P:kt * P + P], diag[:, u % 4, :],
                                               start=(u == maps[0]), stop=(u == maps[-1]))
                ins.then_inc(pt_written, 1)

            ada = [("ada", s) for s in range(4, 12)] + [("ada2", 0, s) for s in range(12)]
            before = None

            scores(0)
            scores(1)
            for j in range(12):
                u0, n0 = (2 * j, 2 * j) if j < 8 else (16 + 4 * (j - 8), 16 + 2 * (j - 8))
                if j < 8:
                    for b in range(2):
                        u = 2 * j + b
                        turn(n0 + b, [u])
                        if u + 2 < 32:
                            scores(u + 2)
                    before = modulation(ada[:2], conds, before, flush=False)
                    del ada[:2]
                    if j % 2:
                        begin(("oa", j // 2))
                        pe.wait_ge(pt_ready, n0 + 2)
                        for a in range(2):
                            for kt in range(KEY_TILES):
                                ins = nc.tensor.matmul(
                                    half(("oa", j // 2), 0)[a * HD:a * HD + HD],
                                    v_all[:, kt, a * HD:a * HD + HD],
                                    p_t[:, a, kt * T:kt * T + T], start=(kt == 0), stop=(kt == KEY_TILES - 1))
                        end(ins)
                else:
                    for b in range(2):
                        turn(n0 + b, [u0 + 2 * b, u0 + 2 * b + 1])
                        for c in range(2):
                            if u0 + 2 * b + c + 2 < 32:
                                scores(u0 + 2 * b + c + 2)
                    before = modulation(ada[:1], conds, before, flush=False)
                    del ada[:1]
                    begin(("ob", j - 8))
                    pe.wait_ge(pt_ready, n0 + 2)
                    for kt in range(KEY_TILES):
                        ins = nc.tensor.matmul(half(("ob", j - 8), 0),
                                               v_all[:, kt, P * (j - 7):P * (j - 7) + P],
                                               p_t[:, j % 2, kt * T:kt * T + T],
                                               start=(kt == 0), stop=(kt == KEY_TILES - 1))
                    end(ins)
            modulation_cols(before)
            wo = [slab(("wo0", "wo1")[n]) for n in range(2)]

            def wo_tile(n, m, k0, k1):
                key = (("wo0", "wo1")[n], m // 2)
                if k0 == 0 and m % 2 == 0:
                    begin(key)
                for k in range(k0, k1):
                    ins = nc.tensor.matmul(half(key, m % 2), wo[n][:, k, m * P:m * P + P], mix[:, k, :],
                                           start=(k == 0), stop=(k == KD - 1))
                if k1 == KD and m % 2:
                    end(ins)

            arrived("wo0")
            for i in range(4):
                copied(pe, ("oa", i))
            for m in (0, 2):
                wo_tile(0, m, 0, 4)
            for i in range(2):
                pe.wait_ge(qk_square, 3 + i)
                nc.tensor.matmul(psum[:, 4 + i, :], con("ones"), flat(sq[:, 2 * i:2 * i + 2, :]),
                                 start=True, stop=True).then_inc(onorm_ready, 1)
            arrived("wo1")
            for m in (0, 2):
                wo_tile(1, m, 0, 4)
            pe.wait_ge(mix_ready, 1)
            for n in range(2):
                for m in (0, 2):
                    wo_tile(n, m, 4, KD)
                    wo_tile(n, m + 1, 0, KD)

            norm(2)
            begin(("router", 0))
            pe.wait_ge(router_in, 16)
            for t in range(TT):
                for k in range(KD):
                    if t == 0:
                        pe.wait_ge(h_ready, H_BASE[2] + k + 1)
                    ins = nc.tensor.matmul(bank(("router", 0))[:, t * E:t * E + E],
                                           h_moe[:, k, t * P:t * P + P], w_rt[:, k, :],
                                           start=(k == 0), stop=(k == KD - 1))
            end(ins)
            for c in range(4):
                begin(("htok", c))
                for m in range(4):
                    k = 4 * (c % 2) + m
                    ins = nc.tensor.matmul(bank(("htok", c))[:, m * P:m * P + P],
                                           h_moe[:, k, (c // 2) * P:(c // 2) * P + P], con("ident"),
                                           start=True, stop=True)
                end(ins)
            begin(("pos", 0))
            pe.wait_ge(mask_ready, 1)
            b = bank(("pos", 0))
            nc.tensor.matmul(b[:, 0:E], con("before"), mask[:, 0, :], start=True, stop=True)
            nc.tensor.matmul(b[:, E:2 * E], con("ones"), mask[:, 0, :], start=True, stop=False)
            nc.tensor.matmul(b[:, E:2 * E], con("before"), mask[:, 1, :], start=False, stop=True)
            nc.tensor.matmul(b[:, 2 * E:3 * E], con("ones"), mask[:, 0, :], start=True, stop=False)
            end(nc.tensor.matmul(b[:, 2 * E:3 * E], con("ones"), mask[:, 1, :], start=False, stop=True))
            begin(("gates", 0))
            pe.wait_ge(mask_ready, 2)
            for t in range(TT):
                ins = nc.tensor.matmul(bank(("gates", 0))[0:E, t * P:t * P + P], gate[:, t, :],
                                       con("ident"), start=True, stop=True)
            end(ins)
            for c in range(4):
                begin(("bout", c))
                if c == 0:
                    pe.wait_ge(bout_in, 16)
                    copied(pe, ("gates", 0))
                for m in range(2):
                    k = 2 * c + m
                    ins = nc.tensor.matmul(half(("bout", c), m), b_out_sb[0:E, k * P:k * P + P],
                                           gates_t[0:E, :], start=True, stop=True)
                end(ins)
            for c in range(4):
                copied(pe, ("bout", c))

            def gather(s, n):
                width = CAP * s.halves
                pe.wait_ge(s.sel_ready, n)
                for c in range(2):
                    for m in range(4):
                        k = 4 * c + m
                        for t in range(TT):
                            ins = nc.tensor.matmul(psum[:, c, m * P:m * P + width],
                                                   h_tok[:, t, k * P:k * P + P], sel[:, t, 0:width],
                                                   start=(t == 0), stop=(t == TT - 1))
                    ins.then_inc(s.gather_ready, 1)

            def scatter(s, at, free_at):
                for c in range(4):
                    pe.wait_ge(s.x_free[c % 2], free_at + c // 2)
                    for m in range(2):
                        k = 2 * c + m
                        ins = nc.tensor.matmul(psum[:, 6 + c % 2, m * T:m * T + T],
                                               y_slot[:, k * P:k * P + P], g_slot,
                                               start=True, stop=True)
                    ins.then_inc(s.x_ready, 1)

            def experts(s, i, full, ring_slot):
                width = CAP * s.halves

                def product(p, act):
                    for e in range(s.halves):
                        full(s.halves * p + e)
                    for k in range(KD):
                        for e in range(s.halves):
                            w = in_ring(ring_slot(s.halves * p + e), source("wo0"))
                            at = CAP * (e if s.halves == 2 else k % 2)
                            ins = nc.tensor.matmul(psum[at:at + CAP, p, :], act[:, k, CAP * e:CAP * e + CAP],
                                                   w[:, k, :], start=(k < 3 - s.halves),
                                                   stop=(k >= KD - 3 + s.halves))
                    ins.then_inc(s.product_ready, 1)

                def turn_h(c):
                    pe.wait_ge(s.h_copied, i * 4 + (c + 1))
                    pe.wait_ge(s.x_free[c % 2], i * 4 + (c // 2 + 1))
                    for m in range(4):
                        ins = nc.tensor.matmul(psum[:, 6 + c % 2, m * P:m * P + width],
                                               h_cat[:, c, m * P:m * P + P],
                                               con("ident" if s.halves == 2 else "fold"), start=True, stop=True)
                    ins.then_inc(s.x_ready, 1)

                pe.wait_ge(s.x_copied, i * 2 + 2)
                product(0, x_e)
                product(1, x_e)
                turn_h(0)
                product(2, x_e)
                turn_h(1)
                product(3, x_e)
                turn_h(2)
                turn_h(3)
                gather(s, i + 2)
                pe.wait_ge(s.y_copied, i * 2 + 2)
                scatter(s, 4, i * 4 + 3)
                for t in range(TT):
                    ins = nc.tensor.matmul(psum[:, 2, t * P:t * P + P], gsel[:, t, :],
                                           con("ident"), start=True, stop=True)
                ins.then_inc(s.gates_turned, 1)
                pe.wait_ge(s.act_ready, i + 1)
                product(4, lin)
                pe.wait_ge(s.gates_copied, i + 1)
                product(5, lin)

            def last_scatter(s, n):
                pe.wait_ge(s.y_copied, n * 2 + 2)
                scatter(s, 0, n * 4 + 1)

            gather(moe, 1)
            with pe.Fori(0, PAIRS) as i:
                def full(j):
                    n = SLABS_1 + j
                    pe.wait_ge(ring_full[n % RING], i * 32 + 16 * (n // RING + 1))
                experts(moe, i, full, lambda j: (SLABS_1 + j) % RING)
            last_scatter(moe, PAIRS)
            pe.wait_ge(over_ready, 1)
            n_jobs = pe.value_load(jobs[0:1, MAX_JOBS + 2:MAX_JOBS + 3], min_val=0, max_val=MAX_JOBS)
            with pe.If(n_jobs > 0):
                gather(again, 1)
                with pe.Fori(0, n_jobs) as i:
                    experts(again, i, lambda j: pe.wait_ge(again_full[j], i * 16 + 16), lambda j: j)
                last_scatter(again, n_jobs)
                pe.wait_ge(again.done, 1)

            norm(3)
            norm(4)
            for s in range(2):
                features(("rq", s), lambda k: h2[:, k, :], 2, first=h_tiles(4) if s == 0 else None)
            for s in range(2):
                features(("rk", s), lambda k: h2[:, k, :], 2)
            for s in range(4):
                arrived(("rv", s))
                tokens(("rv", s), lambda k, t: h2[:, k, t * P:t * P + P], TT, BANK)
            for s in range(4):
                features(("rg", s), lambda k: h2[:, k, :], 2)
            pe.wait_ge(ret_qk, 8)
            before = None
            for step in RET_STEPS:
                kind, h = step[0], step[1]
                if kind == "ada2":
                    before = modulation([step], conds, before, flush=False)
                    continue
                begin(step)
                if kind == "rs":
                    for m in range(TT):
                        for j in range(2):
                            ins = nc.tensor.matmul(half(step, m), rk[:, 2 * h + j, m * P:m * P + P],
                                                   rq[:, 2 * h + j, :], start=(j == 0), stop=(j == 1))
                elif kind == "ro":
                    c = step[2]
                    if c == 0:
                        pe.wait_ge(ret_s, h + 1)
                        if h == 0:
                            for s in range(4):
                                for t in range(TT):
                                    copied(pe, (("rv", s), t))
                    for m in range(2):
                        for t in range(TT):
                            at = h * 512 + (2 * c + m) * P
                            ins = nc.tensor.matmul(half(step, m), rv[:, t, at:at + P],
                                                   rs[:, t * T:t * T + T], start=(t == 0), stop=(t == 1))
                elif kind == "rmean":
                    copied(pe, ("ro", h, 0))
                    copied(pe, ("ro", h, 1))
                    for k in range(4):
                        ins = nc.tensor.matmul(half(step, 0), con("ones"), ro[:, k, :],
                                               start=(k == 0), stop=(k == 3))
                else:
                    pe.wait_ge(ret_sq, h + 1)
                    for k in range(4):
                        ins = nc.tensor.matmul(half(step, 0), con("ones"), sq[:, k, :],
                                               start=(k == 0), stop=(k == 3))
                end(ins)
            modulation_cols(before)
            pe.wait_ge(ret_done, RET_HEADS)
            for s in range(4):
                features(("rout", s), lambda k: rg[:, k, :], 2, k_tiles=16, m_tiles=2)

            def ffn(layer):
                norm(5 + 2 * layer)
                for s in range(11):
                    features(("up", layer, s), lambda k: h2[:, k, :], 2,
                             first=h_tiles(5 + 2 * layer) if s == 0 else None)
                for s in range(8):
                    features(("down", layer, s), lambda k: val[:, k, :], 1, k_tiles=KF, m_tiles=1,
                             first=(lambda k: pe.wait_ge(act_ready, 11 * layer + k // 2 + 1)) if s == 0 else None)

            ffn(0)
            norm(6)
            for s in range(2):
                features(("s5in", s), lambda k: h2[:, k, :], 2, first=h_tiles(6) if s == 0 else None)
            pe.wait_ge(s5_bc, 1)
            for c in range(2):
                for s in range(2):
                    copied(pe, (("s5in", s), c))

            def state_inputs(u):
                j, q = divmod(u, 4)
                begin(("bu", u))
                for c in range(2):
                    ins = nc.tensor.matmul(half(("bu", u), c), b_bd[32 * q:32 * q + 32, c, j, :],
                                           u5[32 * q:32 * q + 32, j, :], start=True, stop=True)
                end(ins)

            for u in range(3):
                state_inputs(u)
            for u in range(S5_PAIRS):
                if u + 3 < S5_PAIRS:
                    state_inputs(u + 3)
                j, q = divmod(u, 4)
                if q == 0 and j >= 2:
                    pe.wait_ge(s5_y_read, j - 1)
                pe.wait_ge(s5_state, u + 1)
                wc, ws = two(z_cos[u % 2]), two(z_sin[u % 2])
                terms = ((c_bd[:, 0, u, :], wc[:, 0, :]), (c_bd[:, 1, u, :], wc[:, 1, :]),
                         (c_bd[:, 1, u, :], ws[:, 0, :]), (c_neg[:, u, :], ws[:, 1, :]))
                for n, (mat, z) in enumerate(terms):
                    ins = nc.tensor.matmul(psum[32 * q:32 * q + 32, 4 + j % 2, 0:T], mat, z,
                                           start=(n == 0), stop=(n == 3))
                ins.then_inc(s5_used, 1)
            pe.wait_ge(s5_y, 8)
            for s in range(4):
                features(("glu", s), lambda k: y5[:, k, :], 2)
            ffn(1)
            norm(8)

        @block.scalar
        def _(act):
            own = Steps(act, act_step)

            def norm(i):
                src = NORMS[i][0]
                if i == 0:
                    act.wait_ge(ctx_in, 16)
                elif i == 1:
                    act.wait_ge(x_in, 16)
                    read_ready(act, ("norm", 0))
                elif i == 3:
                    act.wait_ge(x_ready, X_READY[i])
                elif i == 4:
                    act.wait_ge(act_g, KD)
                if i < 2:
                    nc.scalar.activation(sq[:], src[:], ACT.Square).then_inc(squares_ready, 1)
                    return
                for n in range(4):
                    for key in NORM_AFTER[i][n] if i in NORM_AFTER else []:
                        copied(act, key)
                    nc.scalar.activation(sq[:, 2 * n:2 * n + 2, :], src[:, 2 * n:2 * n + 2, :], ACT.Square
                                         ).then_inc(squares_ready, 1)
                nc.scalar.activation(tiny[:, 538:539], con("eps"), ACT.Ln)

            def guesses(pairs, n, signal):
                for out, src in pairs:
                    own.mark(nc.scalar.activation(out, src, ACT.Ln, scale=1.0 / n, bias=con("eps")))
                act.wait_ge(act_step, own.n)
                for out, _ in pairs:
                    nc.scalar.activation(out, out, ACT.Exp, scale=-0.5).then_inc(signal, 1)

            def guess(key, out, width, n, signal):
                read_ready(act, key)
                guesses([(out, bank(key)[:, 0:width])], n, signal)

            def apply(i):
                guess(("norm", i), rstd[:, 0, :], T, D, guess_ready)
                scale_and_shift(i)

            def scale_and_shift(i):
                _, out, row, shift = NORMS[i]
                if row is None:
                    g = sml(G_ONLY[i])
                    for k in range(KD):
                        act.wait_ge(normed_ready, 4 * i + k // 2 + 1)
                        nc.scalar.activation(out[:, k, :], out[:, k, :], ACT.Copy, scale=g[:, k:k + 1]
                                             ).then_inc(act_g, 1)
                    return
                act.wait_ge(affine_ready, AFFINE[i])
                for k in range(KD):
                    act.wait_ge(normed_ready, 4 * i + k // 2 + 1)
                    nc.scalar.activation(out[:, k, :], out[:, k, :], ACT.Identity,
                                         scale=aff[:, row, k:k + 1], bias=shift[:, k:k + 1]
                                         ).then_inc(h_ready, 1)

            def copy_rows(key):
                n = MOD_NUMBER[key]
                if n >= 2:
                    read_ready(act, ("cols", MOD_KEYS[n - 2]))
                read_ready(act, (key, 0))
                read_done(nc.scalar.activation(rows_of(key), bank((key, 0)), ACT.Copy), (key, 0))

            act.wait_ge(small_in, 16)
            for n, name in enumerate(("cond", "cond2")):
                w = SMALL[name][1]
                ins = nc.scalar.activation(tiny[:, 500 + 16 * n:500 + 16 * n + w], sml(name), ACT.Tanh, scale=0.5)
                ins.then_inc(cond_tanh, 1)
            act.wait_ge(const_in, 16)
            norm(0)
            guess(("norm", 0), rstd[:, 0, :], T, D, guess_ready)
            norm(1)
            act.wait_ge(normed_ready, 4)
            guess(("norm", 1), rstd[:, 0, :], T, D, guess_ready)
            for s in range(4):
                copy_rows(("ada", s))
            scale_and_shift(0)
            scale_and_shift(1)
            act.wait_ge(lam_sum, 1)
            nc.scalar.activation(lam[:, 2:4], lam[:, 0:2], ACT.Exp).then_inc(lam_exp, 1)

            def copy(key, out, width=BANK, scale=1.0):
                read_ready(act, key)
                src = bank(key)[:, 0:width]
                if len(out.shape) == 3:
                    src = src.rearrange("p (a b) -> p a b", b=out.shape[2])
                read_done(nc.scalar.activation(out, src, ACT.Copy, scale=scale), key)

            copy(("qa", 0), q_all[:, 0:2, :])
            copy(("qa", 1), q_all[:, 2:4, :])
            copy(("kva", 0), k_all[:, 0, :])
            for key in (("qa", 0), ("qa", 1), ("kva", 0)):
                copied(act, key)
            nc.scalar.activation(sq[:, 0:4, :], q_all[:, 0:4, :], ACT.Square).then_inc(qk_square, 1)
            nc.scalar.activation(flat(sq[:, 4:6, :]), k_all[:, 0, :], ACT.Square).then_inc(qk_square, 1)
            copy(("kva", 1), v_all[:, :, 0:P])
            copy(("qb", 0), q_all[:, 4:6, :])
            copy(("qb", 1), q_all[:, 6:8, :])
            for i in range(4):
                copy(("kb", i), k_all[:, 1 + i, :])
            read_ready(act, ("qknorm", 2))
            guesses([(y, bank(("qknorm", i))) for i, y in enumerate(QK_RSTD)], HD, qk_guess)
            for i in range(4):
                copy(("vb", i), v_all[:, i, P:P + BANK])

            def probabilities(u):
                act.wait_ge(max_ready, u + 1)
                if u >= 4:
                    act.wait_ge(pt_written, TURN_OF[u - 4] + 1)
                nc.scalar.activation(probs[:, u % 4, :], psum[:, 4 + u % 2, :], ACT.Exp,
                                     bias=soft[:, u, 0:1], scale=ATT_SCALE, accum_out=soft[:, u, 1:2]
                                     ).then_inc(probs_ready, 1)

            def copy_turned(n):
                act.wait_ge(pt_written, n + 1)
                if n < 16:
                    pair, b = n // 2, n % 2
                    slot = pair % 2
                    if n >= 4 and b == 0 and slot == 0:
                        read_ready(act, ("oa", pair // 2 - 1))
                else:
                    pair, b = n // 2, n % 2
                    slot = pair % 2
                    if b == 0:
                        if pair - 8 >= 2:
                            read_ready(act, ("ob", pair - 8 - 2))
                        else:
                            read_ready(act, ("oa", 3))
                dst = p_t[:, slot, :].rearrange("p (k t) -> p k t", t=T)[:, :, b * P:b * P + P]
                src = psum[:, 6 + n % 2, :].rearrange("p (k t) -> p k t", t=P)
                nc.scalar.activation(dst, src, ACT.Copy).then_inc(pt_ready, 1)

            probabilities(0)
            probabilities(1)
            ada = MOD_KEYS[4:24]
            for n in range(24):
                copy_turned(n)
                for u in NEW_MAPS[n]:
                    probabilities(u)
                if n % 2:
                    for key in ada[:2 if n < 16 else 1]:
                        copy_rows(key)
                    del ada[:2 if n < 16 else 1]
                if n < 16 and n % 4 == 3:
                    copy(("oa", n // 4), mix[:, n // 4, :], T)
                if n >= 16 and n % 2:
                    copy(("ob", (n - 16) // 2), mix[:, 4 + (n - 16) // 2, :], T)
            for i in range(2):
                for j in range(2):
                    copied(act, ("ob", 2 * i + j))
                nc.scalar.activation(sq[:, 2 * i:2 * i + 2, :], mix[:, 4 + 2 * i:6 + 2 * i, :], ACT.Square
                                     ).then_inc(qk_square, 1)
            act.wait_ge(onorm_ready, 2)
            guesses([(y, psum[:, 4 + i, :]) for i, y in enumerate(QK_RSTD[:2])], P, qk_guess)

            norm(2)
            apply(2)
            for c in range(4):
                copy(("htok", c), h_tok[:, c // 2, BANK * (c % 2):BANK * (c % 2) + BANK])
            act.wait_ge(top_ready, 1)
            nc.scalar.activation(top_e[:, :, 0:TOP_K], top_e[:, :, 0:TOP_K], ACT.Exp).then_inc(top_exp, 1)
            read_ready(act, ("gates", 0))
            read_done(nc.scalar.activation(gates_t[0:E, :], bank(("gates", 0))[0:E, 0:T], ACT.Copy), ("gates", 0))

            def copy_bank(s, out, src, signal):
                nc.scalar.activation(out, src, ACT.Copy).then_inc(signal, 1)

            def gathered(s, base):
                width = CAP * s.halves
                for c in range(2):
                    act.wait_ge(s.gather_ready, base + (c + 1))
                    copy_bank(s, x_e[:, 4 * c:4 * c + 4, 0:width],
                              psum[:, c, :].rearrange("p (a b) -> p a b", b=P)[:, :, 0:width], s.x_copied)

            def experts(s, i):
                width = CAP * s.halves
                for c in range(4):
                    act.wait_ge(s.product_ready, i * 6 + (s.base + c + 1))
                    copy_bank(s, h_cat[:, c, :], psum[:, c, :], s.h_copied)
                act.wait_ge(s.glu_ready, i + 1)
                nc.scalar.activation(tanh_e[:, :, 0:width], glu[:, :, 0:width], ACT.Tanh, scale=ALPHA / 2
                                     ).then_inc(s.tanh_ready, 1)
                gathered(s, i * 2 + 2)
                act.wait_ge(s.gates_turned, i + 1)
                copy_bank(s, g_slot, psum[:, 2, 0:T], s.gates_copied)
                for c in range(2):
                    act.wait_ge(s.product_ready, i * 6 + (s.base + 4 + c + 1))
                    copy_bank(s, y_slot[:, BANK * c:BANK * c + BANK], psum[:, 4 + c, :], s.y_copied)

            gathered(moe, 0)
            with act.Fori(0, PAIRS) as i:
                experts(moe, i)
            act.wait_ge(over_ready, 1)
            n_jobs = act.value_load(jobs[0:1, MAX_JOBS + 2:MAX_JOBS + 3], min_val=0, max_val=MAX_JOBS)
            with act.If(n_jobs > 0):
                gathered(again, 0)
                with act.Fori(0, n_jobs) as i:
                    experts(again, i)
                act.wait_ge(again.done, 1)
            act.wait_ge(moe.x_copied, 2 * PAIRS + 2)

            norm(3)
            apply(3)
            norm(4)
            apply(4)
            act.wait_ge(angle_ready, 1)
            for n, a in enumerate((cos2, sin2)):
                nc.scalar.activation(a, rot[:, 0, n * T:n * T + T], ACT.Sin).then_inc(sin_ready, 1)
            for s in range(4):
                for t in range(TT):
                    copy((("rv", s), t), rv[:, t, BANK * s:BANK * s + BANK])
                if s == 0:
                    act.wait_ge(s5_dt, 1)
                    nc.scalar.activation(s5[:, 0, :], sml("log_dt"), ACT.Exp).then_inc(s5_exp, 1)
                elif s == 1:
                    act.wait_ge(s5_dt, 2)
                    nc.scalar.activation(s5[:, 1, :], s5[:, 1, :], ACT.Exp).then_inc(s5_exp, 1)
                elif s == 2:
                    act.wait_ge(s5_angle, 1)
                    for n in range(2):
                        nc.scalar.activation(s5[:, 4 + n, :], s5[:, 2 + n, :], ACT.Sin).then_inc(s5_exp, 1)
            for s in range(4):
                for c in range(2):
                    key = (("rg", s), c)
                    read_ready(act, key)
                    n = 2 * s + c
                    if n == 0:
                        act.wait_ge(ret_qk, 8)
                    if n >= 2:
                        act.wait_ge(ret_gate, n - 1)
                    nc.scalar.activation(rot[:, n % 2, :], bank(key), ACT.Tanh, scale=0.5).then_inc(ret_tanh, 1)
            act.wait_ge(ret_gate, 8)
            for step in RET_STEPS:
                kind, h = step[0], step[1]
                if kind == "ada2":
                    copy_rows(step)
                elif kind == "ro":
                    c = step[2]
                    if c == 0 and h:
                        act.wait_ge(ret_done, h)
                    copy(step, ro[:, 2 * c:2 * c + 2, :])
                elif kind == "rmean":
                    act.wait_ge(ret_o, h + 1)
                    if h:
                        read_ready(act, ("rvar", h - 1))
                    nc.scalar.activation(sq[:, 0:4, :], ro[:], ACT.Square).then_inc(ret_sq, 1)
                elif kind == "rvar":
                    guess(step, rstd[:, 0, :], T, 512, ret_guess)

            def ffn(layer):
                norm(5 + 2 * layer)
                apply(5 + 2 * layer)
                w = sml("conv_w").rearrange("p (l c k) -> p l c k", l=2, c=3)[:, layer]
                b = sml("conv_b").rearrange("p (l k) -> p l k", l=2)[:, layer]
                for s in range(11):
                    for c in range(2):
                        n = 2 * s + c
                        key = (("up", layer, s), c)
                        if n < 11:
                            copy(key, val[:, 2 * n:2 * n + 2, :])
                            continue
                        m = n - 11
                        read_ready(act, key)
                        if m >= 2:
                            act.wait_ge(act_ready, 11 * layer + m - 1)
                        for a in range(2):
                            k = 2 * m + a
                            ins = nc.scalar.activation(conv[:, m % 2, a * T:a * T + T], half(key, a), ACT.Identity,
                                                       scale=w[:, 2, k:k + 1], bias=b[:, k:k + 1])
                            ins.then_inc(conv_start, 1)
                        if m >= 1:
                            tanh(layer, m - 1)
                tanh(layer, 10)

            def tanh(layer, m):
                act.wait_ge(conv_ready, 11 * layer + m + 1)
                nc.scalar.activation(conv_t[:, m % 2, :], conv[:, m % 2, :], ACT.Tanh, scale=0.5
                                     ).then_inc(conv_tanh, 1)

            ffn(0)
            norm(6)
            apply(6)
            for s in range(2):
                for c in range(2):
                    copy((("s5in", s), c), u5[:, 4 * s + 2 * c:4 * s + 2 * c + 2, :])
            for j in range(8):
                act.wait_ge(s5_y_read, j + 1)
                nc.scalar.activation(gl[:, j, :], y5[:, j, :], ACT.Square, scale=float(np.sqrt(0.044715))
                                     ).then_inc(s5_sq, 1)
                act.wait_ge(s5_gelu_in, j + 1)
                nc.scalar.activation(gl[:, j, :], gl[:, j, :], ACT.Tanh, scale=GELU_C).then_inc(s5_gelu_t, 1)
            act.wait_ge(s5_y, 8)
            for s in range(2):
                for c in range(2):
                    copy((("glu", s), c), gl[:, 4 * s + 2 * c:4 * s + 2 * c + 2, :], scale=0.25)
            for s in range(2, 4):
                for c in range(2):
                    n = 2 * (s - 2) + c
                    key = (("glu", s), c)
                    read_ready(act, key)
                    nc.scalar.activation(u5[:, 2 * n:2 * n + 2, :], two(bank(key)), ACT.Tanh, scale=0.25)\
                        .then_inc(glu_tanh, 1)
            ffn(1)
            norm(8)
            apply(8)

        @block.vector
        def _(dve):
            own = Steps(dve, dve_step)
            V = nc.vector

            def refine(src, y, v, t, n, guess_sem, count):
                dve.wait_ge(guess_sem, count)
                own.link(V.tensor_scalar(v, src, -0.5 / n, -0.5 * EPS, ALU.mult, ALU.add))
                own.link(V.tensor_tensor(t, y, y, ALU.mult))
                own.link(V.tensor_tensor(t, t, v, ALU.mult))
                ins = V.scalar_tensor_tensor(out=y, in0=t, scalar=1.5, in1=y, op0=ALU.add, op1=ALU.mult)
                return ins

            def norm(i):
                src, out, row, _ = NORMS[i]
                key = ("norm", i)
                read_ready(dve, key)
                read_done(refine(half(key, 0), rstd[:, 0, :], rstd[:, 1, :], rstd[:, 2, :], D, guess_ready, i + 1), key)
                copied(dve, key)
                for n in range(4):
                    V.tensor_tensor(out[:, 2 * n:2 * n + 2, :], src[:, 2 * n:2 * n + 2, :],
                                    over_tiles(rstd[:, 0, :], 2), ALU.mult).then_inc(normed_ready, 1)

            own.mark(V.memset(cond32[:], 0.0))
            own.link(V.memset(cond32_2[:], 0.0))
            for n, (name, dst, w) in enumerate((("cond", cond32, 2), ("cond2", cond32_2, 1))):
                dve.wait_ge(cond_tanh, n + 1)
                t = tiny[:, 500 + 16 * n:500 + 16 * n + KD * w]
                own.link(V.scalar_tensor_tensor(out=t, in0=t, scalar=1.0, in1=sml(name), op0=ALU.add, op1=ALU.mult))
                V.tensor_scalar(dst[:, :, 0:w], t.rearrange("p (k c) -> p k c", c=w), 0.5, None, ALU.mult
                                ).then_inc(cond_ready, 1)
            dl = sml("dlam").rearrange("p (a b) -> p a b", b=HD)
            for j in range(2):
                own.link(V.tensor_tensor(lam_prod[:, j, :], dl[:, 2 * j, :], dl[:, 2 * j + 1, :], ALU.mult))
            V.tensor_reduce(lam[:, 0:2], lam_prod, AX_X, ALU.add).then_inc(lam_sum, 1)

            def modulation(key):
                s = key[-1]
                read_ready(dve, ("cols", key))
                src = bank(("cols", key)).rearrange("p (m c) -> p m c", c=P)
                if key[0] == "ada":
                    b = sml("b_ada")[:, 4 * s:4 * s + 4].unsqueeze(2).to_broadcast([P, 4, 2])
                    ins = V.tensor_tensor(mod[:, 4 * s:4 * s + 4, :], src[:, :, 0:2], b, ALU.add)
                else:
                    at = 48 * key[1] + 4 * s
                    ins = V.tensor_tensor(mod2[:, key[1], 4 * s:4 * s + 4], src[:, :, 0],
                                          sml("b_ada2")[:, at:at + 4], ALU.add)
                read_done(ins, ("cols", key))

            dve.wait_ge(const_in, 16)
            norm(0)
            norm(1)
            for s in range(4):
                modulation(("ada", s))
            for s in range(4):
                copied(dve, ("cols", ("ada", s)))
            dve.wait_ge(dve_step, own.n)
            own.mark(V.scalar_tensor_tensor(out=aff[:, 0, :], in0=mod[:, 8:16, 1], scalar=1.0, in1=sml("g_attn"),
                                            op0=ALU.add, op1=ALU.mult))
            V.scalar_tensor_tensor(out=aff[:, 1, :], in0=mod[:, 8:16, 0], scalar=1.0, in1=sml("g_attn"),
                                   op0=ALU.add, op1=ALU.mult).then_inc(affine_ready, 1)
            dve.wait_ge(lam_exp, 1)
            own.link(V.tensor_tensor(lam[:, 4:5], lam[:, 3:4], lam[:, 2:3], ALU.subtract))
            own.link(V.tensor_scalar(lam[:, 5:6], lam[:, 4:5], -LAMBDA_INIT, None, ALU.add))

            for i, y in enumerate(QK_RSTD):
                key = ("qknorm", i)
                read_ready(dve, key)
                read_done(refine(bank(key), y, rope_t[:, 0, :], rope_t[:, 1, :], HD, qk_guess, i + 1), key)
                copied(dve, key)
                src = flat(q_all[:, 2 * i:2 * i + 2, :]) if i < 2 else k_all[:, 0, :]
                V.scalar_tensor_tensor(out=src, in0=src, scalar=sml("g_q" if i < 2 else "g_k"), in1=y,
                                       op0=ALU.mult, op1=ALU.mult).then_inc(q_normed, 1)
            dve.wait_ge(q_normed, 3)
            for n_done, i in enumerate(i for after in ROPES_AFTER for i in after):
                key = ("rope", i)
                read_ready(dve, key)
                if i < 4:
                    dst, ps = q_all[:, 2 * i:2 * i + 2, :], two(bank(key))
                    n = 2
                else:
                    dst, ps = k_all[:, i - 4:i - 3, T:N_KEYS], bank(key)[:, 0:T].unsqueeze(1)
                    n = 1
                t = rope_t[:, 0, 0:n * T].rearrange("p (a b) -> p a b", b=T)
                own.mark(V.tensor_tensor(dst, dst, over_tiles(con("rope_cos"), n), ALU.mult))
                ins = V.tensor_tensor(t, ps, over_tiles(con("rope_sin"), n), ALU.mult)
                read_done(ins, key)
                dve.wait_ge(dve_step, own.n)
                copied(dve, key)
                V.tensor_tensor(dst, dst, t, ALU.add).then_inc(q_ready, 1)
                dve.wait_ge(q_ready, n_done + 1)

            def maximum(u):
                dve.wait_ge(scores_ready, u + 1)
                own.link(V.tensor_reduce(soft[:, u, 2:3], psum[:, 4 + u % 2, :], AX_X, ALU.max))
                V.tensor_scalar(soft[:, u, 0:1], soft[:, u, 2:3], -ATT_SCALE, None, ALU.mult).then_inc(max_ready, 1)

            def factor(u):
                dve.wait_ge(probs_ready, u + 1)
                if u >= 4:
                    dve.wait_ge(pt_written, TURN_OF[u - 4] + 1)
                own.link(V.reciprocal(soft[:, u, 3:4], soft[:, u, 1:2]))
                if u >= 16 and u % 2:
                    own.link(V.tensor_tensor(soft[:, u, 3:4], soft[:, u, 3:4], lam[:, 5:6], ALU.mult))
                V.tensor_scalar(diag[:, u % 4, :], con("ident"), soft[:, u, 3:4], None, ALU.mult
                                ).then_inc(diag_ready, 1)

            ada = MOD_KEYS[4:24]

            maximum(0)
            maximum(1)
            for j in range(12):
                maps = [[2 * j], [2 * j + 1]] if j < 8 else [[4 * j - 16, 4 * j - 15], [4 * j - 14, 4 * j - 13]]
                for turned in maps:
                    for u in turned:
                        factor(u)
                    for u in turned:
                        if u + 2 < 32:
                            maximum(u + 2)
                n = (2 if j < 8 else 1) - (j == 0)
                for key in ada[:n]:
                    modulation(key)
                del ada[:n]
            modulation(ada.pop(0))
            assert not ada
            for key in MOD_KEYS[4:24]:
                copied(dve, ("cols", key))
            V.scalar_tensor_tensor(out=aff[:, 2, :], in0=mod[:, 32:40, 0], scalar=1.0, in1=sml("g_ffn"),
                                   op0=ALU.add, op1=ALU.mult).then_inc(affine_ready, 1)
            own.mark(V.tensor_scalar(aff[:, 3, :], mod2[:, 0, 8:16], 1.0, None, ALU.add))
            V.tensor_scalar(aff[:, 4, :], mod2[:, 0, 32:40], 1.0, None, ALU.add).then_inc(affine_ready, 1)
            for i in range(2):
                y = QK_RSTD[i]
                dve.wait_ge(onorm_ready, i + 1)
                own.link(refine(psum[:, 4 + i, :], y, rope_t[:, 0, :], rope_t[:, 1, :], P, qk_guess, 4 + i))
                o = mix[:, 4 + 2 * i:6 + 2 * i, :]
                own.link(V.tensor_tensor(o, o, two(y), ALU.mult))
                ins = V.tensor_scalar(o, o, sml("g_sub"), 1.0 - LAMBDA_INIT, ALU.mult, ALU.mult)
                if i == 0:
                    own.link(ins)
                else:
                    ins.then_inc(mix_ready, 1)
                    dve.wait_ge(mix_ready, 1)

            def add_to_x(key, m0, gate_col, n=2, last=None):
                read_ready(dve, key)
                for m in range(n):
                    ins = V.scalar_tensor_tensor(out=x[:, m0 + m, :], in0=half(key, m),
                                                 scalar=gate_col[:, m0 + m:m0 + m + 1], in1=x[:, m0 + m, :],
                                                 op0=ALU.mult, op1=ALU.add)
                    if m < n - 1:
                        own.mark(ins)
                read_done(ins, key)

            def x_complete(keys):
                for key in keys:
                    copied(dve, key)
                V.memset(tiny[:, 499:500], 0.0).then_inc(x_ready, 1)

            keys = [("wo0", 0), ("wo0", 1), ("wo1", 0), ("wo1", 1)]
            for n, key in enumerate(keys):
                add_to_x(key, 2 * n, mod[:, 16:24, 0])
            dve.wait_ge(dve_step, own.n)
            x_complete(keys)
            norm(2)

            key = ("router", 0)
            read_ready(dve, key)
            read_done(V.tensor_tensor(logits, bank(key)[:, 0:TT * E].rearrange("p (a b) -> p a b", b=E),
                                      over_tiles(sml("b_router"), TT), ALU.add), key)
            copied(dve, key)
            for t in range(TT):
                own.link(V.max(top[:, t, :], logits[:, t, :]))
                own.link(V.max_index(top_i[:, t, :].bitcast(U32), top[:, t, :], logits[:, t, :]))
            own.link(V.tensor_copy(top_f, top_i.bitcast(U32)))
            V.tensor_tensor(top_e[:, :, 0:TOP_K], top[:, :, 0:TOP_K],
                            top[:, :, 0:1].to_broadcast([P, TT, TOP_K]), ALU.subtract).then_inc(top_ready, 1)
            shape = [P, TT, TOP_K, E]

            def of_choices(a):
                return a[:, :, 0:TOP_K].unsqueeze(3).to_broadcast(shape)

            def sum_choices(out, a):
                return V.tensor_reduce(out, a.rearrange("p t r e -> p t e r"), AX_X, ALU.add)

            own.link(V.tensor_tensor(onehot[0], con("experts").unsqueeze(1).unsqueeze(1).to_broadcast(shape),
                                     of_choices(top_f), ALU.is_equal))
            sum_choices(mask, onehot[0]).then_inc(mask_ready, 1)
            dve.wait_ge(top_exp, 1)
            own.link(V.tensor_reduce(gate_sum[:, 0:2], top_e[:, :, 0:TOP_K], AX_X, ALU.add))
            own.link(V.reciprocal(gate_sum[:, 2:4], gate_sum[:, 0:2]))
            own.link(V.tensor_tensor(top_e[:, :, 0:TOP_K], top_e[:, :, 0:TOP_K],
                                     gate_sum[:, 2:4].unsqueeze(2).to_broadcast([P, TT, TOP_K]), ALU.mult))
            own.link(V.tensor_tensor(onehot[1], onehot[0], of_choices(top_e), ALU.mult))
            sum_choices(gate, onehot[1]).then_inc(mask_ready, 1)
            key = ("pos", 0)
            read_ready(dve, key)
            dve.wait_ge(mask_ready, 2)
            b = bank(key)
            own.mark(V.tensor_copy(count, b[:, 2 * E:3 * E]))
            own.link(V.scalar_tensor_tensor(out=slot_of, in0=b[:, 0:2 * E].rearrange("p (a b) -> p a b", b=E),
                                            scalar=1.0, in1=mask, op0=ALU.add, op1=ALU.mult))
            ins = V.tensor_scalar(slot_of, slot_of, -1.0, None, ALU.add)
            read_done(ins, key)
            copied(dve, key)
            for c in range(4):
                key = ("bout", c)
                read_ready(dve, key)
                read_done(V.tensor_copy(y_moe[:, 2 * c:2 * c + 2, :], two(bank(key))), key)
            for c in range(4):
                copied(dve, ("bout", c))

            def one(e):
                return slice(e, e + 1) if isinstance(e, int) else bass.ds(e, 1)

            def block_slots(b):
                at = b * CAP
                return con("slots")[:, at:at + CAP] if isinstance(b, int) else con("slots")[:, bass.ds(at, CAP)]

            def select(s, experts_of, b):
                for h in range(s.halves):
                    for t in range(TT):
                        ins = V.tensor_scalar(sel[:, t, CAP * h:CAP * h + CAP], block_slots(b),
                                              slot_of[:, t, one(experts_of[h])], None, ALU.is_equal)
                ins.then_inc(s.sel_ready, 1)

            def add_scattered(s, base):
                for c in range(4):
                    dve.wait_ge(s.x_ready, base + (c + 1))
                    V.tensor_tensor(y_moe[:, 2 * c:2 * c + 2, :], y_moe[:, 2 * c:2 * c + 2, :],
                                    two(psum[:, 6 + c % 2, :]), ALU.add).then_inc(s.x_free[c % 2], 1)

            def experts(s, i, experts_of, b, next_experts, next_b):
                width = CAP * s.halves
                step = Steps(dve, s.step, i * STEPS_OF[s.halves])
                dve.wait_ge(s.product_ready, i * 6 + (s.base + 1))
                for h in range(2):
                    e = one(experts_of[h % s.halves])
                    for t in range(TT):
                        step.mark(V.tensor_scalar(gsel[:, t, CAP * h:CAP * h + CAP], block_slots(b),
                                                  slot_of[:, t, e], gate[:, t, e], ALU.is_equal, ALU.mult))
                for h in range(s.halves):
                    ins = V.tensor_copy(bias[:, h, :], sml("b_in").rearrange("p (e k) -> p e k", k=16)
                                        [:, one(experts_of[h]), :].rearrange("p a k -> p (a k)"))
                    step.mark(ins)
                dve.wait_ge(s.step, step.base + step.n)
                select(s, next_experts, next_b)
                for c in range(4):
                    dve.wait_ge(s.x_ready, i * 8 + (c + 1))
                    dst = (glu if c < 2 else lin)[:, 4 * (c % 2):4 * (c % 2) + 4, 0:width]
                    src = psum[:, 6 + c % 2, :].rearrange("p (a b) -> p a b", b=P)[:, :, 0:width]
                    bb = bias[:, 0:s.halves, 4 * c:4 * c + 4].rearrange("p e k -> p k e")
                    V.tensor_tensor(dst.rearrange("p k (e n) -> p k e n", n=CAP),
                                    src.rearrange("p k (e n) -> p k e n", n=CAP),
                                    bb.unsqueeze(3).to_broadcast([P, 4, s.halves, CAP]), ALU.add
                                    ).then_inc(s.x_free[c % 2], 1)
                    if c % 2 == 0:
                        continue
                    for bank_free in s.x_free:
                        dve.wait_ge(bank_free, i * 4 + (c // 2 + 2))
                    if c == 1:
                        V.tensor_scalar(glu[:, :, 0:width], glu[:, :, 0:width], LIMIT, None, ALU.min
                                        ).then_inc(s.glu_ready, 1)
                t_e, g_e, l_e = tanh_e[:, :, 0:width], glu[:, :, 0:width], lin[:, :, 0:width]
                step.link(V.tensor_scalar(l_e, l_e, LIMIT, -LIMIT, ALU.min, ALU.max))
                step.link(V.tensor_scalar(l_e, l_e, 0.5, 0.5, ALU.mult, ALU.add))
                dve.wait_ge(s.tanh_ready, i + 1)
                step.link(V.scalar_tensor_tensor(out=t_e, in0=t_e, scalar=1.0, in1=g_e, op0=ALU.add, op1=ALU.mult))
                V.tensor_tensor(l_e, l_e, t_e, ALU.mult).then_inc(s.act_ready, 1)
                add_scattered(s, i * 8 + 4)
                assert step.n == STEPS_OF[s.halves]

            def last_scattered(s, n):
                for c in range(2):
                    dve.wait_ge(s.x_free[c], n * 4 + 1)
                add_scattered(s, n * 8)
                for c in range(2):
                    dve.wait_ge(s.x_free[c], n * 4 + 3)

            STEPS_OF = {2: 9, 1: 8}

            def start(s):
                ins = V.memset(g_slot, 0.0)
                own.link(ins)
                for c in range(2):
                    dve.sem_inc(s.x_free[c], 1)
                if s.base:
                    dve.sem_inc(s.product_ready, s.base)
                for c in range(2):
                    dve.sem_inc(s.y_copied, 1)

            own.link(V.memset(y_slot, 0.0))
            start(moe)
            select(moe, (0, 1), 0)
            for b in range(1, BLOCKS):
                own.mark(V.tensor_scalar(flags[:, b - 1, :], count, float(CAP * b), None, ALU.is_gt))
            dve.wait_ge(dve_step, own.n)
            n_flags = (BLOCKS - 1) * E
            own.link(V.tensor_tensor_scan(out=cum, data0=con("ones")[:, 0:n_flags], data1=flat(flags), initial=0.0,
                                          op0=ALU.mult, op1=ALU.add))
            n_list = MAX_JOBS + 2
            cmp = flat(h_moe)[:, 0:n_list * n_flags].rearrange("p (a b) -> p a b", b=n_flags)
            own.link(V.tensor_tensor(cmp, over_tiles(cum, n_list),
                                     con("slots")[:, 0:n_list].unsqueeze(2).to_broadcast([P, n_list, n_flags]),
                                     ALU.is_le))
            own.mark(V.tensor_reduce(jobs_f[:, 0:n_list], cmp, AX_X, ALU.add))
            own.link(V.tensor_copy(jobs_f[:, n_list:n_list + 1], cum[:, n_flags - 1:n_flags]))
            V.tensor_copy(jobs, jobs_f).then_inc(over_ready, 1)
            with dve.Fori(0, PAIRS) as i:
                n = ((i + 1) % PAIRS) * 2
                experts(moe, i, (i * 2, i * 2 + 1), 0, (n, n + 1), 0)
            last_scattered(moe, PAIRS)
            dve.wait_ge(over_ready, 1)
            n_jobs = dve.value_load(jobs[0:1, MAX_JOBS + 2:MAX_JOBS + 3], min_val=0, max_val=MAX_JOBS)
            with dve.If(n_jobs > 0):
                def job_at(i):
                    job = dve.value_load(jobs[0:1, bass.ds(i, 1)], min_val=0, max_val=(BLOCKS - 1) * E)
                    return (job % E,), job // E + 1

                start(again)
                select(again, *job_at(0))
                with dve.Fori(0, n_jobs) as i:
                    experts(again, i, *job_at(i), *job_at(i + 1))
                last_scattered(again, n_jobs)
                V.memset(tiny[:, 498:499], 0.0).then_inc(again.done, 1)

            for k in range(KD):
                own.mark(V.scalar_tensor_tensor(out=x[:, k, :], in0=y_moe[:, k, :], scalar=mod[:, 40 + k, 0:1],
                                                in1=x[:, k, :], op0=ALU.mult, op1=ALU.add))
            dve.wait_ge(dve_step, own.n)
            V.memset(tiny[:, 499:500], 0.0).then_inc(x_ready, 1)

            norm(3)
            dve.wait_ge(act_g, KD)
            V.memset(tiny[:, 499:500], 0.0).then_inc(x_ready, 1)
            norm(4)

            def reduce_angle(a, n, sin_out, cos_out):
                own.link(V.tensor_scalar(n, a, float(1 / TWO_PI), ROUND, ALU.mult, ALU.add))
                own.link(V.tensor_scalar(n, n, ROUND, None, ALU.subtract))
                for part in (PI2_A, PI2_B, PI2_C):
                    own.link(V.scalar_tensor_tensor(out=a, in0=n, scalar=-part, in1=a, op0=ALU.mult, op1=ALU.add))
                own.link(V.tensor_scalar(sin_out, a, PI_IN, -PI_IN, ALU.min, ALU.max))
                own.link(V.tensor_scalar(n, sin_out, float(np.pi / 2), -TWO_PI, ALU.is_gt, ALU.mult))
                own.link(V.scalar_tensor_tensor(out=n, in0=n, scalar=float(np.pi / 2), in1=sin_out,
                                                op0=ALU.add, op1=ALU.add))
                return V.tensor_scalar(cos_out, n, PI_IN, -PI_IN, ALU.min, ALU.max)

            dve.wait_ge(pos_ready, 1)
            own.link(V.tensor_scalar(rk[:, 0, :], rk[:, 0, :], con("inv_freq"), None, ALU.mult))
            reduce_angle(rk[:, 0, :], rk[:, 1, :], rot[:, 0, T:2 * T], rot[:, 0, 0:T]).then_inc(angle_ready, 1)
            dve.wait_ge(sin_ready, 2)
            for n, (name, dst) in enumerate((("rq", rq), ("rk", rk))):
                for h in range(RET_HEADS):
                    key = ((name, h // 2), h % 2)
                    read_ready(dve, key)
                    a, b = two(rot[:, 0, :]), two(rot[:, 1, :])
                    own.mark(V.tensor_tensor(a, two(bank(key)), over_tiles(cos2, 2), ALU.mult))
                    read_done(V.tensor_tensor(b, two(bank(key)), over_tiles(sin2, 2), ALU.mult), key)
                    dve.wait_ge(dve_step, own.n)
                    copied(dve, key)
                    own.mark(V.tensor_tensor(dst[:, 2 * h, :], a[:, 0, :], b[:, 1, :], ALU.subtract))
                    V.tensor_tensor(dst[:, 2 * h + 1, :], a[:, 1, :], b[:, 0, :], ALU.add).then_inc(ret_qk, 1)
                    dve.wait_ge(dve_step, own.n)
                    dve.wait_ge(ret_qk, 4 * n + h + 1)
            row = lambda n: s5[:, n, :]
            re, im = sml("lam_re"), sml("lam_im")
            V.memset(tiny[:, 639:640], 0.0).then_inc(s5_dt, 1)
            dve.wait_ge(s5_exp, 1)
            own.link(V.tensor_tensor(row(10), im, row(0), ALU.mult))
            V.tensor_tensor(row(1), re, row(0), ALU.mult).then_inc(s5_dt, 1)
            reduce_angle(row(10), row(11), row(3), row(2)).then_inc(s5_angle, 1)
            dve.wait_ge(s5_exp, 4)
            own.mark(V.tensor_tensor(row(6), row(1), row(4), ALU.mult))
            own.link(V.tensor_tensor(row(7), row(1), row(5), ALU.mult))
            own.mark(V.tensor_scalar(row(10), row(6), -1.0, None, ALU.add))
            own.mark(V.tensor_tensor(row(11), re, re, ALU.mult))
            own.link(V.tensor_tensor(row(12), im, im, ALU.mult))
            own.link(V.tensor_tensor(row(11), row(11), row(12), ALU.add))
            own.link(V.reciprocal(row(11), row(11)))
            own.mark(V.tensor_tensor(row(12), row(10), re, ALU.mult))
            own.link(V.tensor_tensor(row(13), row(7), im, ALU.mult))
            own.link(V.tensor_tensor(row(12), row(12), row(13), ALU.add))
            own.link(V.tensor_tensor(row(8), row(12), row(11), ALU.mult))
            own.mark(V.tensor_tensor(row(12), row(7), re, ALU.mult))
            own.link(V.tensor_tensor(row(13), row(10), im, ALU.mult))
            own.link(V.tensor_tensor(row(12), row(12), row(13), ALU.subtract))
            own.link(V.tensor_tensor(row(9), row(12), row(11), ALU.mult))
            V.memset(tiny[:, 639:640], 0.0).then_inc(s5_ab, 1)
            for s in range(4):
                for c in range(2):
                    n = 2 * s + c
                    key = (("rg", s), c)
                    dve.wait_ge(ret_tanh, n + 1)
                    ins = V.scalar_tensor_tensor(out=rg[:, 2 * n:2 * n + 2, :].rearrange("p a b -> p (a b)"),
                                                 in0=rot[:, n % 2, :], scalar=1.0, in1=bank(key),
                                                 op0=ALU.add, op1=ALU.mult)
                    read_done(ins, key)
                    copied(dve, key)
                    V.memset(tiny[:, 499:500], 0.0).then_inc(ret_gate, 1)
            dve.wait_ge(decay_in, 16)
            before = None
            for step in RET_STEPS:
                kind, h = step[0], step[1]
                key = step
                if kind == "ada2":
                    if before:
                        modulation(before)
                    before = step
                elif kind == "rs":
                    read_ready(dve, key)
                    if h:
                        read_ready(dve, ("ro", h - 1, 1))
                    mask_h = con("decay")[:, 2 * T * h:2 * T * h + 2 * T]
                    read_done(V.tensor_tensor(rs, bank(key), mask_h, ALU.mult), key)
                    copied(dve, key)
                    V.memset(tiny[:, 499:500], 0.0).then_inc(ret_s, 1)
                elif kind == "rmean":
                    read_ready(dve, key)
                    own.link(V.tensor_scalar(rstd[:, 3, :], half(key, 0), 1.0 / 512, None, ALU.mult))
                    ins = V.tensor_tensor(ro, ro, over_tiles(rstd[:, 3, :], 4), ALU.subtract)
                    read_done(ins, key)
                    copied(dve, key)
                    V.memset(tiny[:, 499:500], 0.0).then_inc(ret_o, 1)
                elif kind == "rvar":
                    read_ready(dve, key)
                    read_done(refine(half(key, 0), rstd[:, 0, :], rstd[:, 1, :], rstd[:, 2, :], 512, ret_guess,
                                     h + 1), key)
                    copied(dve, key)
                    own.link(V.tensor_tensor(ro, ro, over_tiles(rstd[:, 0, :], 4), ALU.mult))
                    g = rg[:, 4 * h:4 * h + 4, :]
                    V.scalar_tensor_tensor(out=flat(g), in0=flat(ro), scalar=0.5, in1=flat(g), op0=ALU.mult,
                                           op1=ALU.mult).then_inc(ret_done, 1)
                    dve.wait_ge(ret_done, h + 1)
            modulation(before)
            for s in range(12):
                copied(dve, ("cols", ("ada2", 1, s)))
            own.mark(V.tensor_scalar(aff[:, 5, :], mod2[:, 1, 8:16], 1.0, None, ALU.add))
            V.tensor_scalar(aff[:, 6, :], mod2[:, 1, 32:40], 1.0, None, ALU.add).then_inc(affine_ready, 1)
            keys = [(("rout", s), 0) for s in range(4)]
            for s, key in enumerate(keys):
                add_to_x(key, 2 * s, mod2[:, 0, 16:24])
            dve.wait_ge(dve_step, own.n)
            x_complete(keys)

            def ffn(layer):
                norm(5 + 2 * layer)
                w = sml("conv_w").rearrange("p (l c k) -> p l c k", l=2, c=3)[:, layer]
                for m in range(11):
                    n = m + 11
                    key = (("up", layer, n // 2), n % 2)
                    dve.wait_ge(conv_start, 22 * layer + 2 * m + 2)
                    ps = two(bank(key))
                    cv = two(conv[:, m % 2, :])
                    for lag in (1, 2):
                        for a in range(2):
                            k = 2 * m + a
                            ins = V.scalar_tensor_tensor(out=cv[:, a, lag:T], in0=ps[:, a, 0:T - lag],
                                                         scalar=w[:, 2 - lag, k:k + 1], in1=cv[:, a, lag:T],
                                                         op0=ALU.mult, op1=ALU.add)
                            if lag == 2 and a == 1:
                                read_done(ins, key)
                            else:
                                own.mark(ins)
                        if lag == 1:
                            dve.wait_ge(dve_step, own.n)
                    dve.wait_ge(dve_step, own.n)
                    copied(dve, key)
                    V.memset(tiny[:, 499:500], 0.0).then_inc(conv_ready, 1)
                    if m >= 1:
                        finish(layer, m - 1)
                finish(layer, 10)
                keys = [(("down", layer, s), 0) for s in range(8)]
                for s, key in enumerate(keys):
                    add_to_x(key, s, mod2[:, layer, 40:48], n=1)
                x_complete(keys)

            def finish(layer, m):
                dve.wait_ge(conv_tanh, 11 * layer + m + 1)
                t, cv = conv_t[:, m % 2, :], conv[:, m % 2, :]
                n = m
                own.link(V.scalar_tensor_tensor(out=t, in0=t, scalar=1.0, in1=cv, op0=ALU.add, op1=ALU.mult))
                copied(dve, (("up", layer, n // 2), n % 2))
                v = flat(val[:, 2 * m:2 * m + 2, :])
                V.scalar_tensor_tensor(out=v, in0=t, scalar=0.5, in1=v, op0=ALU.mult, op1=ALU.mult
                                       ).then_inc(act_ready, 1)
                dve.wait_ge(act_ready, 11 * layer + m + 1)

            ffn(0)
            norm(6)

            dve.wait_ge(s5_in, 64)
            fr = row(8).unsqueeze(2).to_broadcast([P, S5_PAIRS, GROUP])
            fi = row(9).unsqueeze(2).to_broadcast([P, S5_PAIRS, GROUP])
            own.mark(V.tensor_tensor(c_f[:, 0], c_in5[:, 0], fr, ALU.mult))
            own.link(V.tensor_tensor(c_t, c_in5[:, 1], fi, ALU.mult))
            own.link(V.tensor_tensor(c_f[:, 0], c_f[:, 0], c_t, ALU.subtract))
            own.mark(V.tensor_tensor(c_f[:, 1], c_in5[:, 0], fi, ALU.mult))
            own.link(V.tensor_tensor(c_t, c_in5[:, 1], fr, ALU.mult))
            own.link(V.scalar_tensor_tensor(out=flat(c_f[:, 1]), in0=flat(c_f[:, 1]), scalar=-1.0, in1=flat(c_t),
                                            op0=ALU.mult, op1=ALU.subtract))
            own.link(V.tensor_scalar(c_t, c_f[:, 0], -1.0, None, ALU.mult))
            for g in range(2):
                own.mark(V.tensor_scalar(c_neg[:, :, GROUP * g:GROUP * g + GROUP], c_t,
                                         con("state_mask")[:, g:g + 1], None, ALU.mult))
            for c in range(2):
                for g in range(2):
                    own.mark(V.tensor_scalar(c_bd[:, c, :, GROUP * g:GROUP * g + GROUP], c_f[:, c],
                                             con("state_mask")[:, g:g + 1], None, ALU.mult))
                    own.mark(V.tensor_scalar(b_bd[:, c, :, STATE * g:STATE * g + STATE], b_in5[:, c],
                                             con("in_mask")[:, g:g + 1], None, ALU.mult))
            dve.wait_ge(dve_step, own.n)
            V.memset(tiny[:, 639:640], 0.0).then_inc(s5_bc, 1)

            def outputs(j):
                dve.wait_ge(s5_used, 4 * j + 4)
                V.scalar_tensor_tensor(out=y5[:, j, :], in0=u5[:, j, :], scalar=sml("s5_d")[:, j:j + 1],
                                       in1=psum[:, 4 + j % 2, 0:T], op0=ALU.mult, op1=ALU.add
                                       ).then_inc(s5_y_read, 1)

            def gelu_in(j):
                dve.wait_ge(s5_sq, j + 1)
                V.scalar_tensor_tensor(out=gl[:, j, :], in0=gl[:, j, :], scalar=1.0, in1=y5[:, j, :],
                                       op0=ALU.add, op1=ALU.mult).then_inc(s5_gelu_in, 1)

            def gelu_out(j):
                dve.wait_ge(s5_gelu_t, j + 1)
                V.scalar_tensor_tensor(out=y5[:, j, :], in0=gl[:, j, :], scalar=1.0, in1=y5[:, j, :],
                                       op0=ALU.add, op1=ALU.mult).then_inc(s5_y, 1)

            dve.wait_ge(s5_table, 1)
            for u in range(S5_PAIRS):
                key = ("bu", u)
                read_ready(dve, key)
                ct, st = over_tiles(cos_t[:, u, :], 4), over_tiles(sin_t[:, u, :], 4)
                w, in4 = z2[:, u % 2, :], bank(key).rearrange("p (a b) -> p a b", b=P)
                quarters = lambda a: a.rearrange("p (a b) -> p a b", b=P)
                if u >= 1:
                    dve.wait_ge(s5_turned, u)
                own.mark(V.tensor_tensor(quarters(z1), in4, ct, ALU.mult))
                if u >= 2:
                    dve.wait_ge(s5_state, u - 1)
                read_done(V.tensor_tensor(quarters(w), in4, st, ALU.mult), key)
                dve.wait_ge(dve_step, own.n)
                copied(dve, key)
                own.mark(V.tensor_tensor(z1[:, 0:T], z1[:, 0:T], w[:, T:2 * T], ALU.add))
                own.link(V.tensor_tensor(z1[:, T:2 * T], z1[:, T:2 * T], w[:, 0:T], ALU.subtract))
                m = row(1)[:, u:u + 1].to_broadcast([P, P])
                for c in range(2):
                    own.mark(V.tensor_tensor_scan(out=w[:, c * T:c * T + P], data0=m, data1=z1[:, c * T:c * T + P],
                                                  initial=0.0, op0=ALU.mult, op1=ALU.add))
                dve.wait_ge(dve_step, own.n)
                c_p, s_p = row(12)[:, u:u + 1], row(13)[:, u:u + 1]
                last = [w[:, c * T + P - 1:c * T + P] for c in range(2)]
                own.mark(V.tensor_scalar(carry[:, 0:1], last[1], s_p, None, ALU.mult))
                own.link(V.tensor_scalar(carry[:, 1:2], last[0], s_p, None, ALU.mult))
                own.mark(V.scalar_tensor_tensor(out=carry[:, 2:3], in0=last[0], scalar=c_p, in1=carry[:, 0:1],
                                                op0=ALU.mult, op1=ALU.subtract))
                own.link(V.scalar_tensor_tensor(out=carry[:, 3:4], in0=last[1], scalar=c_p, in1=carry[:, 1:2],
                                                op0=ALU.mult, op1=ALU.add))
                for c in range(2):
                    ins = V.tensor_tensor_scan(out=w[:, c * T + P:c * T + T], data0=m,
                                               data1=z1[:, c * T + P:c * T + T], initial=carry[:, 2 + c:3 + c],
                                               op0=ALU.mult, op1=ALU.add)
                    if c == 0:
                        own.mark(ins)
                ins.then_inc(s5_turned, 1)
                j, q = divmod(u - 5, 4)
                if u >= 5 and q < 3:
                    (outputs, gelu_in, gelu_out)[q](j)
            for stage in (outputs, gelu_in, gelu_out):
                stage(7)
            dve.wait_ge(s5_y, 8)
            for n in range(4):
                dve.wait_ge(glu_tanh, n + 1)
                key = (("glu", n // 2), n % 2)
                copied(dve, key)
                a = flat(gl[:, 2 * n:2 * n + 2, :])
                t = flat(u5[:, 2 * n:2 * n + 2, :])
                own.link(V.scalar_tensor_tensor(out=a, in0=t, scalar=1.0, in1=a, op0=ALU.add, op1=ALU.mult))
                for m in range(2):
                    k = 2 * n + m
                    ins = V.scalar_tensor_tensor(out=x[:, k, :], in0=gl[:, k, :], scalar=mod2[:, 1, 16 + k:17 + k],
                                                 in1=x[:, k, :], op0=ALU.mult, op1=ALU.add)
                    if m == 0:
                        own.mark(ins)
                key = (("glu", 2 + n // 2), n % 2)
                read_done(ins, key)
            dve.wait_ge(dve_step, own.n)
            x_complete([(("glu", 2 + n // 2), n % 2) for n in range(4)])
            ffn(1)
            norm(8)

        @block.gpsimd
        def _(pool):
            own = Steps(pool, pool_step)
            G = nc.gpsimd
            pool.wait_ge(x_ready, 1)
            pool.dma_start(w_rt, w_router.rearrange("(k p) n -> p k n", p=P)).then_inc(router_in, 16)
            pool.dma_start(b_out_sb[0:E, :], b_out).then_inc(bout_in, 16)
            pool.wait_ge(x_ready, 2)
            pool.dma_start(rot[:, 0, 0:T].bitcast(I32), pos).then_inc(pos_in, 16)
            pool.wait_ge(pos_in, 16)
            G.tensor_copy(rk[:, 0, :], rot[:, 0, 0:T].bitcast(I32)).then_inc(pos_ready, 1)
            pool.wait_ge(x_ready, X_READY[5])
            pool.wait_ge(s5_ab, 1)

            def square(c_new, s_new, ch, sh):
                w = tab_t[:, 0:S5_PAIRS].unsqueeze(2)
                own.mark(G.tensor_tensor(c_new, ch, ch, ALU.mult))
                own.mark(G.tensor_tensor(w, sh, sh, ALU.mult))
                own.link(G.tensor_tensor(s_new, ch, sh, ALU.mult))
                own.mark(G.tensor_tensor(c_new, c_new, w, ALU.subtract))
                own.link(G.tensor_tensor(s_new, s_new, s_new, ALU.add))

            def column(a, t):
                return a[:, :, t:t + 1]

            own.mark(G.memset(column(cos_t, 0), 1.0))
            own.mark(G.memset(column(sin_t, 0), 0.0))
            own.mark(G.tensor_copy(column(cos_t, 1), s5[:, 4, :].unsqueeze(2)))
            own.link(G.tensor_copy(column(sin_t, 1), s5[:, 5, :].unsqueeze(2)))
            n = 2
            while n < P:
                square(column(cos_t, n), column(sin_t, n), column(cos_t, n // 2), column(sin_t, n // 2))
                w = n - 1
                pairs = min(S5_PAIRS, BANK // n)
                for g in range(0, S5_PAIRS, pairs):
                    c_g, s_g = cos_t[:, g:g + pairs, :], sin_t[:, g:g + pairs, :]
                    t = tab_t[:, 0:pairs * w].rearrange("p (a b) -> p a b", b=w)
                    v = tab_u[:, 0:pairs * w].rearrange("p (a b) -> p a b", b=w)
                    bc, bs = c_g[:, :, n:n + 1].to_broadcast([P, pairs, w]), s_g[:, :, n:n + 1].to_broadcast([P, pairs, w])
                    hi_c, hi_s = c_g[:, :, n + 1:2 * n], s_g[:, :, n + 1:2 * n]
                    own.mark(G.tensor_tensor(hi_c, c_g[:, :, 1:n], bc, ALU.mult))
                    own.mark(G.tensor_tensor(t, s_g[:, :, 1:n], bs, ALU.mult))
                    own.mark(G.tensor_tensor(hi_s, s_g[:, :, 1:n], bc, ALU.mult))
                    own.link(G.tensor_tensor(v, c_g[:, :, 1:n], bs, ALU.mult))
                    own.mark(G.tensor_tensor(hi_c, hi_c, t, ALU.subtract))
                    own.link(G.tensor_tensor(hi_s, hi_s, v, ALU.add))
                n *= 2
            square(s5[:, 12, :].unsqueeze(2), s5[:, 13, :].unsqueeze(2), column(cos_t, P // 2), column(sin_t, P // 2))
            G.memset(tab_t[:, 0:1], 0.0).then_inc(s5_table, 1)
            pool.wait_ge(s5_table, 1)
            pool.wait_ge(x_ready, X_READY[6])
            for c in range(2):
                pool.dma_start(b_in5[:, c], s5_b[c]).then_inc(s5_in, 16)
                pool.dma_start(c_in5[:, c], s5_c[c]).then_inc(s5_in, 16)
            for u in range(S5_PAIRS):
                pool.wait_ge(s5_turned, u + 1)
                if u >= 2:
                    pool.wait_ge(s5_used, u - 1)
                w = z2[:, u % 2, :].rearrange("p (a b) -> p a b", b=P)
                for table, z in ((cos_t, z_cos[u % 2]), (sin_t, z_sin[u % 2])):
                    ins = G.tensor_tensor(z.rearrange("p (a b) -> p a b", b=P), w, over_tiles(table[:, u, :], 4),
                                          ALU.mult)
                ins.then_inc(s5_state, 1)



def kernel(**inputs):
    import concourse.bacc as bacc
    from concourse.bass_utils import run_bass_kernel_spmd

    a = {k: np.asarray(v) for k, v in inputs.items()}

    def columns(v):
        return v.reshape(-1, P).T

    def lay(v):
        return np.ascontiguousarray(v)

    heads = np.arange(512).reshape(2, 4, HD).transpose(1, 0, 2).reshape(-1)
    w_qkv = a["w_qkv"][0]
    w_qkv = np.concatenate([w_qkv[:, heads], w_qkv[:, 512:]], 1)
    w_o = np.concatenate([a["w_o"][0][heads], a["w_o"][0][512:]], 0)

    def states(v):
        return v.reshape(S5_PAIRS, 2 * STATE).T

    log_dt = np.repeat(a["s5_log_dt_2"][0].reshape(S5_PAIRS, 2).T, STATE, axis=0)
    parts = {
        "cond": np.stack([columns(a["c"][0]), columns(a["c_ctx"])], 2).reshape(P, 16),
        "b_ada": columns(a["b_ada"][0]), "g_attn": columns(a["g_attn"][0]),
        "g_q": np.tile(a["gqa_q_norm"][0], 2)[:, None], "g_k": np.tile(a["gqa_k_norm"][0], 2)[:, None],
        "g_sub": a["diff_subln"][0][:, None], "g_ffn": columns(a["g_ffn"][0]),
        "g_final": columns(a["g_final"]),
        "b_in": a["b_in"][0].reshape(E, 16, P).transpose(2, 0, 1).reshape(P, E * 16),
        "cond2": columns(a["c_2"][0]),
        "b_ada2": a["ada_b_2"].reshape(2, 48, P).transpose(2, 0, 1).reshape(P, 96),
        "lam_re": states(a["s5_lam_re_2"][0]), "lam_im": states(a["s5_lam_im_2"][0]), "log_dt": log_dt,
        "s5_d": columns(a["s5_d_2"][0]),
        "conv_w": a["ffn_conv_w_2"][:, :, 0].reshape(2, 3, KF, P).transpose(3, 0, 1, 2).reshape(P, -1),
        "conv_b": a["ffn_conv_b_2"].reshape(2, KF, P).transpose(2, 0, 1).reshape(P, -1),
        "g_final2": columns(a["final_norm_g_2"]),
        "dlam": np.broadcast_to(a["diff_lambda"][0].reshape(1, 4 * HD), (P, 4 * HD)),
        "b_router": np.broadcast_to(a["b_router"][0][None], (P, E)),
    }
    small = np.concatenate([parts[name] for name in SMALL], 1)
    s5_b = np.stack([a[n][0].reshape(8, 4, 2, STATE, GROUP).transpose(1, 2, 4, 0, 3).reshape(P, 8, STATE)
                     for n in ("s5_b_re_2", "s5_b_im_2")])
    s5_c = np.stack([a[n][0].reshape(S5_PAIRS, 2, GROUP, STATE).transpose(1, 3, 0, 2).reshape(P, S5_PAIRS, GROUP)
                     for n in ("s5_c_re_2", "s5_c_im_2")])
    arrays = {
        "small": small, "const": constants(),
        "xT": a["x"][0].T, "cT": a["ctx"][0].T,
        "pos": np.broadcast_to(a["pos_2"], (P, T)),
        "w_ada": a["w_ada"][0], "w_qkv": w_qkv, "w_o": w_o, "w_router": a["w_router"][0],
        "w_in": a["w_in"][0], "w_out": a["w_out"][0], "b_out": a["b_out"][0],
        "w_ada2": a["ada_w_2"], "w_ret": a["ret_w_in_2"][0],
        "w_rout": a["ret_w_out_2"][0].reshape(16, P, 4, T).transpose(2, 1, 0, 3),
        "w_s5in": a["s5_w_in_2"][0], "s5_b": s5_b, "s5_c": s5_c, "w_glu": a["s5_w_glu_2"][0],
        "w_up": a["ffn_w_up_2"],
        "w_down": a["ffn_w_down_2"].reshape(2, KF, P, KD, P).transpose(0, 3, 2, 1, 4),
    }
    nc = bacc.Bacc("TRN2", target_bir_lowering=False, num_devices=1)
    feed, args = {}, []
    for name, v in arrays.items():
        v = lay(v)
        feed[f"in_{name}_dram"] = v
        args.append(nc.dram_tensor(f"in_{name}_dram", v.shape, mybir.dt.from_np(v.dtype), kind="ExternalInput").ap())
    out = nc.dram_tensor("out_dram", (D, T), F32, kind="ExternalOutput").ap()
    transformer_blocks_kernel(nc, *args, out)
    r = run_bass_kernel_spmd(nc, [feed], core_ids=[0])
    return np.ascontiguousarray(r.results[0]["out_dram"].T).reshape(1, T, D)
```
